# Optimizing a Trainium2 kernel written in Bass

```python
import math
import jax
import jax.numpy as jnp
from jax import lax
import numpy as np

D_MODEL = 1024
BATCH = 1
SEQ = 128
DEPTH = 4
DEC_BATCH = 1
DEC_SEQ = 512
PAST_LEN = 128

GRID_W = 64
N_MIXERS = 3
N_LAYERS_A = (DEPTH + 2) // 3
N_LAYERS_B = (DEPTH + 1) // 3
N_LAYERS_C = DEPTH // 3
N_MOD = 6
D_FF = 4 * D_MODEL
DEEPNORM_ALPHA = (2.0 * DEPTH) ** 0.25
DEEPNORM_BETA = (8.0 * DEPTH) ** -0.25
LN_EPS = 1e-5

RW_HEAD = 64
RW_HEADS = D_MODEL // RW_HEAD
RW_DECAY_RANK = 64
RW_ICL_RANK = 64
RW_GATE_RANK = 128
RW_GN_EPS = 64e-5

AT_HEAD = 64
AT_HEADS = D_MODEL // AT_HEAD
AT_KV_HEADS = AT_HEADS // 4
Q_BLOCK = 128
ROPE_THETA = 10000.0

DN_HEADS = 8
DN_HEAD_K = D_MODEL // DN_HEADS
DN_HEAD_V = D_MODEL // DN_HEADS
DN_CONV = 3
DN_CHUNK = 64

kernel_name = 'hybrid_dit_rwkv7_gqa_gdn_step'

def layer_norm(x, g, b):
    xf = x.astype(jnp.float32)
    mu = jnp.mean(xf, axis=-1, keepdims=True)
    var = jnp.mean(jnp.square(xf - mu), axis=-1, keepdims=True)
    return ((xf - mu) * lax.rsqrt(var + LN_EPS)).astype(x.dtype) * g + b

def rms_norm(x, g, eps=1e-6):
    xf = x.astype(jnp.float32)
    y = xf * lax.rsqrt(jnp.mean(jnp.square(xf), axis=-1, keepdims=True) + eps)
    return y.astype(x.dtype) * g

def l2_normalize(x, eps=1e-6):
    xf = x.astype(jnp.float32)
    return (xf * lax.rsqrt(jnp.sum(jnp.square(xf), axis=-1, keepdims=True) + eps)).astype(x.dtype)

def modulation(cond, w_mod, b_mod):
    m = jax.nn.silu(cond) @ w_mod + b_mod
    return jnp.split(m[..., None, :], N_MOD, axis=-1)

def modulate(x, shift, scale):
    return x * (1 + scale) + shift

def deepnorm_residual(x, delta, gate, g, b):
    return layer_norm(DEEPNORM_ALPHA * x + gate * delta, g, b)

def squared_relu_mlp(h, w_fc1, w_fc2):
    return jnp.square(jax.nn.relu(h @ w_fc1)) @ w_fc2

def axial_rope_tables(n_tokens, head_dim):
    rows = n_tokens // GRID_W
    row = jnp.repeat(jnp.arange(rows), GRID_W)
    col = jnp.tile(jnp.arange(GRID_W), rows)
    n_freq = head_dim // 4
    inv_freq = ROPE_THETA ** (-jnp.arange(n_freq, dtype=jnp.float32) / n_freq)
    ang = jnp.stack([row, col], axis=-1).astype(jnp.float32)[:, :, None] * inv_freq
    return jnp.cos(ang), jnp.sin(ang)

def apply_axial_rope(x, cos, sin):
    b, t, h, hd = x.shape
    n_freq = hd // 4
    xr = x.astype(jnp.float32).reshape(b, t, h, 2, 2, n_freq)
    x1, x2 = xr[..., 0, :], xr[..., 1, :]
    cos, sin = cos[None, :, None], sin[None, :, None]
    out = jnp.stack([x1 * cos - x2 * sin, x2 * cos + x1 * sin], axis=-2)
    return out.reshape(b, t, h, hd).astype(x.dtype)

def attention_qkv(h, w_qkv, q_gain, k_gain):
    b, t, _ = h.shape
    qkv = h @ w_qkv
    q, k, v = jnp.split(qkv, [AT_HEADS * AT_HEAD, (AT_HEADS + AT_KV_HEADS) * AT_HEAD], axis=-1)
    q = rms_norm(q.reshape(b, t, AT_HEADS, AT_HEAD), q_gain)
    k = rms_norm(k.reshape(b, t, AT_KV_HEADS, AT_HEAD), k_gain)
    v = v.reshape(b, t, AT_KV_HEADS, AT_HEAD)
    return q, k, v

def block_attention(q, k, v):
    b, tq, h, hd = q.shape
    grp = h // AT_KV_HEADS
    nb = tq // Q_BLOCK
    scale = hd ** -0.5
    qb = q.reshape(b, nb, Q_BLOCK, AT_KV_HEADS, grp, hd).transpose(1, 0, 2, 3, 4, 5)

    def one_block(q_blk):
        s = jnp.einsum('bqhgd,bkhd->bhgqk', q_blk, k).astype(jnp.float32) * scale
        p = jax.nn.softmax(s, axis=-1).astype(v.dtype)
        return jnp.einsum('bhgqk,bkhd->bqhgd', p, v)

    o = lax.map(one_block, qb)
    return o.transpose(1, 0, 2, 3, 4, 5).reshape(b, tq, h * hd)

def attention_context(h, w_qkv, q_gain, k_gain, w_o):
    q, k, v = attention_qkv(h, w_qkv, q_gain, k_gain)
    return block_attention(q, k, v) @ w_o, k, v

def attention_latent(h, ctx_k, ctx_v, w_qkv, q_gain, k_gain, w_o):
    q, k, v = attention_qkv(h, w_qkv, q_gain, k_gain)
    cos, sin = axial_rope_tables(h.shape[1], AT_HEAD)
    q = apply_axial_rope(q, cos, sin)
    k = apply_axial_rope(k, cos, sin)
    k_all = jnp.concatenate([ctx_k.astype(k.dtype), k], axis=1)
    v_all = jnp.concatenate([ctx_v.astype(v.dtype), v], axis=1)
    return block_attention(q, k_all, v_all) @ w_o

def centred_token_shift(x):
    prev = jnp.pad(x[:, :-1], ((0, 0), (1, 0), (0, 0)))
    nxt = jnp.pad(x[:, 1:], ((0, 0), (0, 1), (0, 0)))
    return 0.5 * (prev + nxt) - x

def rwkv7_scan(r, w, k, v, kk, a, s0):
    def step(s, inp):
        r_t, w_t, k_t, v_t, kk_t, a_t = inp
        sa = jnp.einsum('bhvk,bhk->bhv', s, -kk_t)
        s = (s * w_t[:, :, None, :] + sa[..., None] * (kk_t * a_t)[:, :, None, :]
             + v_t[..., None] * k_t[:, :, None, :])
        return s, jnp.einsum('bhvk,bhk->bhv', s, r_t)

    xs = tuple(jnp.swapaxes(z, 0, 1) for z in (r, w, k, v, kk, a))
    s_final, o = lax.scan(step, s0.astype(jnp.float32), xs)
    return jnp.swapaxes(o, 0, 1), s_final

def rwkv7_mixer(h, s0_fwd, s0_bwd, mu_mix, w_rkv, w0, w1, w2, a0, a1, a2, g1, g2,
                k_k, k_a, r_k, gn_g, gn_b, w_o):
    b, t, d = h.shape

    def heads(z):
        return z.astype(jnp.float32).reshape(z.shape[:-1] + (RW_HEADS, RW_HEAD))

    def flip(z):
        return jnp.flip(z, axis=1)

    xx = centred_token_shift(h)
    xr, xw, xk, xv, xa, xg = [h + xx * mu_mix[i] for i in range(6)]
    r = xr @ w_rkv[0]
    k = xk @ w_rkv[1]
    v = xv @ w_rkv[2]
    lw = jnp.tanh(jnp.einsum('btc,ecr->betr', xw, w1))
    w_log = -jax.nn.softplus(-(w0[None, :, None, :] + jnp.einsum('betr,erc->betc', lw, w2))) - 0.5
    decay = jnp.exp(-jnp.exp(w_log.astype(jnp.float32)))
    la = jnp.einsum('btc,ecr->betr', xa, a1)
    a = jax.nn.sigmoid(a0[None, :, None, :] + jnp.einsum('betr,erc->betc', la, a2))
    g = jax.nn.sigmoid(xg @ g1) @ g2
    kk = l2_normalize(heads(k * k_k))
    k_dir = heads(k[:, None] * (1 + (a - 1) * k_a))
    a_h, decay_h = heads(a), heads(decay)
    rh, vh = heads(r), heads(v)
    o_f, s_f = rwkv7_scan(rh, decay_h[:, 0], k_dir[:, 0], vh, kk, a_h[:, 0], s0_fwd)
    o_b, s_b = rwkv7_scan(flip(rh), flip(decay_h[:, 1]), flip(k_dir[:, 1]), flip(vh),
                          flip(kk), flip(a_h[:, 1]), s0_bwd)
    o = o_f + flip(o_b)
    mean = jnp.mean(o, axis=-1, keepdims=True)
    var = jnp.mean(jnp.square(o - mean), axis=-1, keepdims=True)
    y = ((o - mean) * lax.rsqrt(var + RW_GN_EPS)).reshape(b, t, d) * gn_g + gn_b
    bonus = jnp.sum(rh[:, None] * k_dir * r_k, axis=-1).sum(axis=1)[..., None] * vh
    y = (y + bonus.reshape(b, t, d)) * g
    return y.astype(h.dtype) @ w_o, s_f, s_b

def short_conv(x, w):
    width, ch = w.shape
    return lax.conv_general_dilated(
        x, w[:, None, :].astype(x.dtype), window_strides=(1,),
        padding=[((width - 1) // 2, width // 2)],
        dimension_numbers=('NWC', 'WIO', 'NWC'), feature_group_count=ch)

def gated_delta_chunked(q, k, v, g, beta, s0):
    b, t, h, _ = q.shape
    dv = v.shape[-1]
    n = t // DN_CHUNK

    def chunks(z):
        z = z.astype(jnp.float32).reshape((b, n, DN_CHUNK) + z.shape[2:])
        return jnp.moveaxis(z, 3, 1)

    q, k, v, g, beta = (chunks(z) for z in (q, k, v, g, beta))
    g = jnp.cumsum(g, axis=-1)
    kb = k * beta[..., None]
    vb = v * beta[..., None]
    idx = jnp.arange(DN_CHUNK)
    incl = idx[:, None] >= idx[None, :]
    strict = idx[:, None] > idx[None, :]
    diff = g[..., :, None] - g[..., None, :]
    decay = jnp.where(incl, jnp.exp(jnp.where(incl, diff, 0.0)), 0.0)
    low = jnp.where(strict, jnp.einsum('bhncd,bhnsd->bhncs', kb, k) * decay, 0.0)
    eye = jnp.eye(DN_CHUNK, dtype=jnp.float32)
    tmat = lax.linalg.triangular_solve(eye + low, jnp.broadcast_to(eye, low.shape),
                                       left_side=True, lower=True)
    u = tmat @ vb
    w = tmat @ (kb * jnp.exp(g)[..., None])
    qk = jnp.einsum('bhncd,bhnsd->bhncs', q, k) * decay
    q_dec = q * jnp.exp(g)[..., None]
    k_dec = k * jnp.exp(g[..., -1:] - g)[..., None]
    g_last = jnp.exp(g[..., -1])

    def step(s, inp):
        q_i, k_i, u_i, w_i, qk_i, gl_i = inp
        v_new = u_i - w_i @ s
        o_i = q_i @ s + qk_i @ v_new
        s = s * gl_i[..., None, None] + jnp.einsum('bhcd,bhce->bhde', k_i, v_new)
        return s, o_i

    xs = tuple(jnp.moveaxis(z, 2, 0) for z in (q_dec, k_dec, u, w, qk, g_last))
    s_final, o = lax.scan(step, s0.astype(jnp.float32), xs)
    o = jnp.moveaxis(jnp.moveaxis(o, 0, 2), 1, 3).reshape(b, t, h, dv)
    return o, s_final

def deltanet_mixer(h, s0_fwd, s0_bwd, w_in, conv_w, a_log, dt_bias, norm_g, w_o):
    b, t, _ = h.shape
    hk, hv = DN_HEADS * DN_HEAD_K, DN_HEADS * DN_HEAD_V

    def flip(z):
        return jnp.flip(z, axis=1)

    proj = h @ w_in
    qkv, z, gate_a, gate_b = jnp.split(
        proj, [2 * hk + hv, 2 * hk + 2 * hv, 2 * hk + 2 * hv + 2 * DN_HEADS], axis=-1)
    qkv = jax.nn.silu(short_conv(qkv, conv_w))
    q, k, v = jnp.split(qkv, [hk, 2 * hk], axis=-1)
    q = l2_normalize(q.reshape(b, t, DN_HEADS, DN_HEAD_K)) * (DN_HEAD_K ** -0.5)
    k = l2_normalize(k.reshape(b, t, DN_HEADS, DN_HEAD_K))
    v = v.reshape(b, t, DN_HEADS, DN_HEAD_V)
    gate_a = gate_a.astype(jnp.float32).reshape(b, t, 2, DN_HEADS)
    log_decay = -jnp.exp(a_log) * jax.nn.softplus(gate_a + dt_bias)
    beta = jax.nn.sigmoid(gate_b.astype(jnp.float32).reshape(b, t, 2, DN_HEADS))
    o_f, s_f = gated_delta_chunked(q, k, v, log_decay[:, :, 0], beta[:, :, 0], s0_fwd)
    o_b, s_b = gated_delta_chunked(flip(q), flip(k), flip(v), flip(log_decay[:, :, 1]),
                                   flip(beta[:, :, 1]), s0_bwd)
    zg = jax.nn.silu(z.reshape(b, t, DN_HEADS, DN_HEAD_V).astype(jnp.float32))
    o = rms_norm(o_f + flip(o_b), norm_g) * zg
    return o.reshape(b, t, hv).astype(h.dtype) @ w_o, s_f, s_b

def setup_inputs(seed: int = 0) -> dict:
    key = jax.random.key(seed)
    ks = iter(jax.random.split(key, 48))
    d = D_MODEL
    hk, hv = DN_HEADS * DN_HEAD_K, DN_HEADS * DN_HEAD_V
    at_cols = (AT_HEADS + 2 * AT_KV_HEADS) * AT_HEAD

    def nrm(shape, scale):
        return scale * jax.random.normal(next(ks), shape, jnp.float32)

    def unif(shape, lo, hi):
        return jax.random.uniform(next(ks), shape, jnp.float32, lo, hi)

    inp = {}
    inp['x_prompt'] = nrm((BATCH, SEQ, d), 1.0)
    inp['x_sample'] = nrm((DEC_BATCH, DEC_SEQ, d), 1.0)
    inp['state_rwkv'] = nrm((DEC_BATCH, N_LAYERS_A, 2, RW_HEADS, RW_HEAD, RW_HEAD), 0.5)
    inp['cache_k'] = nrm((DEC_BATCH, N_LAYERS_B, PAST_LEN, AT_KV_HEADS, AT_HEAD), 1.0)
    inp['cache_v'] = nrm((DEC_BATCH, N_LAYERS_B, PAST_LEN, AT_KV_HEADS, AT_HEAD), 1.0)
    inp['state_delta'] = nrm((DEC_BATCH, N_LAYERS_C, 2, DN_HEADS, DN_HEAD_K, DN_HEAD_V), 0.1)
    inp['c'] = nrm((DEC_BATCH, d), 1.0)
    inp['c_ctx'] = nrm((d,), 1.0)
    inp['w_mod'] = nrm((DEPTH, d, N_MOD * d), 0.5 * d ** -0.5)
    inp['b_mod'] = nrm((DEPTH, N_MOD * d), 0.02)
    inp['ln_g'] = 1.0 + nrm((DEPTH, 2, d), 0.02)
    inp['ln_b'] = nrm((DEPTH, 2, d), 0.02)
    inp['w_fc1'] = nrm((DEPTH, d, D_FF), d ** -0.5)
    inp['w_fc2'] = nrm((DEPTH, D_FF, d), DEEPNORM_BETA * D_FF ** -0.5)
    inp['rw_mu'] = unif((N_LAYERS_A, 6, d), 0.0, 1.0)
    inp['rw_wrkv'] = nrm((N_LAYERS_A, 3, d, d), d ** -0.5)
    inp['rw_w0'] = unif((N_LAYERS_A, 2, d), -4.0, 1.0)
    inp['rw_w1'] = nrm((N_LAYERS_A, 2, d, RW_DECAY_RANK), d ** -0.5)
    inp['rw_w2'] = nrm((N_LAYERS_A, 2, RW_DECAY_RANK, d), 0.3 * RW_DECAY_RANK ** -0.5)
    inp['rw_a0'] = nrm((N_LAYERS_A, 2, d), 0.3)
    inp['rw_a1'] = nrm((N_LAYERS_A, 2, d, RW_ICL_RANK), d ** -0.5)
    inp['rw_a2'] = nrm((N_LAYERS_A, 2, RW_ICL_RANK, d), 0.3 * RW_ICL_RANK ** -0.5)
    inp['rw_g1'] = nrm((N_LAYERS_A, d, RW_GATE_RANK), d ** -0.5)
    inp['rw_g2'] = nrm((N_LAYERS_A, RW_GATE_RANK, d), RW_GATE_RANK ** -0.5)
    inp['rw_kk'] = 0.85 + nrm((N_LAYERS_A, d), 0.02)
    inp['rw_ka'] = 1.0 + nrm((N_LAYERS_A, d), 0.02)
    inp['rw_rk'] = nrm((N_LAYERS_A, RW_HEADS, RW_HEAD), 0.1)
    inp['rw_gn_g'] = 1.0 + nrm((N_LAYERS_A, d), 0.02)
    inp['rw_gn_b'] = nrm((N_LAYERS_A, d), 0.02)
    inp['rw_wo'] = nrm((N_LAYERS_A, d, d), DEEPNORM_BETA * d ** -0.5)
    inp['at_wqkv'] = nrm((N_LAYERS_B, d, at_cols), d ** -0.5)
    inp['at_qn'] = 1.0 + nrm((N_LAYERS_B, AT_HEAD), 0.02)
    inp['at_kn'] = 1.0 + nrm((N_LAYERS_B, AT_HEAD), 0.02)
    inp['at_wo'] = nrm((N_LAYERS_B, AT_HEADS * AT_HEAD, d), DEEPNORM_BETA * (AT_HEADS * AT_HEAD) ** -0.5)
    inp['dn_win'] = jnp.concatenate([
        nrm((N_LAYERS_C, d, 2 * hk + 2 * hv), d ** -0.5),
        nrm((N_LAYERS_C, d, 2 * DN_HEADS), 0.1 * d ** -0.5),
        nrm((N_LAYERS_C, d, 2 * DN_HEADS), d ** -0.5)], axis=-1)
    inp['dn_conv'] = nrm((N_LAYERS_C, DN_CONV, 2 * hk + hv), DN_CONV ** -0.5)
    inp['dn_alog'] = jnp.log(unif((N_LAYERS_C, 2, DN_HEADS), 1.0, 16.0))
    dt = jnp.exp(unif((N_LAYERS_C, 2, DN_HEADS), math.log(1e-3), math.log(1e-1)))
    inp['dn_dtb'] = dt + jnp.log(-jnp.expm1(-dt))
    inp['dn_ng'] = 1.0 + nrm((N_LAYERS_C, DN_HEAD_V), 0.02)
    inp['dn_wo'] = nrm((N_LAYERS_C, hv, d), DEEPNORM_BETA * hv ** -0.5)
    return inp

def reference(x_prompt, x_sample, state_rwkv, cache_k, cache_v, state_delta, c, c_ctx,
              w_mod, b_mod, ln_g, ln_b, w_fc1, w_fc2,
              rw_mu, rw_wrkv, rw_w0, rw_w1, rw_w2, rw_a0, rw_a1, rw_a2, rw_g1, rw_g2,
              rw_kk, rw_ka, rw_rk, rw_gn_g, rw_gn_b, rw_wo,
              at_wqkv, at_qn, at_kn, at_wo,
              dn_win, dn_conv, dn_alog, dn_dtb, dn_ng, dn_wo):
    xp, xs = x_prompt, x_sample
    n_ctx = xp.shape[0]
    new_rwkv, new_k, new_v, new_delta = [], [], [], []
    for l in range(DEPTH):
        kind, j = l % N_MIXERS, l // N_MIXERS
        mp = modulation(c_ctx, w_mod[l], b_mod[l])
        ms = modulation(c, w_mod[l], b_mod[l])
        hp = modulate(xp, mp[0], mp[1])
        hs = modulate(xs, ms[0], ms[1])
        if kind == 0:
            prm = (rw_mu[j], rw_wrkv[j], rw_w0[j], rw_w1[j], rw_w2[j], rw_a0[j], rw_a1[j],
                   rw_a2[j], rw_g1[j], rw_g2[j], rw_kk[j], rw_ka[j], rw_rk[j], rw_gn_g[j],
                   rw_gn_b[j], rw_wo[j])
            zero = jnp.zeros((n_ctx, RW_HEADS, RW_HEAD, RW_HEAD), jnp.float32)
            dp, s_f, s_b = rwkv7_mixer(hp, zero, zero, *prm)
            ds, _, _ = rwkv7_mixer(hs, state_rwkv[:, j, 0], state_rwkv[:, j, 1], *prm)
            new_rwkv.append(jnp.stack([s_f, s_b], axis=1).astype(xp.dtype))
        elif kind == 1:
            prm = (at_wqkv[j], at_qn[j], at_kn[j], at_wo[j])
            dp, kp, vp = attention_context(hp, *prm)
            ds = attention_latent(hs, cache_k[:, j], cache_v[:, j], *prm)
            new_k.append(kp)
            new_v.append(vp)
        else:
            prm = (dn_win[j], dn_conv[j], dn_alog[j], dn_dtb[j], dn_ng[j], dn_wo[j])
            zero = jnp.zeros((n_ctx, DN_HEADS, DN_HEAD_K, DN_HEAD_V), jnp.float32)
            dp, s_f, s_b = deltanet_mixer(hp, zero, zero, *prm)
            ds, _, _ = deltanet_mixer(hs, state_delta[:, j, 0], state_delta[:, j, 1], *prm)
            new_delta.append(jnp.stack([s_f, s_b], axis=1).astype(xp.dtype))
        xp = deepnorm_residual(xp, dp, mp[2], ln_g[l, 0], ln_b[l, 0])
        xs = deepnorm_residual(xs, ds, ms[2], ln_g[l, 0], ln_b[l, 0])
        hp = modulate(xp, mp[3], mp[4])
        hs = modulate(xs, ms[3], ms[4])
        xp = deepnorm_residual(xp, squared_relu_mlp(hp, w_fc1[l], w_fc2[l]), mp[5], ln_g[l, 1], ln_b[l, 1])
        xs = deepnorm_residual(xs, squared_relu_mlp(hs, w_fc1[l], w_fc2[l]), ms[5], ln_g[l, 1], ln_b[l, 1])
    new_state_rwkv = jnp.stack(new_rwkv, axis=1)
    new_cache_k = jnp.stack(new_k, axis=1)
    new_cache_v = jnp.stack(new_v, axis=1)
    new_state_delta = jnp.stack(new_delta, axis=1)
    return (xp, xs, new_state_rwkv, new_cache_k, new_cache_v, new_state_delta)


_drawn_inputs = setup_inputs


def setup_inputs(seed=0):
    import zlib

    import numpy as np

    out = dict(_drawn_inputs(seed))
    spreads = {}
    factors = {'state_rwkv': 8.0,
     'cache_k': 8.0,
     'cache_v': 8.0,
     'state_delta': 8.0,
     'rw_g1': 2.751,
     'rw_kk': 2.691,
     'rw_gn_g': 8.0,
     'rw_gn_b': 8.0,
     'at_qn': 8.0,
     'at_kn': 8.655,
     'dn_ng': 52.669}
    for name, (base, spread) in spreads.items():
        noise = np.random.default_rng([zlib.crc32(name.encode()), seed]).standard_normal(out[name].shape)
        drawn = base * np.exp(spread * noise) if base else spread * noise
        out[name] = jnp.asarray(drawn.astype(out[name].dtype))
    for name, factor in factors.items():
        out[name] = (out[name] * factor).astype(out[name].dtype)
    return out
```

```python
from contextlib import ExitStack, contextmanager

import concourse.bass as bass
import numpy as np
from concourse import mybir

F32 = mybir.dt.float32
ACT = mybir.ActivationFunctionType
ALU = mybir.AluOpType
AX = mybir.AxisListType

P = 128
D = 1024
DEPTH = 4
NB = D // P
LAT, CTX = 512, 128
T = LAT + CTX
FF = 4 * D
NFB = FF // P
GRID_W = 64
C = 64
ALPHA = (2.0 * DEPTH) ** 0.25
LN_EPS = 1e-5
GN_EPS = 64e-5
NRM_EPS = 1e-6
HALF_DECAY = float(np.exp(-0.5))
RW_LAYERS = 2
RW_HEADS, DN_HEADS = 16, 8
AT_HEADS, AT_KV, HD = 16, 4, 64

HW = T + 4
H_LAT = slice(1, 1 + LAT)
H_CTX = slice(2 + LAT, 2 + LAT + CTX)
S_LAT = slice(0, LAT)
S_CTX = slice(LAT, T)

TT = 2 * T
NCHUNK = T // C
NLAT = LAT // C
GROUP = 4
NGROUP = NCHUNK // 2
LEVELS = 5

K_ID, K_BO, K_ONE = 0, 128, 256
K_MEAN, K_SP, K_IP, K_L0 = 384, 512, 640, 768
K_LV = 896
K_SCAN = K_LV + LEVELS * P
K_EPS = K_SCAN + TT
K_END = K_EPS + 4

V_LN = 0
V_MU = V_LN + DEPTH * 2 * 2 * NB
V_END = V_MU + RW_LAYERS * 6 * NB


def constant_table():
    t = np.zeros((P, K_END), np.float32)
    r = np.arange(P)
    same = r[:, None] // C == r[None, :] // C
    row, col = r[:, None], r[None, :]
    t[:, K_ID:K_ID + P] = np.eye(P)
    t[:, K_BO:K_BO + P] = same
    t[:, K_ONE:K_ONE + P] = 1.0
    t[:, K_MEAN:K_MEAN + P] = 1.0 / D
    t[:, K_SP:K_SP + P] = same & (col > row)
    t[:, K_IP:K_IP + P] = same & (col >= row)
    t[:, K_L0:K_L0 + P] = (row // 2 == col // 2) & (col > row)
    for n in range(LEVELS):
        b = 2 << n
        at = K_LV + n * P
        t[:, at:at + P] = (row // (2 * b) == col // (2 * b)) & (row // b > col // b)
    t[:, K_SCAN:K_SCAN + TT] = np.arange(TT) % C != 0
    t[:, K_EPS], t[:, K_EPS + 1], t[:, K_EPS + 2] = LN_EPS, GN_EPS, NRM_EPS
    return t


def at(i, per, k):
    return i * per + k


def wait_alone(eng, sem, value, passed):
    eng.wait_ge(sem, value)
    eng.sem_inc(passed, 1)


class Link:

    def __init__(self, eng, sem, i=0, per=0):
        self.eng, self.sem, self.i, self.per, self.n = eng, sem, i, per, 0

    def __call__(self, ins):
        ins.then_inc(self.sem, 1)
        self.n += 1
        self.eng.wait_ge(self.sem, at(self.i, self.per, self.n))

    def end(self):
        assert self.n == self.per, f"the body has {self.n} links"


_count = [0]


def unique(name):
    _count[0] += 1
    return f"{name}_{_count[0]}"


@contextmanager
def phase(nc, *names):
    made, all_of = {}, []
    assert len(set(names)) == len(names)
    for name in names:
        key, _, n = name.partition(":")
        sems = [nc.alloc_semaphore(unique(f"{key}_{m}")) for m in range(int(n or 1))]
        made[key] = sems if n else sems[0]
        all_of += sems
    yield made
    nc.clear_and_free_semaphores(all_of)
    nc.all_engine_barrier()


@contextmanager
def buffers(nc):
    with ExitStack() as stack:
        count = [0]

        def sb(name, *shape):
            return stack.enter_context(nc.sbuf_tensor(unique(name), [P, *shape], F32))

        def banks(n):
            return [stack.enter_context(nc.psum_tensor(unique(f"bank{b}"), [P, 512], F32)) for b in range(n)]

        yield sb, banks


def slab(dram, n):
    return dram[bass.ds(n, 1)].rearrange("a p n -> p (a n)")


def blocks(dram):
    return dram.rearrange("b p t -> p b t")


def mod_at(layer, piece):
    return (layer * 6 + piece) * NB




def start(nc, g):
    with phase(nc, "loaded", "sig") as s, nc.Block() as block:

        @block.sync
        def _(sp):
            sp.dma_start(g.x[:, :, :], blocks(g.d["x_t"])).then_inc(s["loaded"], 16)
            sp.dma_start(g.const[:, :], g.d["consts"]).then_inc(s["loaded"], 16)
            sp.dma_start(g.vec[:, :], g.d["vectors"]).then_inc(s["loaded"], 16)
            sp.dma_start(g.bmod[:, :], g.d["b_mod_t"]).then_inc(s["loaded"], 16)
            sp.dma_start(g.cond[:, :, :], g.d["cond_t"]).then_inc(s["loaded"], 16)

        @block.scalar
        def _(act):
            act.wait_ge(s["loaded"], 80)
            nc.scalar.activation(g.silu[:, :, :], g.cond[:, :, :], ACT.Sigmoid).then_inc(s["sig"], 1)

        @block.vector
        def _(dve):
            dve.wait_ge(s["sig"], 1)
            nc.vector.tensor_tensor(g.silu[:, :, :], g.silu[:, :, :], g.cond[:, :, :], ALU.mult)


def modulation(nc, g):
    NS = 512
    STEPS = DEPTH * 6 * D // NS
    with buffers(nc) as (sb, banks), phase(
            nc, "w_loaded:2", "rows_ready", "rows_copied", "cols_ready", "cols_added", "passed") as s:
        ring = sb("mod_ring", 2, NB, NS)
        rows = sb("mod_rows", 2, NS)
        bank = banks(4)
        with nc.Block() as block:

            @block.sync
            def _(sp):
                with sp.Fori(0, STEPS // 2) as i:
                    for b in range(2):
                        sp.wait_ge(s["rows_ready"], at(i, 2, b + 1))
                        sp.dma_start(ring[:, b].rearrange("p k n -> p (k n)"),
                                     slab(g.d["w_mod"], i * 2 + b)).then_inc(s["w_loaded"][b], 16)

            @block.tensor
            def _(pe):
                pe.sem_inc(s["rows_ready"], 2)
                with pe.Fori(0, STEPS // 2) as i:
                    for b in range(2):
                        pe.wait_ge(s["w_loaded"][b], at(i, 16, 16))
                        pe.wait_ge(s["rows_copied"], at(i, 2, b + 1))
                        for k in range(NB):
                            last = nc.tensor.matmul(bank[b][0:2, 0:NS], g.silu[:, k, :], ring[:, b, k, :],
                                                    start=(k == 0), stop=(k == NB - 1))
                        last.then_inc(s["rows_ready"], 1)
                        pe.wait_ge(s["rows_copied"], at(i, 2, b + 3))
                        wait_alone(pe, s["cols_added"], at(i, 2, b + 1), s["passed"])
                        for n in range(NS // P):
                            last = nc.tensor.transpose(bank[2 + b][:, 2 * n:2 * n + 2], rows[0:2, b, n * P:(n + 1) * P],
                                                       g.ident[0:2, 0:2])
                        last.then_inc(s["cols_ready"], 1)

            @block.scalar
            def _(act):
                act.sem_inc(s["rows_copied"], 2)
                with act.Fori(0, STEPS // 2) as i:
                    for b in range(2):
                        act.wait_ge(s["rows_ready"], at(i, 2, b + 3))
                        nc.scalar.copy(rows[0:2, b, :], bank[b][0:2, 0:NS]).then_inc(s["rows_copied"], 1)

            @block.vector
            def _(dve):
                dve.sem_inc(s["cols_added"], 2)
                with dve.Fori(0, STEPS // 2) as i:
                    for b in range(2):
                        dve.wait_ge(s["cols_ready"], at(i, 2, b + 1))
                        for c in range(2):
                            last = nc.vector.tensor_tensor(
                                g.mods[:, bass.ds(i * 8 + 4 * b, 4), c:c + 1].rearrange("p n o -> p (n o)"),
                                bank[2 + b][:, c:8:2],
                                g.bmod[:, bass.ds(i * 8 + 4 * b, 4)], ALU.add)
                        last.then_inc(s["cols_added"], 1)
                dve.wait_ge(s["cols_added"], STEPS + 2)
                for layer in range(DEPTH):
                    for piece in (1, 4):
                        part = g.mods[:, mod_at(layer, piece):mod_at(layer, piece) + NB, :]
                        nc.vector.tensor_scalar_add(part, part, 1.0)


def modulate_blocks(dve, nc, g, ready, scale, shift, done=None):
    for b in range(NB):
        ready(b)
        for c, (hs, xs) in enumerate(((H_LAT, S_LAT), (H_CTX, S_CTX))):
            last = nc.vector.tensor_scalar(g.h[:, b, hs], g.x[:, b, xs], g.mods[:, scale + b, c:c + 1],
                                           g.mods[:, shift + b, c:c + 1], ALU.mult, ALU.add)
        if done is not None:
            last.then_inc(done, 1)


def first_modulate(nc, g):
    with phase(nc, "unused"), nc.Block() as block:

        @block.vector
        def _(dve):
            modulate_blocks(dve, nc, g, lambda b: None, mod_at(0, 1), mod_at(0, 0))




def h_cols(g):
    return lambda k: (g.h[:, k, H_LAT], g.h[:, k, H_CTX])


def plain_cols(buf):
    return lambda k: (buf[:, k, S_LAT], buf[:, k, S_CTX])


def projection(nc, g, w, n_pairs, kg, src, out=None, hidden=None, mix=None, load=None):
    SLOTS = min(4, 2 * kg)
    VISITS = 2 * kg // SLOTS
    names = ["w_loaded:%d" % SLOTS, "mm_done", "evacuated", "stored:4", "squared", "mixed", "src_loaded"]
    with buffers(nc) as (sb, banks), phase(nc, *names) as s:
        ring = sb("ring", SLOTS, NB, 2 * P)
        stage = sb("stage", 4, T)
        bank = banks(8)
        acc = [(bank[2 * u], bank[2 * u + 1]) for u in range(4)]
        with nc.Block() as block:

            @block.sync
            def _(sp):
                if load is not None:
                    for b in range(NB):
                        sp.dma_start(load[0][:, b, :], load[1][b]).then_inc(s["src_loaded"], 16)
                with sp.Fori(0, n_pairs // 2) as i:
                    for n in range(2 * kg):
                        sp.wait_ge(s["mm_done"], at(i, 4 * kg, 2 * n + 2))
                        sp.dma_start(ring[:, n % SLOTS].rearrange("p k n -> p (k n)"),
                                     slab(w, i * (2 * kg) + n)).then_inc(s["w_loaded"][n % SLOTS], 16)

            @block.tensor
            def _(pe):
                pe.sem_inc(s["mm_done"], 2 * SLOTS)
                if mix is not None:
                    pe.wait_ge(s["mixed"], NB)
                if load is not None:
                    pe.wait_ge(s["src_loaded"], 16 * NB)
                with pe.Fori(0, n_pairs // 2) as i:
                    for n in range(2 * kg):
                        pair, part = divmod(n, kg)
                        pe.wait_ge(s["w_loaded"][n % SLOTS], at(i, 16 * VISITS, 16 * (n // SLOTS + 1)))
                        for m in range(2):
                            u = 2 * pair + m
                            if part == 0:
                                pe.wait_ge(s["evacuated"], at(i, 4, u + 1))
                            for k in range(NB):
                                lat, ctx = src(part * NB + k)
                                wt = ring[:, n % SLOTS, k, m * P:(m + 1) * P]
                                first, end = part == 0 and k == 0, part == kg - 1 and k == NB - 1
                                nc.tensor.matmul(acc[u][0][:, :], wt, lat, start=first, stop=end)
                                last = nc.tensor.matmul(acc[u][1][:, 0:CTX], wt, ctx, start=first, stop=end)
                            last.then_inc(s["mm_done"], 1)

            @block.scalar
            def _(act):
                act.sem_inc(s["evacuated"], 4)
                if hidden is None:
                    for u in range(4):
                        act.sem_inc(s["stored"][u], 16)
                with act.Fori(0, n_pairs // 2) as i:
                    for u in range(4):
                        pair, m = divmod(u, 2)
                        act.wait_ge(s["mm_done"], at(i, 4 * kg, 2 * SLOTS + 2 * (pair * kg + kg - 1) + m + 1))
                        if hidden is None:
                            act.wait_ge(s["stored"][u], at(i, 16, 16))
                        else:
                            act.wait_ge(s["squared"], at(i, 4, u + 1))
                        fn = ACT.Copy if hidden is None else ACT.Relu
                        nc.scalar.activation(stage[:, u, S_LAT], acc[u][0][:, :], fn)
                        nc.scalar.activation(stage[:, u, S_CTX], acc[u][1][:, 0:CTX], fn).then_inc(s["evacuated"], 1)
                        if hidden is None:
                            act.wait_ge(s["evacuated"], at(i, 4, u + 5))
                            act.dma_start(slab(out, i * 4 + u), stage[:, u, :]).then_inc(s["stored"][u], 16)
                if hidden is None:
                    for u in range(4):
                        act.wait_ge(s["stored"][u], 16 * (n_pairs // 2 + 1))

            @block.vector
            def _(dve):
                if mix is not None:
                    buf, col = mix
                    for b in range(NB):
                        nc.vector.scalar_tensor_tensor(buf[:, b, :], g.xx[:, b, :], g.vec[:, col + b:col + b + 1],
                                                       g.h[:, b, :], ALU.mult, ALU.add).then_inc(s["mixed"], 1)
                if hidden is not None:
                    dve.sem_inc(s["squared"], 4)
                    with dve.Fori(0, n_pairs // 2) as i:
                        for u in range(4):
                            dve.wait_ge(s["evacuated"], at(i, 4, u + 5))
                            nc.vector.tensor_tensor(hidden[:, bass.ds(i * 4 + u, 1), :].rearrange("p o t -> p (o t)"),
                                                    stage[:, u, :], stage[:, u, :], ALU.mult).then_inc(s["squared"], 1)




def norm(nc, g, delta, layer, sub, gate, nxt):
    col = V_LN + (layer * 2 + sub) * 2 * NB
    names = ["loaded", "gated", "added", "sums", "centred", "squares", "variances", "root", "inverse",
             "scaled", "gained", "stored"]
    with buffers(nc) as (sb, banks), phase(nc, *names) as s:
        dl = sb("delta", NB, T)
        rs = sb("rstd", T)
        mean_l, mean_c, var_l, var_c = banks(4)
        parts = ((S_LAT, mean_l, var_l, LAT), (S_CTX, mean_c, var_c, CTX))
        with nc.Block() as block:

            @block.sync
            def _(sp):
                for b in range(NB):
                    sp.dma_start(dl[:, b, :], delta[b]).then_inc(s["loaded"], 16)
                if nxt is None:
                    for b in range(NB):
                        sp.wait_ge(s["gained"], b + 1)
                        sp.dma_start(g.d["y_out"][b], g.x[:, b, :]).then_inc(s["stored"], 16)
                    sp.wait_ge(s["stored"], 16 * NB)

            @block.scalar
            def _(act):
                act.wait_ge(s["loaded"], 16 * NB)
                for b in range(NB):
                    for c, (cols, _, _, _) in enumerate(parts):
                        last = nc.scalar.activation(dl[:, b, cols], dl[:, b, cols], ACT.Identity,
                                                    scale=g.mods[:, gate + b, c:c + 1])
                    last.then_inc(s["gated"], 1)
                for b in range(NB):
                    act.wait_ge(s["centred"], b + 1)
                    nc.scalar.activation(dl[:, b, :], g.x[:, b, :], ACT.Square).then_inc(s["squares"], 1)
                act.wait_ge(s["variances"], 1)
                for cols, _, var, n in parts:
                    nc.scalar.activation(rs[:, cols], var[:, 0:n], ACT.Sqrt, bias=g.eps_ln).then_inc(s["root"], 1)
                for b in range(NB):
                    act.wait_ge(s["scaled"], b + 1)
                    nc.scalar.activation(g.x[:, b, :], g.x[:, b, :], ACT.Identity, scale=g.vec[:, col + b:col + b + 1],
                                         bias=g.vec[:, col + NB + b:col + NB + b + 1]).then_inc(s["gained"], 1)

            @block.tensor
            def _(pe):
                for b in range(NB):
                    pe.wait_ge(s["added"], b + 1)
                    for cols, mean, _, n in parts:
                        last = nc.tensor.matmul(mean[:, 0:n], g.mean_w, g.x[:, b, cols], start=(b == 0), stop=(b == NB - 1))
                last.then_inc(s["sums"], 1)
                for b in range(NB):
                    pe.wait_ge(s["squares"], b + 1)
                    for cols, _, var, n in parts:
                        last = nc.tensor.matmul(var[:, 0:n], g.mean_w, dl[:, b, cols], start=(b == 0), stop=(b == NB - 1))
                last.then_inc(s["variances"], 1)

            @block.vector
            def _(dve):
                for b in range(NB):
                    dve.wait_ge(s["gated"], b + 1)
                    nc.vector.scalar_tensor_tensor(g.x[:, b, :], g.x[:, b, :], ALPHA, dl[:, b, :],
                                                   ALU.mult, ALU.add).then_inc(s["added"], 1)
                dve.wait_ge(s["sums"], 1)
                for b in range(NB):
                    for cols, mean, _, n in parts:
                        last = nc.vector.tensor_tensor(g.x[:, b, cols], g.x[:, b, cols], mean[:, 0:n], ALU.subtract)
                    last.then_inc(s["centred"], 1)
                dve.wait_ge(s["root"], 2)
                nc.vector.reciprocal(rs[:, :], rs[:, :]).then_inc(s["inverse"], 1)
                dve.wait_ge(s["inverse"], 1)
                for b in range(NB):
                    nc.vector.tensor_tensor(g.x[:, b, :], g.x[:, b, :], rs[:, :], ALU.mult).then_inc(s["scaled"], 1)
                if nxt is not None:
                    modulate_blocks(dve, nc, g, lambda b: dve.wait_ge(s["gained"], b + 1), *nxt)




def chunked(ap):
    return ap.rearrange("p (u c) -> p u c", c=C)


def by_direction(buf, plain):
    yield buf[:, :, 0, :], chunked(plain)
    yield buf[:, 0:NLAT, 1, :], chunked(plain[:, S_LAT][:, ::-1])
    yield buf[:, NLAT:NCHUNK, 1, :], chunked(plain[:, S_CTX][:, ::-1])


def unit(u, hh):
    return GROUP * (u // 2) + 2 * hh + u % 2


def flat4(ap):
    return ap.rearrange("p u n -> p (u n)")


INVERSE_SEMS = ["first_t", "first_n_ps", "xx_ready", "y_ps", "ly_ready", "x_ps", "inv_ready"]
PER_GROUP = dict(first_t=2, first_n_ps=2, xx_ready=2 + 2 * (LEVELS - 1), y_ps=2 * LEVELS, ly_ready=2 * LEVELS,
                 x_ps=2 * LEVELS, inv_ready=2)


def group_at(i, j, name, k):
    return at(i, PER_GROUP[name] * NGROUP, PER_GROUP[name] * j + k)


def invert_pe(pe, nc, g, s, w, i, j):
    for h in range(2):
        pe.wait_ge(s["first_t"], group_at(i, j, "first_t", h + 1))
        for n in range(2):
            last = nc.tensor.transpose(w.y_bank[h][:, n * P:(n + 1) * P], w.xx[:, h, 1, n, :], g.ident)
        last.then_inc(s["first_n_ps"], 1)
    for lv in range(LEVELS):
        for h in range(2):
            pe.wait_ge(s["xx_ready"], group_at(i, j, "xx_ready", 2 * lv + h + 1))
            for n in range(2):
                last = nc.tensor.matmul(w.y_bank[h][:, n * P:(n + 1) * P], w.lt[:, 2 * h + n, :], w.xx[:, h, 0, n, :],
                                        start=True, stop=True)
            last.then_inc(s["y_ps"], 1)
        for h in range(2):
            pe.wait_ge(s["ly_ready"], group_at(i, j, "ly_ready", 2 * lv + h + 1))
            for n in range(2):
                last = nc.tensor.matmul(w.x_bank[h][:, (2 + n) * P:(3 + n) * P], w.y[:, h, n, :], w.xx[:, h, 1, n, :],
                                        start=True, stop=True)
            if lv < LEVELS - 1:
                for n in range(2):
                    last = nc.tensor.matmul(w.x_bank[h][:, n * P:(n + 1) * P], w.xx[:, h, 1, n, :], w.y[:, h, n, :],
                                            start=True, stop=True)
            last.then_inc(s["x_ps"], 1)


def invert_dve(dve, nc, g, s, w, i, j, link):
    l0 = g.mask(K_L0)
    for h in range(2):
        link(nc.vector.tensor_tensor(w.xx[:, h, 1, :, :], w.lt[:, 2 * h:2 * h + 2, :], l0.unsqueeze(1).to_broadcast([P, 2, P]),
                                     ALU.mult))
        nc.vector.tensor_tensor(w.xx[:, h, 1, :, :], w.xx[:, h, 1, :, :],
                                g.ident.unsqueeze(1).to_broadcast([P, 2, P]), ALU.add).then_inc(s["first_t"], 1)
    for h in range(2):
        dve.wait_ge(s["first_n_ps"], group_at(i, j, "first_n_ps", h + 1))
        nc.vector.tensor_copy(flat4(w.xx[:, h, 0, :, :]), w.y_bank[h][:, 0:2 * P]).then_inc(s["xx_ready"], 1)
    for lv in range(LEVELS):
        below = g.mask(K_LV + lv * P)
        for h in range(2):
            dve.wait_ge(s["y_ps"], group_at(i, j, "y_ps", 2 * lv + h + 1))
            nc.vector.tensor_tensor(w.y[:, h, :, :], w.y_bank[h][:, 0:2 * P].rearrange("p (n c) -> p n c", n=2),
                                    below.unsqueeze(1).to_broadcast([P, 2, P]), ALU.mult).then_inc(s["ly_ready"], 1)
        for h in range(2):
            dve.wait_ge(s["x_ps"], group_at(i, j, "x_ps", 2 * lv + h + 1))
            if lv < LEVELS - 1:
                both = w.xx[:, h].rearrange("p t n c -> p (t n c)")
                nc.vector.tensor_tensor(both, w.x_bank[h][:, :], both, ALU.add).then_inc(s["xx_ready"], 1)
            else:
                out = w.tt[:, GROUP * j + 2 * h:GROUP * j + 2 * h + 2, :]
                nc.vector.tensor_tensor(flat4(out), w.x_bank[h][:, 2 * P:4 * P], flat4(w.xx[:, h, 1, :, :]),
                                        ALU.add).then_inc(s["inv_ready"], 1)


class Work:
    pass



W_W0, W_A0, W_KK, W_KA, W_RK, W_GG, W_GB = 0, 2, 4, 5, 6, 7, 8
W_COLS = 9
W_END = 3 * P + W_COLS


def token_shift(nc, g):
    with phase(nc, "neighbours") as s, nc.Block() as block:

        @block.vector
        def _(dve):
            nc.vector.memset(g.xx[:, :, :], 0.0).then_inc(s["neighbours"], 1)
            for edge in (slice(0, 1), slice(H_LAT.stop, H_CTX.start), slice(H_CTX.stop, HW)):
                nc.vector.memset(g.h[:, :, edge], 0.0).then_inc(s["neighbours"], 1)
            dve.wait_ge(s["neighbours"], 4)
            for b in range(NB):
                nc.vector.tensor_tensor(g.xx[:, b, 1:HW - 1], g.h[:, b, 0:HW - 2], g.h[:, b, 2:HW],
                                        ALU.add).then_inc(s["neighbours"], 1)
            for b in range(NB):
                dve.wait_ge(s["neighbours"], b + 5)
                nc.vector.scalar_tensor_tensor(g.xx[:, b, 1:HW - 1], g.xx[:, b, 1:HW - 1], 0.5, g.h[:, b, 1:HW - 1],
                                               ALU.mult, ALU.subtract)


def low_rank(nc, g, j, low):
    with buffers(nc) as (sb, banks), phase(nc, "loaded", "mixed", "mm_done", "evacuated") as s:
        wt = sb("low_w", 3, NB, P)
        xi = sb("low_x", 2, NB, HW)
        bank = banks(4)
        with nc.Block() as block:

            @block.sync
            def _(sp):
                sp.dma_start(wt[:, :, :, :].rearrange("p a k n -> p a (k n)"),
                             g.d["rw_low"][3 * j:3 * j + 3].rearrange("a p n -> p a n")).then_inc(s["loaded"], 16)

            @block.vector
            def _(dve):
                for n, m in enumerate((1, 4, 5)):
                    if n >= 2:
                        dve.wait_ge(s["mm_done"], n - 1)
                    for b in range(NB):
                        col = V_MU + (j * 6 + m) * NB + b
                        last = nc.vector.scalar_tensor_tensor(xi[:, n % 2, b, :], g.xx[:, b, :], g.vec[:, col:col + 1],
                                                              g.h[:, b, :], ALU.mult, ALU.add)
                    last.then_inc(s["mixed"], 1)

            @block.tensor
            def _(pe):
                pe.wait_ge(s["loaded"], 16)
                for n in range(3):
                    pe.wait_ge(s["mixed"], n + 1)
                    if n >= 2:
                        pe.wait_ge(s["evacuated"], n - 1)
                    for k in range(NB):
                        nc.tensor.matmul(bank[2 * (n % 2)][:, :], wt[:, n, k, :], xi[:, n % 2, k, H_LAT],
                                         start=(k == 0), stop=(k == NB - 1))
                        last = nc.tensor.matmul(bank[2 * (n % 2) + 1][:, 0:CTX], wt[:, n, k, :], xi[:, n % 2, k, H_CTX],
                                                start=(k == 0), stop=(k == NB - 1))
                    last.then_inc(s["mm_done"], 1)

            @block.scalar
            def _(act):
                for n, fn in enumerate((ACT.Tanh, ACT.Copy, ACT.Sigmoid)):
                    act.wait_ge(s["mm_done"], n + 1)
                    nc.scalar.activation(low[:, n, S_LAT], bank[2 * (n % 2)][:, :], fn)
                    nc.scalar.activation(low[:, n, S_CTX], bank[2 * (n % 2) + 1][:, 0:CTX], fn).then_inc(s["evacuated"], 1)


STEPS = NCHUNK
ORDER = (8, 9, 0, 1, 2, 3, 4, 5, 6, 7)


def rwkv_heads(nc, g, j, low):
    names = ["passed", "in_loaded", "y_stored", "state_stored", "link", "squares", "projected", "sums", "sig_w", "sig_a", "gates",
             "roots", "scanned", "g_before", "exps", "reversed_v", "bonus_in", "bonus_sums", "bonus", "operands",
             "products", "masked", "tokens", "tokens_out", "chain_x", "x_out", "chain_sa", "sa_out", "chain_s",
             "s0_ready", "s1_ready", "s_first", "values", "saz_out", "o_done", "s_saved", "y_in", "means", "y_centred", "y_squares", "vars", "y_root", "y_ready",
             ] + INVERSE_SEMS
    with buffers(nc) as (sb, banks), phase(nc, *names) as s:
        w = Work()
        rkv, hw, s0 = sb("rkv", 3, T), sb("head_w", W_END), sb("s0", 2, C)
        t1, rn, bs, os_, sq = (sb(n, T) for n in ("t1", "rn", "bs", "os", "sq"))
        ld, icl, gc, e_in, kk, kd, ve, rt, kt, at_, bt = (
            sb(n, NCHUNK, 2, C) for n in ("ld", "icl", "gc", "e_in", "kk2", "kd", "ve", "rt", "kt", "at", "bt"))
        two = sb("e_ex_inv", 2 * NCHUNK, 2, C)
        e_ex, e_inv, vz = two[:, 0:NCHUNK], two[:, NCHUNK:2 * NCHUNK], two
        w.lt, w.xx, w.y = sb("lt", GROUP, P), sb("xx", 2, 2, 2, P), sb("y", 2, 2, P)
        w.tt, ak, rr = sb("tt", 2 * NCHUNK, P), sb("ak", 2 * NCHUNK, P), sb("rr", 2, 2 * NCHUNK, P)
        spare = g.h[:, :, :].rearrange("p b t -> p (b t)")
        tok = spare[:, 0:3 * TT].rearrange("p (u q c) -> p u q c", q=3, c=C)
        bon, gate = spare[:, 3 * TT:3 * TT + T], spare[:, 3 * TT + T:4 * TT]
        xs, sa, saz = sb("xs", 2, C), sb("sa", 2, C), sb("saz", 2, 2, C)
        st = sb("state", 2, 2, C)
        sout = sb("sout", 2, C)
        bank = banks(8)
        w.y_bank, w.x_bank = bank[0:2], bank[2:4]
        lat_banks, ctx_bank = (bank[2], bank[4], bank[5], bank[6]), (bank[3], bank[0])
        r, k, v = rkv[:, 0, :], rkv[:, 1, :], rkv[:, 2, :]
        hcol = lambda n: hw[:, 3 * P + n:3 * P + n + 1]
        flat = lambda buf: buf[:, 0:NCHUNK, :, :].rearrange("p u e c -> p (u e c)")

        with nc.Block() as block:

            @block.sync
            def _(sp):
                sp.sem_inc(s["y_stored"], 16)
                with sp.Fori(0, NB) as i:
                    wait_alone(sp, s["y_stored"], at(i, 16, 16), s["passed"])
                    for n in range(3):
                        sp.dma_start(rkv[:, n, :], slab(g.d["rkv"], i + n * NB)).then_inc(s["in_loaded"], 16)
                    sp.dma_start(hw[:, :], slab(g.d["rw_head"], i + j * NB)).then_inc(s["in_loaded"], 16)
                    sp.dma_start(s0[:, :, :].rearrange("p e v -> p (e v)"),
                                 slab(g.d["rw_state"], i + j * NB)).then_inc(s["in_loaded"], 16)
                    wait_alone(sp, s["s_saved"], at(i, 2, 2), s["passed"])
                    sp.dma_start(slab(g.d["rw_state_out"], i + j * NB),
                                 sout[:, :, :].rearrange("p e v -> p (e v)")).then_inc(s["state_stored"], 16)
                    wait_alone(sp, s["state_stored"], at(i, 16, 16), s["passed"])
                    sp.wait_ge(s["y_ready"], at(i, 1, 1))
                    sp.dma_start(slab(g.d["mixed"], i), os_[:, :]).then_inc(s["y_stored"], 16)
                sp.wait_ge(s["y_stored"], 16 * (NB + 1))

            @block.gpsimd
            def _(pool):
                with pool.Fori(0, NB) as i:
                    wait_alone(pool, s["in_loaded"], at(i, 80, 80), s["passed"])
                    for both, plain in by_direction(ve, v):
                        nc.gpsimd.tensor_copy(both, plain).then_inc(s["reversed_v"], 1)
                    for jg in range(NGROUP):
                        wait_alone(pool, s["tokens_out"], at(i, NGROUP, jg + 1), s["passed"])
                        for e in range(2):
                            nc.gpsimd.tensor_tensor(
                                vz[:, GROUP * jg:GROUP * (jg + 1), e, :], tok[:, GROUP * jg:GROUP * (jg + 1), 1, :],
                                g.const[:, K_BO + e * C:K_BO + (e + 1) * C].unsqueeze(1).to_broadcast([P, GROUP, C]),
                                ALU.mult).then_inc(s["values"], 1)

            @block.scalar
            def _(act):
                with act.Fori(0, NB) as i:
                    act.wait_ge(s["projected"], at(i, 1, 1))
                    for buf, base, col, done in ((ld, 0, W_W0, s["sig_w"]), (icl, 2, W_A0, s["sig_a"])):
                        for e in range(2):
                            lat_bank, ctx_cols = lat_banks[base + e], ctx_bank[e][:, base * C:base * C + P]
                            turn = slice(None, None, -1 if e else 1)
                            nc.scalar.activation(buf[:, 0:NLAT, e, :], chunked(lat_bank[:, turn]), ACT.Sigmoid,
                                                 bias=hcol(col + e))
                            nc.scalar.activation(buf[:, NLAT:NCHUNK, e, :], chunked(ctx_cols[:, turn]), ACT.Sigmoid,
                                                 bias=hcol(col + e)).then_inc(done, 1)
                    nc.scalar.copy(gate[:, S_LAT], bank[7][:, :])
                    nc.scalar.copy(gate[:, S_CTX], bank[1][:, P:2 * P]).then_inc(s["gates"], 1)
                    act.wait_ge(s["sums"], at(i, 1, 1))
                    nc.scalar.activation(rn[:, S_LAT], bank[0][:, :], ACT.Sqrt, bias=g.eps_nrm)
                    nc.scalar.activation(rn[:, S_CTX], bank[1][:, 0:CTX], ACT.Sqrt, bias=g.eps_nrm).then_inc(s["roots"], 1)
                    act.wait_ge(s["scanned"], at(i, 1, 1))
                    nc.scalar.activation(flat(e_in), flat(gc), ACT.Exp).then_inc(s["exps"], 1)
                    nc.scalar.activation(flat(e_inv), flat(gc), ACT.Exp, scale=-1.0).then_inc(s["exps"], 1)
                    act.wait_ge(s["g_before"], at(i, 1, 1))
                    nc.scalar.activation(flat(e_ex), flat(ld), ACT.Exp).then_inc(s["exps"], 1)
                    for jg in range(NGROUP):
                        act.wait_ge(s["tokens"], at(i, 2 * NGROUP, 2 * jg + 2))
                        for hh in range(2):
                            u2 = slice(GROUP * jg + 2 * hh, GROUP * jg + 2 * hh + 2)
                            last = nc.scalar.copy(tok[:, u2, :, :].rearrange("p u q c -> p (u q c)"),
                                                  bank[4 + hh][:, 0:6 * C])
                        last.then_inc(s["tokens_out"], 1)
                    for n in range(STEPS):
                        u = ORDER[n]
                        act.wait_ge(s["chain_s"], at(i, STEPS, n + 1))
                        for e in range(2):
                            last = nc.scalar.activation(st[0:C, e, 0, :], bank[2][0:C, e * C:(e + 1) * C], ACT.Identity,
                                                        scale=e_in[0:C, u, e, C - 1:C])
                        last.then_inc(s["s_first"] if n == 1 else s["s0_ready"], 1)
                    act.wait_ge(s["vars"], at(i, 1, 1))
                    nc.scalar.activation(rn[:, S_LAT], bank[2][:, :], ACT.Sqrt, bias=g.eps_gn)
                    nc.scalar.activation(rn[:, S_CTX], bank[3][:, 0:CTX], ACT.Sqrt, bias=g.eps_gn).then_inc(s["y_root"], 1)

            @block.tensor
            def _(pe):
                def project(dst_l, dst_c, weights, rows, n):
                    nc.tensor.matmul(dst_l, weights, low[rows, n, S_LAT], start=True, stop=True)
                    return nc.tensor.matmul(dst_c, weights, low[rows, n, S_CTX], start=True, stop=True)

                def head_sums(src, lat, ctx):
                    nc.tensor.matmul(lat, g.mask(K_BO), src[:, S_LAT], start=True, stop=True)
                    return nc.tensor.matmul(ctx, g.mask(K_BO), src[:, S_CTX], start=True, stop=True)

                def pair(buf, rows, u):
                    return buf[rows, u, :, :].rearrange("p e c -> p (e c)")

                with pe.Fori(0, NB) as i:
                    pe.wait_ge(s["in_loaded"], at(i, 80, 80))
                    for e in range(2):
                        rows = slice(C * e, C * (e + 1))
                        project(lat_banks[e][:, :], ctx_bank[e][:, 0:P], hw[rows, 0:P], rows, 0)
                        project(lat_banks[2 + e][:, :], ctx_bank[e][:, P:2 * P], hw[rows, P:2 * P], rows, 1)
                    project(bank[7][:, :], bank[1][:, P:2 * P], hw[:, 2 * P:3 * P], slice(0, P), 2).then_inc(s["projected"], 1)
                    pe.wait_ge(s["squares"], at(i, 1, 1))
                    pe.wait_ge(s["gates"], at(i, 1, 1))
                    head_sums(sq, bank[0][:, :], bank[1][:, 0:CTX]).then_inc(s["sums"], 1)
                    pe.wait_ge(s["bonus_in"], at(i, 1, 1))
                    pe.wait_ge(s["roots"], at(i, 1, 1))
                    head_sums(bs, bank[0][:, :], bank[1][:, 0:CTX]).then_inc(s["bonus_sums"], 1)
                    pe.wait_ge(s["operands"], at(i, 7, 7))
                    pe.wait_ge(s["reversed_v"], at(i, 3, 3))
                    pe.wait_ge(s["bonus"], at(i, 1, 1))
                    for jg in range(NGROUP):
                        if jg >= 1:
                            pe.wait_ge(s["inv_ready"], group_at(i, jg - 1, "inv_ready", 2))
                            pe.wait_ge(s["tokens_out"], at(i, NGROUP, jg))
                        for hh in range(2):
                            hr = slice(C * hh, C * (hh + 1))
                            for q, (left, right) in enumerate(((bt, at_), (kt, at_), (kt, rt), (bt, rt))):
                                for n in range(2):
                                    c0 = (2 * (q % 2) + n) * P
                                    last = nc.tensor.matmul(bank[2 * hh + q // 2][:, c0:c0 + P], pair(left, hr, 2 * jg + n),
                                                            pair(right, hr, 2 * jg + n), start=True, stop=True)
                            last.then_inc(s["products"], 1)
                        for hh in range(2):
                            hr = slice(C * hh, C * (hh + 1))
                            for n in range(2):
                                for q, src in enumerate((kt, ve, bt)):
                                    c0 = (3 * n + q) * C
                                    last = nc.tensor.transpose(bank[4 + hh][:, c0:c0 + C], pair(src, hr, 2 * jg + n),
                                                               g.const[hr, K_ID + hr.start:K_ID + hr.stop])
                            last.then_inc(s["tokens"], 1)
                        pe.wait_ge(s["masked"], at(i, 6 * NGROUP, 6 * jg + 6))
                        invert_pe(pe, nc, g, s, w, i, jg)
                    pe.wait_ge(s["inv_ready"], group_at(i, NGROUP - 1, "inv_ready", 2))
                    pe.wait_ge(s["tokens_out"], at(i, NGROUP, NGROUP))
                    pe.wait_ge(s["values"], at(i, 2 * NGROUP, 2 * NGROUP))
                    for n in range(STEPS):
                        u = ORDER[n]
                        uks = [unit(u, hh) for hh in range(2)]
                        o_tile = bank[4 + u // 4][:, (u % 4) * P:(u % 4 + 1) * P]
                        if n:
                            pe.wait_ge(s["s0_ready"], at(i, STEPS, n))
                            pe.wait_ge(s["s1_ready"], at(i, STEPS, n))
                        for hh, uk in enumerate(uks):
                            dst = bank[0][:, hh * P:(hh + 1) * P]
                            nc.tensor.matmul(dst, pair(at_, slice(0, P), u), st[:, :, hh, :], start=True, stop=False)
                            last = nc.tensor.matmul(dst, ak[:, uk, :], tok[:, uk, 1, :].unsqueeze(1).to_broadcast([P, 2, C]),
                                                    start=False, stop=True)
                        last.then_inc(s["chain_x"], 1)
                        for hh, uk in enumerate(uks):
                            hr = slice(C * hh, C * (hh + 1))
                            nc.tensor.matmul(o_tile[hr, :], tok[:, uk, 1, :], rr[:, 0, uk, :], start=True, stop=False,
                                             skip_group_check=True)
                        for e in range(2):
                            nc.tensor.matmul(o_tile[:, e * C:(e + 1) * C], st[:, e, :, :].rearrange("p h v -> p (h v)"),
                                             rt[:, u, e, :], start=False, stop=False, skip_group_check=True)
                        pe.wait_ge(s["x_out"], at(i, 2 * STEPS, 2 * n + 2))
                        for hh, uk in enumerate(uks):
                            last = nc.tensor.matmul(bank[1][:, hh * P:(hh + 1) * P], w.tt[:, uk, :],
                                                    xs[:, hh, :].unsqueeze(1).to_broadcast([P, 2, C]), start=True, stop=True)
                        last.then_inc(s["chain_sa"], 1)
                        for hh, uk in enumerate(uks):
                            hr = slice(C * hh, C * (hh + 1))
                            nc.tensor.matmul(bank[2][hr, 0:P], g.ident[:, hr], st[:, :, hh, :], start=True, stop=False)
                            nc.tensor.matmul(bank[2][hr, 0:P], tok[:, uk, 0, :], pair(vz, slice(0, P), uk), start=False, stop=False)
                        pe.wait_ge(s["saz_out"], at(i, STEPS, n + 1))
                        for hh, uk in enumerate(uks):
                            hr = slice(C * hh, C * (hh + 1))
                            last = nc.tensor.matmul(bank[2][hr, 0:P], tok[:, uk, 2, :], pair(saz, slice(0, P), hh),
                                                    start=False, stop=True)
                        last.then_inc(s["chain_s"], 1)
                        pe.wait_ge(s["sa_out"], at(i, STEPS, n + 1))
                        for hh, uk in enumerate(uks):
                            hr = slice(C * hh, C * (hh + 1))
                            last = nc.tensor.matmul(o_tile[hr, :], sa[:, hh, :], rr[:, 1, uk, :], start=False, stop=True,
                                                    skip_group_check=True)
                        last.then_inc(s["o_done"], 1)
                    pe.wait_ge(s["y_in"], at(i, 3, 3))
                    head_sums(os_, bank[0][:, :], bank[1][:, 0:CTX]).then_inc(s["means"], 1)
                    pe.wait_ge(s["y_squares"], at(i, 1, 1))
                    pe.wait_ge(s["s0_ready"], at(i, STEPS, STEPS))
                    pe.wait_ge(s["s1_ready"], at(i, STEPS, STEPS))
                    nc.tensor.matmul(bank[2][:, :], g.mask(K_BO), sq[:, S_LAT], start=True, stop=True)
                    nc.tensor.matmul(bank[3][:, 0:CTX], g.mask(K_BO), sq[:, S_CTX], start=True, stop=True).then_inc(s["vars"], 1)

            @block.vector
            def _(dve):
                with dve.Fori(0, NB) as i:
                    link = Link(dve, s["link"], i, LINKS_RW)
                    dve.wait_ge(s["in_loaded"], at(i, 80, 80))
                    link(nc.vector.tensor_scalar(t1[:, :], k, hcol(W_KK), None, ALU.mult))
                    nc.vector.tensor_tensor(sq[:, :], t1[:, :], t1[:, :], ALU.mult).then_inc(s["squares"], 1)
                    dve.wait_ge(s["sig_w"], at(i, 2, 2))
                    link(nc.vector.tensor_scalar(flat(ld), flat(ld), -HALF_DECAY, None, ALU.mult))
                    nc.vector.tensor_tensor_scan(flat(gc), g.const[:, K_SCAN:K_SCAN + TT], flat(ld), 0.0,
                                                 ALU.mult, ALU.add).then_inc(s["scanned"], 1)
                    dve.wait_ge(s["scanned"], at(i, 1, 1))
                    nc.vector.tensor_tensor(flat(ld), flat(gc), flat(ld), ALU.subtract).then_inc(s["g_before"], 1)
                    dve.wait_ge(s["sig_a"], at(i, 2, 2))
                    link(nc.vector.tensor_scalar(flat(kd), flat(icl), -1.0, hcol(W_KA), ALU.add, ALU.mult))
                    for both, plain in by_direction(kd, k):
                        last = nc.vector.scalar_tensor_tensor(both, both, 1.0, plain, ALU.add, ALU.mult)
                    link(last)
                    for us in (slice(0, NLAT), slice(NLAT, NCHUNK)):
                        last = nc.vector.tensor_tensor(chunked(bs[:, :])[:, us, :], kd[:, us, 0, :],
                                                       kd[:, us, 1, :][:, ::-1, ::-1], ALU.add)
                    link(last)
                    nc.vector.scalar_tensor_tensor(bs[:, :], r, hcol(W_RK), bs[:, :], ALU.mult, ALU.mult).then_inc(s["bonus_in"], 1)
                    dve.wait_ge(s["roots"], at(i, 1, 1))
                    link(nc.vector.reciprocal(rn[:, :], rn[:, :]))
                    for (both, plain), (_, root) in zip(by_direction(kk, t1[:, :]), by_direction(kk, rn[:, :])):
                        last = nc.vector.tensor_tensor(both, plain, root, ALU.mult)
                    link(last)
                    dve.wait_ge(s["bonus_sums"], at(i, 1, 1))
                    nc.vector.tensor_tensor(bon[:, S_LAT], bank[0][:, :], v[:, S_LAT], ALU.mult)
                    nc.vector.tensor_tensor(bon[:, S_CTX], bank[1][:, 0:CTX], v[:, S_CTX], ALU.mult).then_inc(s["bonus"], 1)
                    link(nc.vector.tensor_tensor(flat(bt), flat(kk), flat(icl), ALU.mult))
                    dve.wait_ge(s["exps"], at(i, 3, 3))
                    nc.vector.scalar_tensor_tensor(flat(bt), flat(bt), -1.0, flat(e_inv), ALU.mult,
                                                   ALU.mult).then_inc(s["operands"], 1)
                    nc.vector.tensor_tensor(flat(at_), flat(kk), flat(e_ex), ALU.mult).then_inc(s["operands"], 1)
                    nc.vector.tensor_tensor(flat(kt), flat(kd), flat(e_inv), ALU.mult).then_inc(s["operands"], 1)
                    for (both, plain), (decay, _) in zip(by_direction(rt, r), by_direction(e_in, r)):
                        nc.vector.tensor_tensor(both, plain, decay, ALU.mult).then_inc(s["operands"], 1)
                    nc.vector.memset(st[:, :, :, :], 0.0).then_inc(s["operands"], 1)
                    for jg in range(NGROUP):
                        for hh in range(2):
                            dve.wait_ge(s["products"], at(i, 2 * NGROUP, 2 * jg + hh + 1))
                            u2 = slice(GROUP * jg + 2 * hh, GROUP * jg + 2 * hh + 2)
                            later = g.mask(K_SP).unsqueeze(1).to_broadcast([P, 2, P])
                            for q, out in enumerate((w.lt[:, 2 * hh:2 * hh + 2, :], ak[:, u2, :])):
                                cols = bank[2 * hh][:, q * 2 * P:(q + 1) * 2 * P].rearrange("p (n c) -> p n c", n=2)
                                nc.vector.tensor_tensor(out, cols, later, ALU.mult).then_inc(s["masked"], 1)
                            nc.vector.tensor_tensor(rr[:, :, u2, :],
                                                    bank[2 * hh + 1][:, :].rearrange("p (q n c) -> p q n c", q=2, n=2),
                                                    g.mask(K_IP).unsqueeze(1).unsqueeze(1).to_broadcast([P, 2, 2, P]),
                                                    ALU.mult).then_inc(s["masked"], 1)
                        dve.wait_ge(s["masked"], at(i, 6 * NGROUP, 6 * jg + 6))
                        invert_dve(dve, nc, g, s, w, i, jg, link)
                    for n in range(STEPS):
                        u = ORDER[n]
                        dve.wait_ge(s["chain_x"], at(i, STEPS, n + 1))
                        for e in range(2):
                            er = slice(C * e, C * (e + 1))
                            nc.vector.tensor_copy(xs[er, :, :], bank[0][er, 0:2 * P].rearrange("p (h n) -> p h n", h=2)[:, :, er]
                                                  ).then_inc(s["x_out"], 1)
                        dve.wait_ge(s["chain_sa"], at(i, STEPS, n + 1))
                        nc.vector.tensor_tensor(saz[:, :, :, :].rearrange("p h e v -> p h (e v)"),
                                                bank[1][:, 0:2 * P].rearrange("p (h n) -> p h n", h=2),
                                                g.mask(K_BO).unsqueeze(1).to_broadcast([P, 2, P]), ALU.mult).then_inc(s["saz_out"], 1)
                        if n >= 1:
                            dve.wait_ge(s["o_done"], at(i, STEPS, n))
                        nc.vector.tensor_copy(sa[:, :, :], bank[1][:, 0:2 * P].rearrange("p (h n) -> p h n", h=2)[:, :, 0:C]
                                              ).then_inc(s["sa_out"], 1)
                        dve.wait_ge(s["chain_s"], at(i, STEPS, n + 1))
                        for e in range(2):
                            last = nc.vector.tensor_scalar(st[C:P, e, 1, :], bank[2][C:P, e * C:(e + 1) * C],
                                                           e_in[C:P, u, e, C - 1:C], None, ALU.mult)
                        if n != 1:
                            last.then_inc(s["s1_ready"], 1)
                            continue
                        link(last)
                        dve.wait_ge(s["s_first"], at(i, 1, 1))
                        dve.wait_ge(s["o_done"], at(i, STEPS, 2))
                        for hh in range(2):
                            hr = slice(C * hh, C * (hh + 1))
                            nc.vector.tensor_copy(sout[hr, :, :], st[hr, :, hh, :]).then_inc(s["s_saved"], 1)
                        dve.wait_ge(s["s_saved"], at(i, 2, 2))
                        for hh, done in enumerate((s["s0_ready"], s["s1_ready"])):
                            hr = slice(C * hh, C * (hh + 1))
                            nc.vector.tensor_copy(st[hr, :, hh, :], s0[hr, :, :]).then_inc(done, 1)
                    dve.wait_ge(s["o_done"], at(i, STEPS, STEPS))
                    tiles = lambda b, m: bank[b][:, 0:m * P].rearrange("p (u e c) -> p u e c", u=m, e=2)
                    spans = ((4, 4, 0, 2 * P), (5, 4, 2 * P, 4 * P), (6, 2, LAT, T))
                    turned = ((4, 4, 2 * P, 4 * P), (5, 4, 0, 2 * P), (6, 2, LAT, T))
                    for b, m, t0, t1_ in spans:
                        last = nc.vector.tensor_copy(chunked(os_[:, t0:t1_]), tiles(b, m)[:, :, 0, :])
                    link(last)
                    for b, m, t0, t1_ in turned:
                        out = chunked(os_[:, t0:t1_])
                        nc.vector.tensor_tensor(out, tiles(b, m)[:, ::-1, 1, ::-1], out, ALU.add).then_inc(s["y_in"], 1)
                    dve.wait_ge(s["means"], at(i, 1, 1))
                    nc.vector.scalar_tensor_tensor(os_[:, S_LAT], bank[0][:, :], -1.0 / C, os_[:, S_LAT], ALU.mult, ALU.add)
                    nc.vector.scalar_tensor_tensor(os_[:, S_CTX], bank[1][:, 0:CTX], -1.0 / C, os_[:, S_CTX],
                                                   ALU.mult, ALU.add).then_inc(s["y_centred"], 1)
                    dve.wait_ge(s["y_centred"], at(i, 1, 1))
                    nc.vector.scalar_tensor_tensor(sq[:, :], os_[:, :], 1.0 / C, os_[:, :], ALU.mult,
                                                   ALU.mult).then_inc(s["y_squares"], 1)
                    dve.wait_ge(s["y_root"], at(i, 1, 1))
                    link(nc.vector.reciprocal(rn[:, :], rn[:, :]))
                    link(nc.vector.tensor_tensor(os_[:, :], os_[:, :], rn[:, :], ALU.mult))
                    link(nc.vector.tensor_scalar(os_[:, :], os_[:, :], hcol(W_GG), hcol(W_GB), ALU.mult, ALU.add))
                    link(nc.vector.tensor_tensor(os_[:, :], os_[:, :], bon[:, :], ALU.add))
                    nc.vector.tensor_tensor(os_[:, :], os_[:, :], gate[:, :], ALU.mult).then_inc(s["y_ready"], 1)
                    link.end()


LINKS_RW = 13 + 2 * NGROUP + 1



KEYS = P + T
KT_LAT, KT_CTX = slice(0, P + LAT), slice(P + LAT, KEYS)
QTILES = T // P
KTILES = KEYS // P
GROUPS = AT_HEADS // AT_KV
A_GAIN, A_COLS = 0, 2
TILES = GROUPS * QTILES


def normed_rotated(nc, g):
    NQK = 10
    names = ["passed", "const", "loaded", "squares", "sums", "root", "inverse", "normed", "swapped", "link", "done", "stored"]
    with buffers(nc) as (sb, banks), phase(nc, *names) as s:
        qb, sq, rn, out = (sb(n, T) for n in ("qk", "sq", "rn", "out"))
        gain = sb("gain", 1)
        tab, perm = sb("rope", 2, T), sb("perm", P)
        ss_l, ss_c, sw_l, sw_c = banks(4)
        with nc.Block() as block:

            @block.sync
            def _(sp):
                sp.dma_start(tab[:, :, :], g.d["rope_t"]).then_inc(s["const"], 16)
                sp.dma_start(perm[:, :], g.d["rope_perm"]).then_inc(s["const"], 16)
                sp.sem_inc(s["stored"], 16)
                with sp.Fori(0, NQK) as i:
                    wait_alone(sp, s["stored"], at(i, 16, 16), s["passed"])
                    sp.dma_start(qb[:, :], slab(g.d["qkv"], i)).then_inc(s["loaded"], 16)
                    sp.dma_start(gain[:, :], slab(g.d["at_gain"], i)).then_inc(s["loaded"], 16)
                    sp.wait_ge(s["done"], at(i, 1, 1))
                    sp.dma_start(slab(g.d["qk_rot"], i), out[:, :]).then_inc(s["stored"], 16)
                sp.wait_ge(s["stored"], 16 * (NQK + 1))
                for b in range(2):
                    sp.dma_start(g.d["kv_out"][b], g.d["qk_rot"][8 + b, :, S_CTX]).then_inc(s["stored"], 16)
                    sp.dma_start(g.d["kv_out"][2 + b], g.d["qkv"][10 + b, :, S_CTX]).then_inc(s["stored"], 16)
                sp.wait_ge(s["stored"], 16 * (NQK + 5))

            @block.scalar
            def _(act):
                with act.Fori(0, NQK) as i:
                    act.wait_ge(s["loaded"], at(i, 32, 32))
                    nc.scalar.activation(sq[:, :], qb[:, :], ACT.Square).then_inc(s["squares"], 1)
                    act.wait_ge(s["sums"], at(i, 1, 1))
                    nc.scalar.activation(rn[:, S_LAT], ss_l[:, :], ACT.Sqrt, bias=g.eps_nrm, scale=1.0 / HD)
                    nc.scalar.activation(rn[:, S_CTX], ss_c[:, 0:CTX], ACT.Sqrt, bias=g.eps_nrm,
                                         scale=1.0 / HD).then_inc(s["root"], 1)

            @block.tensor
            def _(pe):
                pe.wait_ge(s["const"], 32)
                with pe.Fori(0, NQK) as i:
                    pe.wait_ge(s["squares"], at(i, 1, 1))
                    nc.tensor.matmul(ss_l[:, :], g.mask(K_BO), sq[:, S_LAT], start=True, stop=True)
                    nc.tensor.matmul(ss_c[:, 0:CTX], g.mask(K_BO), sq[:, S_CTX], start=True, stop=True).then_inc(s["sums"], 1)
                    pe.wait_ge(s["normed"], at(i, 1, 1))
                    nc.tensor.matmul(sw_l[:, :], perm[:, :], qb[:, S_LAT], start=True, stop=True)
                    nc.tensor.matmul(sw_c[:, 0:CTX], perm[:, :], qb[:, S_CTX], start=True, stop=True).then_inc(s["swapped"], 1)

            @block.vector
            def _(dve):
                dve.wait_ge(s["const"], 32)
                with dve.Fori(0, NQK) as i:
                    link = Link(dve, s["link"], i, 3)
                    dve.wait_ge(s["root"], at(i, 1, 1))
                    link(nc.vector.reciprocal(rn[:, :], rn[:, :]))
                    nc.vector.scalar_tensor_tensor(qb[:, :], qb[:, :], gain[:, 0:1], rn[:, :], ALU.mult,
                                                   ALU.mult).then_inc(s["normed"], 1)
                    dve.wait_ge(s["normed"], at(i, 1, 1))
                    link(nc.vector.tensor_tensor(out[:, :], qb[:, :], tab[:, 0, :], ALU.mult))
                    dve.wait_ge(s["swapped"], at(i, 1, 1))
                    nc.vector.tensor_tensor(rn[:, S_LAT], sw_l[:, :], tab[:, 1, S_LAT], ALU.mult)
                    link(nc.vector.tensor_tensor(rn[:, S_CTX], sw_c[:, 0:CTX], tab[:, 1, S_CTX], ALU.mult))
                    nc.vector.tensor_tensor(out[:, :], out[:, :], rn[:, :], ALU.add).then_inc(s["done"], 1)
                    link.end()


def attention_heads(nc, g):
    normed_rotated(nc, g)
    SCALE = HD ** -0.5
    names = ["passed", "loaded", "v_ps", "v_out", "scores", "link", "negmax", "exps", "normed", "pt_ps", "pt_out", "o_ps",
             "o_out", "stored"]
    with buffers(nc) as (sb, banks), phase(nc, *names) as s:
        kt, vt, vtok = sb("kt", KEYS), sb("vt", T), sb("vtok", KTILES, HD)
        q4, o4 = sb("q4", GROUPS, T), sb("o4", GROUPS, T)
        pb, pt = sb("probs", 2, P + LAT), sb("probs_t", 2, QTILES, P)
        mx, rsum = sb("mx", TILES), sb("rsum", TILES)
        with ExitStack() as stack:
            sc = [stack.enter_context(nc.psum_tensor(unique("scores"), [P, 2, 512], F32)) for _ in range(2)]
            tp = stack.enter_context(nc.psum_tensor(unique("probs_t"), [P, 2, 512], F32))
            ob, vb = (stack.enter_context(nc.psum_tensor(unique(n), [P, 512], F32)) for n in ("ob", "vb"))
            tiles = [(h, q) for h in range(GROUPS) for q in range(QTILES)]
            flat = lambda t: t[:, :, :].rearrange("p a b -> p (a b)")

            def keys_of(q):
                return (KT_LAT, range(0, KTILES - 1)) if q < QTILES - 1 else (KT_CTX, range(KTILES - 1, KTILES))

            with nc.Block() as block:

                @block.sync
                def _(sp):
                    sp.sem_inc(s["stored"], 16)
                    with sp.Fori(0, AT_KV) as i:
                        wait_alone(sp, s["stored"], at(i, 16, 16), s["passed"])
                        sp.dma_start(kt[0:HD, 0:P], slab(g.d["cache_kt"], i)).then_inc(s["loaded"], 16)
                        sp.dma_start(kt[0:HD, P:KEYS], slab(g.d["qk_rot_heads"], i + AT_HEADS)).then_inc(s["loaded"], 16)
                        sp.dma_start(vt[0:HD, :], slab(g.d["qkv_heads"], i + (AT_HEADS + AT_KV))).then_inc(s["loaded"], 16)
                        sp.dma_start(vtok[:, 0, :], slab(g.d["cache_v_tok"], i)).then_inc(s["loaded"], 16)
                        sp.dma_start(q4[0:HD, :, :], g.d["qk_rot_heads"][bass.ds(i * GROUPS, GROUPS)]
                                     .rearrange("h c t -> c h t")).then_inc(s["loaded"], 16)
                        wait_alone(sp, s["o_out"], at(i, TILES, TILES), s["passed"])
                        sp.dma_start(g.d["mixed_heads"][bass.ds(i * GROUPS, GROUPS)].rearrange("h c t -> c h t"),
                                     o4[0:HD, :, :]).then_inc(s["stored"], 16)
                    sp.wait_ge(s["stored"], 16 * (AT_KV + 1))

                @block.tensor
                def _(pe):
                    def scores(i, n):
                        h, q = tiles[n]
                        cols, _ = keys_of(q)
                        if n >= 2:
                            pe.wait_ge(s["exps"], at(i, TILES, n - 1))
                        qs = q4[0:HD, h, q * P:(q + 1) * P]
                        out = sc[n % 2]
                        if q < QTILES - 1:
                            nc.tensor.matmul(out[:, 0, :], qs, kt[0:HD, 0:512], start=True, stop=True)
                            nc.tensor.matmul(out[:, 1, 0:P], qs, kt[0:HD, 512:P + LAT], start=True,
                                             stop=True).then_inc(s["scores"], 1)
                        else:
                            nc.tensor.matmul(out[:, 0, 0:P], qs, kt[0:HD, cols], start=True, stop=True).then_inc(s["scores"], 1)

                    with pe.Fori(0, AT_KV) as i:
                        wait_alone(pe, s["loaded"], at(i, 80, 80), s["passed"])
                        for n in range(QTILES):
                            last = nc.tensor.transpose(vb[:, n * HD:(n + 1) * HD], vt[0:HD, n * P:(n + 1) * P],
                                                       g.const[0:HD, K_ID:K_ID + HD])
                        last.then_inc(s["v_ps"], 1)
                        scores(i, 0)
                        for n, (h, q) in enumerate(tiles):
                            if n + 1 < TILES:
                                scores(i, n + 1)
                            _, kts = keys_of(q)
                            pe.wait_ge(s["normed"], at(i, TILES, n + 1))
                            if n >= 1:
                                pe.wait_ge(s["pt_out"], at(i, TILES, n))
                            for m in range(len(kts)):
                                last = nc.tensor.transpose(flat(tp)[:, m * P:(m + 1) * P], pb[:, n % 2, m * P:(m + 1) * P],
                                                           g.ident)
                            last.then_inc(s["pt_ps"], 1)
                            pe.wait_ge(s["pt_out"], at(i, TILES, n + 1))
                            if n == 0:
                                pe.wait_ge(s["v_out"], at(i, 1, 1))
                            else:
                                pe.wait_ge(s["o_out"], at(i, TILES, n))
                            for m, key in enumerate(kts):
                                last = nc.tensor.matmul(ob[0:HD, 0:P], vtok[:, key, :], pt[:, n % 2, m, :],
                                                        start=(m == 0), stop=(m == len(kts) - 1))
                            last.then_inc(s["o_ps"], 1)

                @block.scalar
                def _(act):
                    with act.Fori(0, AT_KV) as i:
                        act.wait_ge(s["v_ps"], at(i, 1, 1))
                        nc.scalar.copy(vtok[:, 1:KTILES, :].rearrange("p k c -> p (k c)"),
                                       vb[:, 0:QTILES * HD]).then_inc(s["v_out"], 1)

                        def transposed_out(n):
                            width = P * len(keys_of(tiles[n][1])[1])
                            act.wait_ge(s["pt_ps"], at(i, TILES, n + 1))
                            if n >= 2:
                                act.wait_ge(s["o_ps"], at(i, TILES, n - 1))
                            nc.scalar.copy(pt[:, n % 2, :, :].rearrange("p a b -> p (a b)")[:, 0:width],
                                           flat(tp)[:, 0:width]).then_inc(s["pt_out"], 1)

                        for n, (h, q) in enumerate(tiles):
                            width = P * len(keys_of(q)[1])
                            act.wait_ge(s["negmax"], at(i, TILES, n + 1))
                            if n >= 2:
                                act.wait_ge(s["pt_ps"], at(i, TILES, n - 1))
                            nc.scalar.activation(pb[:, n % 2, 0:width], flat(sc[n % 2])[:, 0:width], ACT.Exp, scale=SCALE,
                                                 bias=mx[:, n:n + 1], accum_out=rsum[:, n:n + 1]).then_inc(s["exps"], 1)
                            if n >= 1:
                                transposed_out(n - 1)
                        transposed_out(TILES - 1)

                @block.vector
                def _(dve):
                    with dve.Fori(0, AT_KV) as i:
                        link = Link(dve, s["link"], i, 2 * TILES)

                        def maximum(n):
                            width = P * len(keys_of(tiles[n][1])[1])
                            dve.wait_ge(s["scores"], at(i, TILES, n + 1))
                            link(nc.vector.reduce_max(mx[:, n:n + 1], flat(sc[n % 2])[:, 0:width], AX.X))
                            nc.vector.tensor_scalar(mx[:, n:n + 1], mx[:, n:n + 1], -SCALE, None, ALU.mult).then_inc(s["negmax"], 1)

                        maximum(0)
                        for n, (h, q) in enumerate(tiles):
                            if n + 1 < TILES:
                                maximum(n + 1)
                            width = P * len(keys_of(q)[1])
                            dve.wait_ge(s["exps"], at(i, TILES, n + 1))
                            link(nc.vector.reciprocal(rsum[:, n:n + 1], rsum[:, n:n + 1]))
                            nc.vector.tensor_scalar(pb[:, n % 2, 0:width], pb[:, n % 2, 0:width], rsum[:, n:n + 1], None,
                                                    ALU.mult).then_inc(s["normed"], 1)
                            if n >= 1:
                                hp, qp = tiles[n - 1]
                                dve.wait_ge(s["o_ps"], at(i, TILES, n))
                                nc.vector.tensor_copy(o4[0:HD, hp, qp * P:(qp + 1) * P], ob[0:HD, 0:P]).then_inc(s["o_out"], 1)
                        dve.wait_ge(s["o_ps"], at(i, TILES, TILES))
                        nc.vector.tensor_copy(o4[0:HD, GROUPS - 1, T - P:T], ob[0:HD, 0:P]).then_inc(s["o_out"], 1)
                        link.end()



R_G, R_EG, R_B, R_EL = 0, TT, 2 * TT, 3 * TT
R_END = 3 * TT + 2 * NCHUNK
C_G, C_NBEG, C_B, C_ED = 0, NCHUNK, 2 * NCHUNK, 3 * NCHUNK
C_END = 4 * NCHUNK
N_COLS = 10


def delta_gates(nc, g):
    names = ["passed", "w_loaded", "mm_done", "out", "raw_stored", "raw_loaded", "link", "exps", "rate", "sums", "decays", "scaled",
             "cols_ps", "cols_out", "stored"]
    H8 = slice(0, DN_HEADS)
    with buffers(nc) as (sb, banks), phase(nc, *names) as s:
        wg, raw, small = sb("wg", NB, 4 * DN_HEADS), sb("raw", T), sb("small", 4)
        ab = sb("ab", 2, 2, T)
        tmp = sb("tmp", 2, T)
        rows = sb("rows", R_END)
        nb, ed = sb("neg_beta_decay", TT), sb("to_end", TT)
        cols = sb("cols", DN_HEADS, C_END)
        rate = sb("rate", 2)
        bank = banks(4)
        pairs = lambda r0: rows[H8, r0:r0 + TT].rearrange("p (u e c) -> p u e c", u=NCHUNK, e=2)
        with nc.Block() as block:

            @block.sync
            def _(sp):
                sp.dma_start(wg[:, :, :].rearrange("p k n -> p (k n)"), g.d["dn_wgate"]).then_inc(s["w_loaded"], 16)
                sp.dma_start(small[H8, :], g.d["dn_small"]).then_inc(s["w_loaded"], 16)
                sp.wait_ge(s["out"], 1)
                sp.dma_start(g.d["dn_gates"].rearrange("a e h t -> (a e h) t"), raw[0:4 * DN_HEADS, :]).then_inc(s["raw_stored"], 16)
                sp.wait_ge(s["raw_stored"], 16)
                for a in range(2):
                    sp.dma_start(ab[H8, a, :, :], g.d["dn_gates"][a].rearrange("e h t -> h e t")).then_inc(s["raw_loaded"], 16)
                sp.wait_ge(s["cols_out"], 8)
                for h in range(DN_HEADS):
                    sp.dma_start(g.d["dn_cols"][h], cols[:, h, :]).then_inc(s["stored"], 16)
                sp.dma_start(g.d["dn_rows"], rows[H8, :]).then_inc(s["stored"], 16)
                sp.wait_ge(s["stored"], 16 * (DN_HEADS + 1))

            @block.tensor
            def _(pe):
                pe.wait_ge(s["w_loaded"], 32)
                for k in range(NB):
                    nc.tensor.matmul(bank[0][0:4 * DN_HEADS, :], wg[:, k, :], g.h[:, k, H_LAT], start=(k == 0), stop=(k == NB - 1))
                    last = nc.tensor.matmul(bank[1][0:4 * DN_HEADS, 0:CTX], wg[:, k, :], g.h[:, k, H_CTX],
                                            start=(k == 0), stop=(k == NB - 1))
                last.then_inc(s["mm_done"], 1)
                pe.wait_ge(s["scaled"], 4)
                for n, src in enumerate((rows[H8, R_G:R_G + TT], nb[H8, :], rows[H8, R_B:R_B + TT], ed[H8, :])):
                    if n >= 1:
                        pe.wait_ge(s["cols_out"], 2 * n)
                    for u in range(NCHUNK):
                        last = nc.tensor.transpose(bank[2 + n % 2][:, u * DN_HEADS:(u + 1) * DN_HEADS], src[:, u * P:(u + 1) * P],
                                                   g.ident[H8, H8])
                    last.then_inc(s["cols_ps"], 1)

            @block.scalar
            def _(act):
                act.wait_ge(s["mm_done"], 1)
                nc.scalar.copy(raw[0:4 * DN_HEADS, S_LAT], bank[0][0:4 * DN_HEADS, :])
                nc.scalar.copy(raw[0:4 * DN_HEADS, S_CTX], bank[1][0:4 * DN_HEADS, 0:CTX]).then_inc(s["out"], 1)
                act.wait_ge(s["rate"], 1)
                nc.scalar.activation(tmp[H8, :, :], tmp[H8, :, :], ACT.Exp, scale=-1.0).then_inc(s["exps"], 1)
                nc.scalar.activation(rate[H8, :], small[H8, 0:2], ACT.Exp).then_inc(s["exps"], 1)
                act.wait_ge(s["exps"], 1)
                nc.scalar.activation(tmp[H8, :, :], tmp[H8, :, :], ACT.Ln, bias=g.const[H8, K_ONE:K_ONE + 1]).then_inc(s["exps"], 1)
                nc.scalar.activation(ab[H8, 1, :, :], ab[H8, 1, :, :], ACT.Sigmoid).then_inc(s["exps"], 1)
                act.wait_ge(s["sums"], 1)
                nc.scalar.activation(rows[H8, R_EG:R_EG + TT], rows[H8, R_G:R_G + TT], ACT.Exp).then_inc(s["decays"], 1)
                nc.scalar.activation(rows[H8, R_EL:R_END].rearrange("p (u e) -> p u e", e=2), pairs(R_G)[:, :, :, C - 1],
                                     ACT.Exp).then_inc(s["decays"], 1)
                act.wait_ge(s["sums"], 2)
                nc.scalar.activation(ed[H8, :], ed[H8, :], ACT.Exp).then_inc(s["scaled"], 1)
                for n in range(4):
                    act.wait_ge(s["cols_ps"], n + 1)
                    nc.scalar.copy(cols[:, :, n * NCHUNK:(n + 1) * NCHUNK].rearrange("p h u -> p u h"),
                                   bank[2 + n % 2][:, 0:NCHUNK * DN_HEADS].rearrange("p (u h) -> p u h", h=DN_HEADS)).then_inc(s["cols_out"], 2)

            @block.vector
            def _(dve):
                link = Link(dve, s["link"])
                dve.wait_ge(s["raw_loaded"], 32)
                dve.wait_ge(s["w_loaded"], 32)
                for e in range(2):
                    last = nc.vector.tensor_scalar(ab[H8, 0, e, :], ab[H8, 0, e, :], small[H8, 2 + e:3 + e], None, ALU.add)
                link(last)
                link(nc.vector.tensor_scalar(tmp[H8, :, :], ab[H8, 0, :, :], -1.0, None, ALU.mult))
                nc.vector.tensor_tensor(tmp[H8, :, :], tmp[H8, :, :], ab[H8, 0, :, :], ALU.max).then_inc(s["rate"], 1)
                dve.wait_ge(s["exps"], 4)
                link(nc.vector.scalar_tensor_tensor(ab[H8, 0, :, :], ab[H8, 0, :, :], 0.0, tmp[H8, :, :], ALU.max, ALU.add))
                for e in range(2):
                    last = nc.vector.tensor_scalar(ab[H8, 0, e, :], ab[H8, 0, e, :], rate[H8, e:e + 1], -1.0, ALU.mult, ALU.mult)
                link(last)
                flat_nb = nb[H8, :].rearrange("p (u e c) -> p u e c", u=NCHUNK, e=2)
                for a, out in ((0, flat_nb), (1, pairs(R_B))):
                    for us, ts in ((slice(0, NLAT), S_LAT), (slice(NLAT, NCHUNK), S_CTX)):
                        nc.vector.tensor_copy(out[:, us, 0, :], chunked(ab[H8, a, 0, ts]))
                        last = nc.vector.tensor_copy(out[:, us, 1, :], chunked(ab[H8, a, 1, ts][:, ::-1]))
                link(last)
                nc.vector.tensor_tensor_scan(rows[H8, R_G:R_G + TT], g.const[H8, K_SCAN:K_SCAN + TT], nb[H8, :], 0.0,
                                             ALU.mult, ALU.add).then_inc(s["sums"], 1)
                dve.wait_ge(s["sums"], 1)
                nc.vector.tensor_tensor(ed[H8, :].rearrange("p (n c) -> p n c", c=C),
                                        rows[H8, R_G:R_G + TT].rearrange("p (n c) -> p n c", c=C)[:, :, C - 1:C]
                                        .to_broadcast([DN_HEADS, 2 * NCHUNK, C]),
                                        rows[H8, R_G:R_G + TT].rearrange("p (n c) -> p n c", c=C), ALU.subtract).then_inc(s["sums"], 1)
                dve.wait_ge(s["decays"], 2)
                nc.vector.scalar_tensor_tensor(nb[H8, :], rows[H8, R_EG:R_EG + TT], -1.0, rows[H8, R_B:R_B + TT],
                                               ALU.mult, ALU.mult).then_inc(s["scaled"], 3)


def delta_heads(nc, g):
    D_SCALE = P ** -0.5
    names = ["passed", "in_loaded", "in_free", "link", "conv", "conv_sig", "link_a", "first", "squares", "sums", "root", "operands", "differ", "decay",
             "prepared", "masks", "products", "masked", "tokens", "tokens_out", "state_in", "chain_y", "tmp_out", "chain_v", "v_out",
             "chain_s", "s_out", "o_ps", "o_out", "state_stored", "y_squares", "y_sums", "y_root", "z_sig", "y_ready",
             "y_stored"] + INVERSE_SEMS
    with buffers(nc) as (sb, banks), phase(nc, *names) as s:
        w = Work()
        xin, cv, cs, z = sb("xin", 3, HW), sb("cv", 3, HW), sb("cs", 3, T), sb("z", 2, T)
        rows, el, hcols, fcols = sb("rows", 3 * TT), sb("el", 2, 2 * NCHUNK), sb("hcols", 2, C_END), sb("fcols", 2, N_COLS)
        k2, q2, qd, ve = (sb(n, 2, NCHUNK, P) for n in ("k2", "q2", "qd", "ve"))
        dm, di = sb("dm", 2, NCHUNK, P), sb("di", 2, NCHUNK, P)
        w.lt, w.xx, w.y = sb("lt", GROUP, P), sb("xx", 2, 2, 2, P), sb("y", 2, 2, P)
        w.tt, qk = sb("tt", 2 * NCHUNK, P), sb("qk", 2 * NCHUNK, P)
        sq, rn = sb("sq", T), sb("rn", T)
        tmp, vn, st = sb("tmp", 2, P), sb("vn", 2, P), sb("state", 2, 2, P)
        spare = g.h[:, :, :].rearrange("p b t -> p (b t)")
        kdec = spare[:, 0:2 * TT].rearrange("p (n c) -> p n c", c=P)
        vtok = spare[:, 2 * TT:4 * TT].rearrange("p (n c) -> p n c", c=P)
        os_ = ve
        bank = banks(8)
        w.y_bank, w.x_bank = bank[2:4], bank[6:8]
        split = lambda buf, hh: buf[:, hh, :, :].rearrange("p u (e c) -> p u e c", e=2)
        row = lambda r0: rows[:, r0:r0 + TT].rearrange("p (u n) -> p u n", n=P)
        NI = DN_HEADS // 2
        LOADS = 10
        with nc.Block() as block:

            @block.sync
            def _(sp):
                sp.sem_inc(s["y_stored"], 32)
                with sp.Fori(0, NI) as i:
                    wait_alone(sp, s["y_stored"], at(i, 32, 32), s["passed"])
                    sp.dma_start(fcols[:, :, :].rearrange("p h n -> p (h n)"), slab(g.d["dn_head"], i)).then_inc(s["state_in"], 16)
                    for hh in range(2):
                        if hh:
                            wait_alone(sp, s["prepared"], at(i, 2, 1), s["passed"])
                            wait_alone(sp, s["masks"], at(i, 4, 2), s["passed"])
                        for n in range(3):
                            blk = i * 2 + (n * NB + hh)
                            sp.dma_start(xin[:, n, H_LAT], slab(g.d["dn_lat"], blk)).then_inc(s["in_loaded"], 16)
                            sp.dma_start(xin[:, n, H_CTX], slab(g.d["dn_ctx"], blk)).then_inc(s["in_loaded"], 16)
                        sp.dma_start(z[:, hh, :], slab(g.d["dn_proj"], i * 2 + (3 * NB + hh))).then_inc(s["in_loaded"], 16)
                        sp.dma_start(rows[:, :], g.d["dn_rows"][bass.ds(i * 2 + hh, 1), 0:3 * TT].to_broadcast([P, 3 * TT])
                                     ).then_inc(s["in_loaded"], 16)
                        sp.dma_start(el[:, hh, :], g.d["dn_rows"][bass.ds(i * 2 + hh, 1), R_EL:R_END].to_broadcast([P, 2 * NCHUNK])
                                     ).then_inc(s["in_loaded"], 16)
                        sp.dma_start(hcols[:, hh, :], slab(g.d["dn_cols"], i * 2 + hh)).then_inc(s["in_loaded"], 16)
                    wait_alone(sp, s["s_out"], at(i, STEPS + 2, 3), s["passed"])
                    sp.dma_start(slab(g.d["dn_state_out"], i), st[:, :, :, :].rearrange("p h e v -> p (h e v)")
                                 ).then_inc(s["state_stored"], 16)
                    wait_alone(sp, s["state_stored"], at(i, 32, 16), s["passed"])
                    sp.dma_start(st[:, :, :, :].rearrange("p h e v -> p (h e v)"), slab(g.d["dn_state"], i)
                                 ).then_inc(s["state_stored"], 16)
                    for hh in range(2):
                        wait_alone(sp, s["y_ready"], at(i, 2, hh + 1), s["passed"])
                        sp.dma_start(slab(g.d["mixed"], i * 2 + hh), cs[:, hh, :]).then_inc(s["y_stored"], 16)
                sp.wait_ge(s["y_stored"], 32 * (NI + 1))

            @block.gpsimd
            def _(pool):
                with pool.Fori(0, NI) as i:
                    for hh in range(2):
                        wait_alone(pool, s["decay"], at(i, 2, hh + 1), s["passed"])
                        nc.gpsimd.tensor_tensor(dm[:, hh], dm[:, hh], row(R_B), ALU.mult).then_inc(s["masks"], 1)
                        nc.gpsimd.tensor_tensor(di[:, hh], di[:, hh], g.mask(K_IP).unsqueeze(1).to_broadcast([P, NCHUNK, P]),
                                                ALU.mult).then_inc(s["masks"], 1)

            @block.tensor
            def _(pe):
                with pe.Fori(0, NI) as i:
                    for hh in range(2):
                        for n in range(2):
                            pe.wait_ge(s["squares"], at(i, 4, 2 * hh + n + 1))
                            nc.tensor.matmul(bank[0][:, :], g.mask(K_ONE), sq[:, S_LAT], start=True, stop=True)
                            nc.tensor.matmul(bank[1][:, 0:CTX], g.mask(K_ONE), sq[:, S_CTX], start=True, stop=True).then_inc(s["sums"], 1)
                    pe.wait_ge(s["operands"], at(i, 2, 2))
                    for jg in range(NGROUP):
                        if jg >= 1:
                            pe.wait_ge(s["tokens_out"], at(i, NGROUP, jg))
                        units = [(2 * jg + n % 2, n // 2) for n in range(GROUP)]
                        for b, (left, right) in enumerate(((k2, k2), (k2, q2))):
                            for n, (u, hh) in enumerate(units):
                                last = nc.tensor.matmul(bank[b][:, n * P:(n + 1) * P], left[:, hh, u, :], right[:, hh, u, :],
                                                        start=True, stop=True)
                            last.then_inc(s["products"], 1)
                        for b, src in ((4, k2), (5, ve)):
                            for n, (u, hh) in enumerate(units):
                                last = nc.tensor.transpose(bank[b][:, n * P:(n + 1) * P], src[:, hh, u, :], g.ident)
                            last.then_inc(s["tokens"], 1)
                        pe.wait_ge(s["masked"], at(i, 4 * NGROUP, 4 * jg + 4))
                        if jg >= 1:
                            pe.wait_ge(s["inv_ready"], group_at(i, jg - 1, "inv_ready", 2))
                        invert_pe(pe, nc, g, s, w, i, jg)
                    pe.wait_ge(s["inv_ready"], group_at(i, NGROUP - 1, "inv_ready", 2))
                    pe.wait_ge(s["tokens_out"], at(i, NGROUP, NGROUP))
                    for n in range(STEPS):
                        u = ORDER[n]
                        if n == 2:
                            pe.wait_ge(s["state_stored"], at(i, 32, 32))
                        pe.wait_ge(s["s_out"], at(i, STEPS + 2, n + 1))
                        for hh in range(2):
                            last = nc.tensor.matmul(bank[0][:, hh * 2 * P:(hh + 1) * 2 * P], k2[:, hh, u, :],
                                                    st[:, hh, :, :].rearrange("p e v -> p (e v)"), start=True, stop=True)
                        last.then_inc(s["chain_y"], 1)
                        if n >= 2:
                            pe.wait_ge(s["o_out"], at(i, STEPS, n - 1))
                        ob = bank[4 + n % 2]
                        for hh in range(2):
                            for e in range(2):
                                nc.tensor.matmul(ob[:, hh * P + e * C:hh * P + (e + 1) * C], st[:, hh, e, :],
                                                 qd[:, hh, u, e * C:(e + 1) * C], start=(hh == 0 and e == 0), stop=False,
                                                 skip_group_check=True)
                        pe.wait_ge(s["tmp_out"], at(i, STEPS, n + 1))
                        for hh in range(2):
                            last = nc.tensor.matmul(bank[1][:, hh * P:(hh + 1) * P], w.tt[:, unit(u, hh), :], tmp[:, hh, :],
                                                    start=True, stop=True)
                        last.then_inc(s["chain_v"], 1)
                        pe.wait_ge(s["v_out"], at(i, STEPS, n + 1))
                        for e in range(2):
                            er = slice(C * e, C * (e + 1))
                            for hh in range(2):
                                last = nc.tensor.matmul(bank[2 + e][:, hh * P:(hh + 1) * P], kdec[er, unit(u, hh), :], vn[er, hh, :],
                                                        start=True, stop=True)
                            last.then_inc(s["chain_s"], 1)
                        for hh in range(2):
                            last = nc.tensor.matmul(ob[:, hh * P:(hh + 1) * P], vn[:, hh, :], qk[:, unit(u, hh), :], start=False,
                                                    stop=True, skip_group_check=True)
                        last.then_inc(s["o_ps"], 1)
                    for hh in range(2):
                        pe.wait_ge(s["y_squares"], at(i, 2, hh + 1))
                        nc.tensor.matmul(bank[6][:, :], g.mask(K_ONE), sq[:, S_LAT], start=True, stop=True)
                        nc.tensor.matmul(bank[7][:, 0:CTX], g.mask(K_ONE), sq[:, S_CTX], start=True, stop=True).then_inc(s["y_sums"], 1)

            @block.scalar
            def _(act):
                def root(i, done, lat, ctx, scale):
                    nc.scalar.activation(rn[:, S_LAT], lat[:, :], ACT.Sqrt, bias=g.eps_nrm, scale=scale)
                    nc.scalar.activation(rn[:, S_CTX], ctx[:, 0:CTX], ACT.Sqrt, bias=g.eps_nrm, scale=scale).then_inc(done, 1)

                with act.Fori(0, NI) as i:
                    for hh in range(2):
                        act.wait_ge(s["conv"], at(i, 2, hh + 1))
                        nc.scalar.activation(xin[:, :, 1:HW - 1], cv[:, :, 1:HW - 1], ACT.Sigmoid).then_inc(s["conv_sig"], 1)
                        for n in range(2):
                            act.wait_ge(s["sums"], at(i, 4, 2 * hh + n + 1))
                            root(i, s["root"], bank[0], bank[1], 1.0)
                        act.wait_ge(s["differ"], at(i, 2, hh + 1))
                        nc.scalar.activation(di[:, hh], di[:, hh], ACT.Exp).then_inc(s["link_a"], 1)
                        act.wait_ge(s["link_a"], at(i, 2, hh + 1))
                        nc.scalar.copy(dm[:, hh], di[:, hh]).then_inc(s["decay"], 1)
                    for jg in range(NGROUP):
                        act.wait_ge(s["tokens"], at(i, 2 * NGROUP, 2 * jg + 2))
                        for n in range(GROUP):
                            u, hh = 2 * jg + n % 2, n // 2
                            nc.scalar.activation(kdec[:, GROUP * jg + n, :], bank[4][:, n * P:(n + 1) * P], ACT.Identity,
                                                 scale=hcols[:, hh, C_ED + u:C_ED + u + 1])
                            last = nc.scalar.activation(vtok[:, GROUP * jg + n, :], bank[5][:, n * P:(n + 1) * P], ACT.Identity,
                                                        scale=hcols[:, hh, C_B + u:C_B + u + 1])
                        last.then_inc(s["tokens_out"], 1)
                    for n in range(STEPS):
                        act.wait_ge(s["o_ps"], at(i, STEPS, n + 1))
                        nc.scalar.copy(os_[:, :, ORDER[n], :], bank[4 + n % 2][:, 0:2 * P].rearrange("p (h n) -> p h n", h=2)
                                       ).then_inc(s["o_out"], 1)
                    nc.scalar.activation(cv[:, 0:2, 0:T], z[:, :, :], ACT.Sigmoid).then_inc(s["z_sig"], 1)
                    for hh in range(2):
                        act.wait_ge(s["y_sums"], at(i, 2, hh + 1))
                        root(i, s["y_root"], bank[6], bank[7], 1.0 / P)

            @block.vector
            def _(dve):
                link0 = Link(dve, s["first"])
                for edge in (slice(0, 1), slice(H_LAT.stop, H_CTX.start), slice(H_CTX.stop, HW)):
                    link0(nc.vector.memset(xin[:, :, edge], 0.0))
                with dve.Fori(0, NI) as i:
                    link = Link(dve, s["link"], i, LINKS_DN)
                    dve.wait_ge(s["state_in"], at(i, 16, 16))
                    for hh in range(2):
                        dve.wait_ge(s["in_loaded"], at(i, 32 * LOADS, 16 * LOADS * (hh + 1)))
                        for tap in range(3):
                            for n in range(3):
                                f = fcols[:, hh, 3 * n + tap:3 * n + tap + 1]
                                src, out = xin[:, n, tap:tap + HW - 2], cv[:, n, 1:HW - 1]
                                last = (nc.vector.tensor_scalar(out, src, f, None, ALU.mult) if tap == 0 else
                                        nc.vector.scalar_tensor_tensor(out, src, f, out, ALU.mult, ALU.add))
                            if tap < 2:
                                link(last)
                        last.then_inc(s["conv"], 1)
                        dve.wait_ge(s["conv_sig"], at(i, 2, hh + 1))
                        for hs, cols in ((H_LAT, S_LAT), (H_CTX, S_CTX)):
                            last = nc.vector.tensor_tensor(cs[:, :, cols], cv[:, :, hs], xin[:, :, hs], ALU.mult)
                        link(last)
                        for edge in (slice(0, 1), slice(H_LAT.stop, H_CTX.start), slice(H_CTX.stop, HW)):
                            last = nc.vector.memset(xin[:, :, edge], 0.0)
                        link(last)
                        link(nc.vector.tensor_tensor(di[:, hh], row(R_G), hcols[:, hh, C_G:C_G + NCHUNK].unsqueeze(2)
                                                     .to_broadcast([P, NCHUNK, P]), ALU.subtract))
                        nc.vector.tensor_scalar(di[:, hh], di[:, hh], 0.0, None, ALU.min).then_inc(s["differ"], 1)
                        for n, scale in ((0, D_SCALE), (1, 1.0)):
                            nc.vector.tensor_tensor(sq[:, :], cs[:, n, :], cs[:, n, :], ALU.mult).then_inc(s["squares"], 1)
                            dve.wait_ge(s["root"], at(i, 4, 2 * hh + n + 1))
                            link(nc.vector.reciprocal(rn[:, :], rn[:, :]))
                            link(nc.vector.scalar_tensor_tensor(cs[:, n, :], cs[:, n, :], scale, rn[:, :], ALU.mult, ALU.mult))
                        for n, buf in enumerate((q2, k2, ve)):
                            for both, plain in by_direction(split(buf, hh), cs[:, n, :]):
                                last = nc.vector.tensor_copy(both, plain)
                        link(last)
                        nc.vector.tensor_tensor(qd[:, hh], q2[:, hh], row(R_EG), ALU.mult).then_inc(s["prepared"], 1)
                        dve.wait_ge(s["prepared"], at(i, 2, hh + 1))
                        dve.wait_ge(s["masks"], at(i, 4, 2 * hh + 2))
                        nc.vector.scalar_tensor_tensor(dm[:, hh], dm[:, hh], -1.0, g.mask(K_SP).unsqueeze(1).to_broadcast([P, NCHUNK, P]),
                                                       ALU.mult, ALU.mult).then_inc(s["operands"], 1)
                    nc.vector.memset(st[:, :, :, :], 0.0).then_inc(s["s_out"], 1)
                    dve.wait_ge(s["operands"], at(i, 2, 2))
                    for jg in range(NGROUP):
                        for b, (mask, out) in enumerate(((dm, w.lt[:, :, :]), (di, qk[:, GROUP * jg:GROUP * (jg + 1), :]))):
                            dve.wait_ge(s["products"], at(i, 2 * NGROUP, 2 * jg + b + 1))
                            for hh in range(2):
                                nc.vector.tensor_tensor(out[:, 2 * hh:2 * hh + 2, :],
                                                        bank[b][:, 2 * hh * P:2 * (hh + 1) * P].rearrange("p (n c) -> p n c", n=2),
                                                        mask[:, hh, 2 * jg:2 * jg + 2, :], ALU.mult).then_inc(s["masked"], 1)
                        dve.wait_ge(s["masked"], at(i, 4 * NGROUP, 4 * jg + 4))
                        invert_dve(dve, nc, g, s, w, i, jg, link)
                    dve.wait_ge(s["tokens_out"], at(i, NGROUP, NGROUP))
                    for n in range(STEPS):
                        u = ORDER[n]
                        dve.wait_ge(s["chain_y"], at(i, STEPS, n + 1))
                        for hh in range(2):
                            for e in range(2):
                                er = slice(C * e, C * (e + 1))
                                last = nc.vector.scalar_tensor_tensor(
                                    tmp[er, hh, :], bank[0][er, (2 * hh + e) * P:(2 * hh + e + 1) * P],
                                    hcols[er, hh, C_NBEG + u:C_NBEG + u + 1], vtok[er, unit(u, hh), :], ALU.mult, ALU.add)
                        last.then_inc(s["tmp_out"], 1)
                        dve.wait_ge(s["chain_v"], at(i, STEPS, n + 1))
                        if n >= 1:
                            dve.wait_ge(s["o_ps"], at(i, STEPS, n))
                        nc.vector.tensor_copy(vn[:, :, :].rearrange("p h v -> p (h v)"), bank[1][:, 0:2 * P]).then_inc(s["v_out"], 1)
                        if n == 2:
                            dve.wait_ge(s["state_stored"], at(i, 32, 32))
                        for e in range(2):
                            dve.wait_ge(s["chain_s"], at(i, 2 * STEPS, 2 * n + e + 1))
                            for hh in range(2):
                                last = nc.vector.scalar_tensor_tensor(
                                    st[:, hh, e, :], st[:, hh, e, :], el[:, hh, 2 * u + e:2 * u + e + 1],
                                    bank[2 + e][:, hh * P:(hh + 1) * P], ALU.mult, ALU.add)
                        last.then_inc(s["s_out"], 1)
                        dve.wait_ge(s["s_out"], at(i, STEPS + 2, n + 2))
                    dve.sem_inc(s["s_out"], 1)
                    dve.wait_ge(s["o_out"], at(i, STEPS, STEPS))
                    for hh in range(2):
                        o4 = split(os_, hh)
                        out = chunked(cs[:, hh, :])
                        for us in (slice(0, NLAT), slice(NLAT, NCHUNK)):
                            last = nc.vector.tensor_tensor(out[:, us, :], o4[:, us, 0, :], o4[:, us, 1, :][:, ::-1, ::-1], ALU.add)
                        link(last)
                        if hh:
                            dve.wait_ge(s["y_sums"], at(i, 2, 1))
                        nc.vector.tensor_tensor(sq[:, :], cs[:, hh, :], cs[:, hh, :], ALU.mult).then_inc(s["y_squares"], 1)
                        dve.wait_ge(s["y_root"], at(i, 2, hh + 1))
                        link(nc.vector.reciprocal(rn[:, :], rn[:, :]))
                        link(nc.vector.scalar_tensor_tensor(cs[:, hh, :], cs[:, hh, :], fcols[:, hh, 9:10], rn[:, :], ALU.mult, ALU.mult))
                        dve.wait_ge(s["z_sig"], at(i, 1, 1))
                        link(nc.vector.tensor_tensor(cs[:, hh, :], cs[:, hh, :], z[:, hh, :], ALU.mult))
                        nc.vector.tensor_tensor(cs[:, hh, :], cs[:, hh, :], cv[:, hh, 0:T], ALU.mult).then_inc(s["y_ready"], 1)
                    link.end()


LINKS_DN = 2 * 10 + 2 * NGROUP + 2 * 4




class Global:

    def mask(self, col):
        return self.const[:, col:col + P]


def program(nc, d, layers=DEPTH):
    g = Global()
    g.d = d
    with buffers(nc) as (sb, _):
        g.x, g.const, g.vec = sb("x", NB, T), sb("const", K_END), sb("vec", V_END)
        g.mods = sb("mods", DEPTH * 6 * NB, 2)
        g.ident, g.mean_w = g.mask(K_ID), g.mask(K_MEAN)
        g.eps_ln, g.eps_gn, g.eps_nrm = (g.const[:, K_EPS + n:K_EPS + n + 1] for n in range(3))
        g.h = sb("h", NB, HW)
        with buffers(nc) as (sb2, _):
            g.bmod, g.cond, g.silu = sb2("bmod", DEPTH * 6 * NB), sb2("cond", NB, 2), sb2("silu", NB, 2)
            start(nc, g)
            modulation(nc, g)
        first_modulate(nc, g)
        for layer in range(layers):
            kind, j = layer % 3, layer // 3
            with buffers(nc) as (sb2, _):
                if kind == 0:
                    low = sb2("low", 3, T)
                    with buffers(nc) as (sb3, _):
                        g.xx = sb3("xx", NB, HW)
                        token_shift(nc, g)
                        low_rank(nc, g, j, low)
                        for n, m in enumerate((0, 2, 3)):
                            with buffers(nc) as (sb4, _):
                                xi = sb4("xi", NB, HW)
                                cols = lambda k, xi=xi: (xi[:, k, H_LAT], xi[:, k, H_CTX])
                                projection(nc, g, d["rw_wrkv"][(3 * j + n) * 4:(3 * j + n + 1) * 4], 4, 1, cols,
                                           out=d["rkv"][n * NB:(n + 1) * NB], mix=(xi, V_MU + (j * 6 + m) * NB))
                    rwkv_heads(nc, g, j, low)
                    wo = d["rw_wo"][4 * j:4 * j + 4]
                elif kind == 1:
                    projection(nc, g, d["at_wqkv"], 6, 1, h_cols(g), out=d["qkv"])
                    attention_heads(nc, g)
                    wo = d["at_wo"]
                else:
                    projection(nc, g, d["dn_win"], 16, 1, h_cols(g), out=d["dn_proj"])
                    delta_gates(nc, g)
                    delta_heads(nc, g)
                    wo = d["dn_wo"]
            with buffers(nc) as (sb2, _):
                mixed = sb2("mixed", NB, T)
                projection(nc, g, wo, 4, 1, plain_cols(mixed), out=d["delta"], load=(mixed, d["mixed"]))
            norm(nc, g, d["delta"], layer, 0, mod_at(layer, 2), (mod_at(layer, 4), mod_at(layer, 3)))
            with buffers(nc) as (sb2, _):
                hidden = sb2("hidden", NFB, T)
                projection(nc, g, d["w_fc1"][layer * 16:layer * 16 + 16], 16, 1, h_cols(g), hidden=hidden)
                projection(nc, g, d["w_fc2"][layer * 16:layer * 16 + 16], 4, 4, plain_cols(hidden), out=d["delta"])
            nxt = (mod_at(layer + 1, 1), mod_at(layer + 1, 0)) if layer + 1 < layers else None
            norm(nc, g, d["delta"], layer, 1, mod_at(layer, 5), nxt)




def weight_slabs(w, per=2 * P):
    k, n = w.shape
    w = w.reshape(k // D, NB, P, n // per, per)
    return np.ascontiguousarray(w.transpose(3, 0, 2, 1, 4)).reshape(-1, P, NB * per)


def columns(v):
    v = v.reshape(-1, v.shape[-1] // P, P)
    return v.transpose(2, 0, 1).reshape(P, -1)


def transposed(x):
    return x.T.reshape(-1, P, x.shape[0])


def rwkv_layout(a):
    n_j = a["rw_wrkv"].shape[0]
    slabs = [weight_slabs(a["rw_wrkv"][j, n]) for j in range(n_j) for n in range(3)]
    low, head, state = [], [], []
    for j in range(n_j):
        for w in (a["rw_w1"][j], a["rw_a1"][j]):
            low.append(weight_slabs(w.transpose(1, 0, 2).reshape(D, P), P)[0])
        low.append(weight_slabs(a["rw_g1"][j], P)[0])
        mats = [m.reshape(P, D) for m in (a["rw_w2"][j], a["rw_a2"][j], a["rw_g2"][j])]
        cols = [a["rw_w0"][j, 0], a["rw_w0"][j, 1], a["rw_a0"][j, 0], a["rw_a0"][j, 1], a["rw_kk"][j],
                a["rw_ka"][j], a["rw_rk"][j].reshape(D), a["rw_gn_g"][j], a["rw_gn_b"][j]]
        for b in range(NB):
            f = slice(b * P, (b + 1) * P)
            head.append(np.concatenate([m[:, f] for m in mats] + [c[f][:, None] for c in cols], axis=1))
        st = a["state_rwkv"][0, j].transpose(1, 3, 0, 2).reshape(NB, P, 2 * C)
        state.append(st)
    return (np.concatenate(slabs), np.stack(low), np.stack(head), np.concatenate(state),
            np.concatenate([weight_slabs(a["rw_wo"][j]) for j in range(n_j)]))


def arrays_of(a):
    d = {}
    x = np.concatenate([a["x_sample"][0], a["x_prompt"][0]], axis=0)
    d["x_t"] = transposed(x)
    d["consts"] = constant_table()
    mu = [columns(a["rw_mu"][j]) for j in range(RW_LAYERS)]
    ln = np.stack([a["ln_g"], a["ln_b"]], axis=2)
    d["vectors"] = np.concatenate([columns(ln)] + mu, axis=1)
    d["b_mod_t"] = columns(a["b_mod"])
    cond = np.stack([a["c"][0], a["c_ctx"]], axis=0)
    d["cond_t"] = cond.reshape(2, NB, P).transpose(2, 1, 0)
    d["w_mod"] = np.concatenate([weight_slabs(w, 512) for w in a["w_mod"]])
    d["rw_wrkv"], d["rw_low"], d["rw_head"], d["rw_state"], d["rw_wo"] = rwkv_layout(a)
    d["w_fc1"] = np.concatenate([weight_slabs(w) for w in a["w_fc1"]])
    d["w_fc2"] = np.concatenate([weight_slabs(w) for w in a["w_fc2"]])
    attention_layout(a, d)
    delta_layout(a, d)
    return {n: np.ascontiguousarray(v) for n, v in d.items()}


def attention_layout(a, d):
    d["at_wqkv"] = weight_slabs(a["at_wqkv"][0])
    d["at_wo"] = weight_slabs(a["at_wo"][0])
    d["at_gain"] = np.stack([np.tile(a["at_qn"][0], 2)] * 8 + [np.tile(a["at_kn"][0], 2)] * 2)[:, :, None]
    d["cache_kt"] = a["cache_k"][0, 0].transpose(1, 2, 0)
    d["cache_v_tok"] = a["cache_v"][0, 0].transpose(1, 0, 2)
    d["rope_t"], d["rope_perm"] = rope_tables()


def delta_layout(a, d):
    w = a["dn_win"][0]
    gates = 4 * D
    d["dn_win"] = weight_slabs(w[:, :gates])
    d["dn_wgate"] = weight_slabs(w[:, gates:], 4 * DN_HEADS)[0]
    d["dn_wo"] = weight_slabs(a["dn_wo"][0])
    d["dn_small"] = np.concatenate([a["dn_alog"][0].T, a["dn_dtb"][0].T], axis=1)
    taps = a["dn_conv"][0].reshape(3, 3, DN_HEADS, P).transpose(2, 3, 1, 0).reshape(DN_HEADS, P, 9)
    gain = np.broadcast_to(a["dn_ng"][0][None, :, None], (DN_HEADS, P, 1))
    head = np.concatenate([taps, gain], axis=2).reshape(DN_HEADS // 2, 2, P, 10)
    d["dn_head"] = head.transpose(0, 2, 1, 3).reshape(DN_HEADS // 2, P, 20)
    st = a["state_delta"][0, 0].reshape(2, DN_HEADS // 2, 2, P, P)
    d["dn_state"] = st.transpose(1, 3, 2, 0, 4).reshape(DN_HEADS // 2, P, 4 * P)


def rope_tables():
    n_freq = HD // 4
    tok = np.arange(LAT)
    where = np.stack([tok // GRID_W, tok % GRID_W], axis=-1).astype(np.float32)
    inv = np.float32(10000.0) ** (-np.arange(n_freq, dtype=np.float32) / n_freq)
    ang = where[:, :, None] * inv
    tab = np.zeros((P, 2, T), np.float32)
    tab[:, 0, LAT:] = 1.0
    for p in range(P):
        ax, half, f = (p % HD) // (2 * n_freq), (p // n_freq) % 2, p % n_freq
        tab[p, 0, :LAT] = np.cos(ang[:, ax, f])
        tab[p, 1, :LAT] = np.sin(ang[:, ax, f]) * (1.0 if half else -1.0)
    perm = np.zeros((P, P), np.float32)
    perm[np.arange(P) ^ n_freq, np.arange(P)] = 1.0
    return tab, perm


SCRATCH = {"rkv": (3 * NB, P, T), "mixed": (NB, P, T), "delta": (NB, P, T), "qkv": (12, P, T), "qk_rot": (10, P, T),
           "dn_proj": (32, P, T), "dn_gates": (2, 2, DN_HEADS, T),
           "dn_rows": (DN_HEADS, R_END), "dn_cols": (DN_HEADS, P, C_END)}
OUTPUTS = {"y_out": (NB, P, T), "rw_state_out": (RW_LAYERS * NB, P, 2 * C), "kv_out": (4, P, CTX),
           "dn_state_out": (DN_HEADS // 2, P, 2 * 2 * P)}


def declare(nc, arrays):
    d = {}
    for name, a in arrays.items():
        d[name] = nc.dram_tensor(name, a.shape, F32, kind="ExternalInput").ap()
    for name, shape in OUTPUTS.items():
        d[name] = nc.dram_tensor(name, shape, F32, kind="ExternalOutput").ap()
    for name, shape in SCRATCH.items():
        d[name] = nc.dram_tensor(name, shape, F32).ap()
    for name in ("qk_rot", "qkv", "mixed"):
        d[name + "_heads"] = d[name].rearrange("b (h c) t -> (b h) c t", h=2)
    d["dn_lat"], d["dn_ctx"] = d["dn_proj"][:, :, S_LAT], d["dn_proj"][:, :, S_CTX]
    return d


def kernel(**inputs):
    import concourse.bacc as bacc
    from concourse.bass_utils import run_bass_kernel_spmd

    a = {n: np.asarray(v) for n, v in inputs.items()}
    arrays = arrays_of(a)
    nc = bacc.Bacc("TRN2", target_bir_lowering=False, num_devices=1)
    program(nc, declare(nc, arrays))
    r = run_bass_kernel_spmd(nc, [arrays], core_ids=[0]).results[0]
    y = r["y_out"].reshape(D, T).T
    rw = r["rw_state_out"].reshape(RW_LAYERS, RW_HEADS, C, 2, C).transpose(0, 3, 1, 4, 2)[None]
    kv = r["kv_out"].reshape(2, AT_KV, HD, CTX).transpose(0, 3, 1, 2)[:, None, None]
    dn = r["dn_state_out"].reshape(DN_HEADS // 2, P, 2, 2, P).transpose(3, 0, 2, 1, 4).reshape(2, DN_HEADS, P, P)
    out = (y[None, LAT:], y[None, :LAT], rw, kv[0], kv[1], dn[None, None])
    return tuple(np.ascontiguousarray(o) for o in out)
```

```python
from contextlib import ExitStack, contextmanager

import concourse.bass as bass
import numpy as np
from concourse import mybir

F32 = mybir.dt.float32
ACT = mybir.ActivationFunctionType
ALU = mybir.AluOpType
AX = mybir.AxisListType

P = 128
D = 1024
DEPTH = 4
NB = D // P
LAT, CTX = 512, 128
T = LAT + CTX
FF = 4 * D
NFB = FF // P
GRID_W = 64
C = 64
ALPHA = (2.0 * DEPTH) ** 0.25
LN_EPS = 1e-5
GN_EPS = 64e-5
NRM_EPS = 1e-6
HALF_DECAY = float(np.exp(-0.5))
RW_LAYERS = 2
RW_HEADS, DN_HEADS = 16, 8
AT_HEADS, AT_KV, HD = 16, 4, 64

HW = T + 4
H_LAT = slice(1, 1 + LAT)
H_CTX = slice(2 + LAT, 2 + LAT + CTX)
S_LAT = slice(0, LAT)
S_CTX = slice(LAT, T)

TT = 2 * T
NCHUNK = T // C
NLAT = LAT // C
GROUP = 4
NGROUP = NCHUNK // 2
LEVELS = 5

K_ID, K_BO, K_ONE = 0, 128, 256
K_MEAN, K_SP, K_IP, K_L0 = 384, 512, 640, 768
K_LV = 896
K_SCAN = K_LV + LEVELS * P
K_EPS = K_SCAN + TT
K_END = K_EPS + 4

V_LN = 0
V_MU = V_LN + DEPTH * 2 * 2 * NB
V_END = V_MU + RW_LAYERS * 6 * NB


def constant_table():
    t = np.zeros((P, K_END), np.float32)
    r = np.arange(P)
    same = r[:, None] // C == r[None, :] // C
    row, col = r[:, None], r[None, :]
    t[:, K_ID:K_ID + P] = np.eye(P)
    t[:, K_BO:K_BO + P] = same
    t[:, K_ONE:K_ONE + P] = 1.0
    t[:, K_MEAN:K_MEAN + P] = 1.0 / D
    t[:, K_SP:K_SP + P] = same & (col > row)
    t[:, K_IP:K_IP + P] = same & (col >= row)
    t[:, K_L0:K_L0 + P] = (row // 2 == col // 2) & (col > row)
    for n in range(LEVELS):
        b = 2 << n
        at = K_LV + n * P
        t[:, at:at + P] = (row // (2 * b) == col // (2 * b)) & (row // b > col // b)
    t[:, K_SCAN:K_SCAN + TT] = np.arange(TT) % C != 0
    t[:, K_EPS], t[:, K_EPS + 1], t[:, K_EPS + 2] = LN_EPS, GN_EPS, NRM_EPS
    return t


def at(i, per, k):
    return i * per + k


def wait_alone(eng, sem, value, passed):
    eng.wait_ge(sem, value)
    eng.sem_inc(passed, 1)


class Link:

    def __init__(self, eng, sem, i=0, per=0):
        self.eng, self.sem, self.i, self.per, self.n = eng, sem, i, per, 0

    def __call__(self, ins):
        ins.then_inc(self.sem, 1)
        self.n += 1
        self.eng.wait_ge(self.sem, at(self.i, self.per, self.n))

    def end(self):
        assert self.n == self.per, f"the body has {self.n} links"


_count = [0]


def unique(name):
    _count[0] += 1
    return f"{name}_{_count[0]}"


@contextmanager
def phase(nc, *names):
    made, all_of = {}, []
    assert len(set(names)) == len(names)
    for name in names:
        key, _, n = name.partition(":")
        sems = [nc.alloc_semaphore(unique(f"{key}_{m}")) for m in range(int(n or 1))]
        made[key] = sems if n else sems[0]
        all_of += sems
    yield made
    nc.clear_and_free_semaphores(all_of)
    nc.all_engine_barrier()


@contextmanager
def buffers(nc):
    with ExitStack() as stack:
        count = [0]

        def sb(name, *shape):
            return stack.enter_context(nc.sbuf_tensor(unique(name), [P, *shape], F32))

        def banks(n):
            return [stack.enter_context(nc.psum_tensor(unique(f"bank{b}"), [P, 512], F32)) for b in range(n)]

        yield sb, banks


def slab(dram, n):
    return dram[bass.ds(n, 1)].rearrange("a p n -> p (a n)")


def blocks(dram):
    return dram.rearrange("b p t -> p b t")


def mod_at(layer, piece):
    return (layer * 6 + piece) * NB




def start(nc, g):
    with phase(nc, "loaded", "sig") as s, nc.Block() as block:

        @block.sync
        def _(sp):
            sp.dma_start(g.x[:, :, :], blocks(g.d["x_t"])).then_inc(s["loaded"], 16)
            sp.dma_start(g.const[:, :], g.d["consts"]).then_inc(s["loaded"], 16)
            sp.dma_start(g.vec[:, :], g.d["vectors"]).then_inc(s["loaded"], 16)
            sp.dma_start(g.bmod[:, :], g.d["b_mod_t"]).then_inc(s["loaded"], 16)
            sp.dma_start(g.cond[:, :, :], g.d["cond_t"]).then_inc(s["loaded"], 16)

        @block.scalar
        def _(act):
            act.wait_ge(s["loaded"], 80)
            nc.scalar.activation(g.silu[:, :, :], g.cond[:, :, :], ACT.Sigmoid).then_inc(s["sig"], 1)

        @block.vector
        def _(dve):
            dve.wait_ge(s["sig"], 1)
            nc.vector.tensor_tensor(g.silu[:, :, :], g.silu[:, :, :], g.cond[:, :, :], ALU.mult)


def modulation(nc, g):
    NS = 512
    STEPS = DEPTH * 6 * D // NS
    with buffers(nc) as (sb, banks), phase(
            nc, "w_loaded:2", "rows_ready", "rows_copied", "cols_ready", "cols_added", "passed") as s:
        ring = sb("mod_ring", 2, NB, NS)
        rows = sb("mod_rows", 2, NS)
        bank = banks(4)
        with nc.Block() as block:

            @block.sync
            def _(sp):
                with sp.Fori(0, STEPS // 2) as i:
                    for b in range(2):
                        sp.wait_ge(s["rows_ready"], at(i, 2, b + 1))
                        sp.dma_start(ring[:, b].rearrange("p k n -> p (k n)"),
                                     slab(g.d["w_mod"], i * 2 + b)).then_inc(s["w_loaded"][b], 16)

            @block.tensor
            def _(pe):
                pe.sem_inc(s["rows_ready"], 2)
                with pe.Fori(0, STEPS // 2) as i:
                    for b in range(2):
                        pe.wait_ge(s["w_loaded"][b], at(i, 16, 16))
                        pe.wait_ge(s["rows_copied"], at(i, 2, b + 1))
                        for k in range(NB):
                            last = nc.tensor.matmul(bank[b][0:2, 0:NS], g.silu[:, k, :], ring[:, b, k, :],
                                                    start=(k == 0), stop=(k == NB - 1))
                        last.then_inc(s["rows_ready"], 1)
                        pe.wait_ge(s["rows_copied"], at(i, 2, b + 3))
                        wait_alone(pe, s["cols_added"], at(i, 2, b + 1), s["passed"])
                        for n in range(NS // P):
                            last = nc.tensor.transpose(bank[2 + b][:, 2 * n:2 * n + 2], rows[0:2, b, n * P:(n + 1) * P],
                                                       g.ident[0:2, 0:2])
                        last.then_inc(s["cols_ready"], 1)

            @block.scalar
            def _(act):
                act.sem_inc(s["rows_copied"], 2)
                with act.Fori(0, STEPS // 2) as i:
                    for b in range(2):
                        act.wait_ge(s["rows_ready"], at(i, 2, b + 3))
                        nc.scalar.copy(rows[0:2, b, :], bank[b][0:2, 0:NS]).then_inc(s["rows_copied"], 1)

            @block.vector
            def _(dve):
                dve.sem_inc(s["cols_added"], 2)
                with dve.Fori(0, STEPS // 2) as i:
                    for b in range(2):
                        dve.wait_ge(s["cols_ready"], at(i, 2, b + 1))
                        for c in range(2):
                            last = nc.vector.tensor_tensor(
                                g.mods[:, bass.ds(i * 8 + 4 * b, 4), c:c + 1].rearrange("p n o -> p (n o)"),
                                bank[2 + b][:, c:8:2],
                                g.bmod[:, bass.ds(i * 8 + 4 * b, 4)], ALU.add)
                        last.then_inc(s["cols_added"], 1)
                dve.wait_ge(s["cols_added"], STEPS + 2)
                for layer in range(DEPTH):
                    for piece in (1, 4):
                        part = g.mods[:, mod_at(layer, piece):mod_at(layer, piece) + NB, :]
                        nc.vector.tensor_scalar_add(part, part, 1.0)


def modulate_blocks(dve, nc, g, ready, scale, shift, done=None):
    for b in range(NB):
        ready(b)
        for c, (hs, xs) in enumerate(((H_LAT, S_LAT), (H_CTX, S_CTX))):
            last = nc.vector.tensor_scalar(g.h[:, b, hs], g.x[:, b, xs], g.mods[:, scale + b, c:c + 1],
                                           g.mods[:, shift + b, c:c + 1], ALU.mult, ALU.add)
        if done is not None:
            last.then_inc(done, 1)


def first_modulate(nc, g):
    with phase(nc, "unused"), nc.Block() as block:

        @block.vector
        def _(dve):
            modulate_blocks(dve, nc, g, lambda b: None, mod_at(0, 1), mod_at(0, 0))




def h_cols(g):
    return lambda k: (g.h[:, k, H_LAT], g.h[:, k, H_CTX])


def plain_cols(buf):
    return lambda k: (buf[:, k, S_LAT], buf[:, k, S_CTX])


def projection(nc, g, w, n_pairs, kg, src, out=None, hidden=None, mix=None, load=None):
    SLOTS = min(4, 2 * kg)
    VISITS = 2 * kg // SLOTS
    names = ["w_loaded:%d" % SLOTS, "mm_done", "evacuated", "stored:4", "squared", "mixed", "src_loaded"]
    with buffers(nc) as (sb, banks), phase(nc, *names) as s:
        ring = sb("ring", SLOTS, NB, 2 * P)
        stage = sb("stage", 4, T)
        bank = banks(8)
        acc = [(bank[2 * u], bank[2 * u + 1]) for u in range(4)]
        with nc.Block() as block:

            @block.sync
            def _(sp):
                if load is not None:
                    for b in range(NB):
                        sp.dma_start(load[0][:, b, :], load[1][b]).then_inc(s["src_loaded"], 16)
                with sp.Fori(0, n_pairs // 2) as i:
                    for n in range(2 * kg):
                        sp.wait_ge(s["mm_done"], at(i, 4 * kg, 2 * n + 2))
                        sp.dma_start(ring[:, n % SLOTS].rearrange("p k n -> p (k n)"),
                                     slab(w, i * (2 * kg) + n)).then_inc(s["w_loaded"][n % SLOTS], 16)

            @block.tensor
            def _(pe):
                pe.sem_inc(s["mm_done"], 2 * SLOTS)
                if mix is not None:
                    pe.wait_ge(s["mixed"], NB)
                if load is not None:
                    pe.wait_ge(s["src_loaded"], 16 * NB)
                with pe.Fori(0, n_pairs // 2) as i:
                    for n in range(2 * kg):
                        pair, part = divmod(n, kg)
                        pe.wait_ge(s["w_loaded"][n % SLOTS], at(i, 16 * VISITS, 16 * (n // SLOTS + 1)))
                        for m in range(2):
                            u = 2 * pair + m
                            if part == 0:
                                pe.wait_ge(s["evacuated"], at(i, 4, u + 1))
                            for k in range(NB):
                                lat, ctx = src(part * NB + k)
                                wt = ring[:, n % SLOTS, k, m * P:(m + 1) * P]
                                first, end = part == 0 and k == 0, part == kg - 1 and k == NB - 1
                                nc.tensor.matmul(acc[u][0][:, :], wt, lat, start=first, stop=end)
                                last = nc.tensor.matmul(acc[u][1][:, 0:CTX], wt, ctx, start=first, stop=end)
                            last.then_inc(s["mm_done"], 1)

            @block.scalar
            def _(act):
                act.sem_inc(s["evacuated"], 4)
                if hidden is None:
                    for u in range(4):
                        act.sem_inc(s["stored"][u], 16)
                with act.Fori(0, n_pairs // 2) as i:
                    for u in range(4):
                        pair, m = divmod(u, 2)
                        act.wait_ge(s["mm_done"], at(i, 4 * kg, 2 * SLOTS + 2 * (pair * kg + kg - 1) + m + 1))
                        if hidden is None:
                            act.wait_ge(s["stored"][u], at(i, 16, 16))
                        else:
                            act.wait_ge(s["squared"], at(i, 4, u + 1))
                        fn = ACT.Copy if hidden is None else ACT.Relu
                        nc.scalar.activation(stage[:, u, S_LAT], acc[u][0][:, :], fn)
                        nc.scalar.activation(stage[:, u, S_CTX], acc[u][1][:, 0:CTX], fn).then_inc(s["evacuated"], 1)
                        if hidden is None:
                            act.wait_ge(s["evacuated"], at(i, 4, u + 5))
                            act.dma_start(slab(out, i * 4 + u), stage[:, u, :]).then_inc(s["stored"][u], 16)
                if hidden is None:
                    for u in range(4):
                        act.wait_ge(s["stored"][u], 16 * (n_pairs // 2 + 1))

            @block.vector
            def _(dve):
                if mix is not None:
                    buf, col = mix
                    for b in range(NB):
                        nc.vector.scalar_tensor_tensor(buf[:, b, :], g.xx[:, b, :], g.vec[:, col + b:col + b + 1],
                                                       g.h[:, b, :], ALU.mult, ALU.add).then_inc(s["mixed"], 1)
                if hidden is not None:
                    dve.sem_inc(s["squared"], 4)
                    with dve.Fori(0, n_pairs // 2) as i:
                        for u in range(4):
                            dve.wait_ge(s["evacuated"], at(i, 4, u + 5))
                            nc.vector.tensor_tensor(hidden[:, bass.ds(i * 4 + u, 1), :].rearrange("p o t -> p (o t)"),
                                                    stage[:, u, :], stage[:, u, :], ALU.mult).then_inc(s["squared"], 1)




def norm(nc, g, delta, layer, sub, gate, nxt):
    col = V_LN + (layer * 2 + sub) * 2 * NB
    names = ["loaded", "gated", "added", "sums", "centred", "squares", "variances", "root", "inverse",
             "scaled", "gained", "stored"]
    with buffers(nc) as (sb, banks), phase(nc, *names) as s:
        dl = sb("delta", NB, T)
        rs = sb("rstd", T)
        mean_l, mean_c, var_l, var_c = banks(4)
        parts = ((S_LAT, mean_l, var_l, LAT), (S_CTX, mean_c, var_c, CTX))
        with nc.Block() as block:

            @block.sync
            def _(sp):
                for b in range(NB):
                    sp.dma_start(dl[:, b, :], delta[b]).then_inc(s["loaded"], 16)
                if nxt is None:
                    for b in range(NB):
                        sp.wait_ge(s["gained"], b + 1)
                        sp.dma_start(g.d["y_out"][b], g.x[:, b, :]).then_inc(s["stored"], 16)
                    sp.wait_ge(s["stored"], 16 * NB)

            @block.scalar
            def _(act):
                act.wait_ge(s["loaded"], 16 * NB)
                for b in range(NB):
                    for c, (cols, _, _, _) in enumerate(parts):
                        last = nc.scalar.activation(dl[:, b, cols], dl[:, b, cols], ACT.Identity,
                                                    scale=g.mods[:, gate + b, c:c + 1])
                    last.then_inc(s["gated"], 1)
                for b in range(NB):
                    act.wait_ge(s["centred"], b + 1)
                    nc.scalar.activation(dl[:, b, :], g.x[:, b, :], ACT.Square).then_inc(s["squares"], 1)
                act.wait_ge(s["variances"], 1)
                for cols, _, var, n in parts:
                    nc.scalar.activation(rs[:, cols], var[:, 0:n], ACT.Sqrt, bias=g.eps_ln).then_inc(s["root"], 1)
                for b in range(NB):
                    act.wait_ge(s["scaled"], b + 1)
                    nc.scalar.activation(g.x[:, b, :], g.x[:, b, :], ACT.Identity, scale=g.vec[:, col + b:col + b + 1],
                                         bias=g.vec[:, col + NB + b:col + NB + b + 1]).then_inc(s["gained"], 1)

            @block.tensor
            def _(pe):
                for b in range(NB):
                    pe.wait_ge(s["added"], b + 1)
                    for cols, mean, _, n in parts:
                        last = nc.tensor.matmul(mean[:, 0:n], g.mean_w, g.x[:, b, cols], start=(b == 0), stop=(b == NB - 1))
                last.then_inc(s["sums"], 1)
                for b in range(NB):
                    pe.wait_ge(s["squares"], b + 1)
                    for cols, _, var, n in parts:
                        last = nc.tensor.matmul(var[:, 0:n], g.mean_w, dl[:, b, cols], start=(b == 0), stop=(b == NB - 1))
                last.then_inc(s["variances"], 1)

            @block.vector
            def _(dve):
                for b in range(NB):
                    dve.wait_ge(s["gated"], b + 1)
                    nc.vector.scalar_tensor_tensor(g.x[:, b, :], g.x[:, b, :], ALPHA, dl[:, b, :],
                                                   ALU.mult, ALU.add).then_inc(s["added"], 1)
                dve.wait_ge(s["sums"], 1)
                for b in range(NB):
                    for cols, mean, _, n in parts:
                        last = nc.vector.tensor_tensor(g.x[:, b, cols], g.x[:, b, cols], mean[:, 0:n], ALU.subtract)
                    last.then_inc(s["centred"], 1)
                dve.wait_ge(s["root"], 2)
                nc.vector.reciprocal(rs[:, :], rs[:, :]).then_inc(s["inverse"], 1)
                dve.wait_ge(s["inverse"], 1)
                for b in range(NB):
                    nc.vector.tensor_tensor(g.x[:, b, :], g.x[:, b, :], rs[:, :], ALU.mult).then_inc(s["scaled"], 1)
                if nxt is not None:
                    modulate_blocks(dve, nc, g, lambda b: dve.wait_ge(s["gained"], b + 1), *nxt)




def chunked(ap):
    return ap.rearrange("p (u c) -> p u c", c=C)


def by_direction(buf, plain):
    yield buf[:, :, 0, :], chunked(plain)
    yield buf[:, 0:NLAT, 1, :], chunked(plain[:, S_LAT][:, ::-1])
    yield buf[:, NLAT:NCHUNK, 1, :], chunked(plain[:, S_CTX][:, ::-1])


def unit(u, hh):
    return GROUP * (u // 2) + 2 * hh + u % 2


def flat4(ap):
    return ap.rearrange("p u n -> p (u n)")


INVERSE_SEMS = ["first_t", "first_n_ps", "xx_ready", "y_ps", "ly_ready", "x_ps", "inv_ready"]
PER_GROUP = dict(first_t=2, first_n_ps=2, xx_ready=2 + 2 * (LEVELS - 1), y_ps=2 * LEVELS, ly_ready=2 * LEVELS,
                 x_ps=2 * LEVELS, inv_ready=2)


def group_at(i, j, name, k):
    return at(i, PER_GROUP[name] * NGROUP, PER_GROUP[name] * j + k)


def invert_pe(pe, nc, g, s, w, i, j):
    for h in range(2):
        pe.wait_ge(s["first_t"], group_at(i, j, "first_t", h + 1))
        for n in range(2):
            last = nc.tensor.transpose(w.y_bank[h][:, n * P:(n + 1) * P], w.xx[:, h, 1, n, :], g.ident)
        last.then_inc(s["first_n_ps"], 1)
    for lv in range(LEVELS):
        for h in range(2):
            pe.wait_ge(s["xx_ready"], group_at(i, j, "xx_ready", 2 * lv + h + 1))
            for n in range(2):
                last = nc.tensor.matmul(w.y_bank[h][:, n * P:(n + 1) * P], w.lt[:, 2 * h + n, :], w.xx[:, h, 0, n, :],
                                        start=True, stop=True)
            last.then_inc(s["y_ps"], 1)
        for h in range(2):
            pe.wait_ge(s["ly_ready"], group_at(i, j, "ly_ready", 2 * lv + h + 1))
            for n in range(2):
                last = nc.tensor.matmul(w.x_bank[h][:, (2 + n) * P:(3 + n) * P], w.y[:, h, n, :], w.xx[:, h, 1, n, :],
                                        start=True, stop=True)
            if lv < LEVELS - 1:
                for n in range(2):
                    last = nc.tensor.matmul(w.x_bank[h][:, n * P:(n + 1) * P], w.xx[:, h, 1, n, :], w.y[:, h, n, :],
                                            start=True, stop=True)
            last.then_inc(s["x_ps"], 1)


def invert_dve(dve, nc, g, s, w, i, j, link):
    l0 = g.mask(K_L0)
    for h in range(2):
        link(nc.vector.tensor_tensor(w.xx[:, h, 1, :, :], w.lt[:, 2 * h:2 * h + 2, :], l0.unsqueeze(1).to_broadcast([P, 2, P]),
                                     ALU.mult))
        nc.vector.tensor_tensor(w.xx[:, h, 1, :, :], w.xx[:, h, 1, :, :],
                                g.ident.unsqueeze(1).to_broadcast([P, 2, P]), ALU.add).then_inc(s["first_t"], 1)
    for h in range(2):
        dve.wait_ge(s["first_n_ps"], group_at(i, j, "first_n_ps", h + 1))
        nc.vector.tensor_copy(flat4(w.xx[:, h, 0, :, :]), w.y_bank[h][:, 0:2 * P]).then_inc(s["xx_ready"], 1)
    for lv in range(LEVELS):
        below = g.mask(K_LV + lv * P)
        for h in range(2):
            dve.wait_ge(s["y_ps"], group_at(i, j, "y_ps", 2 * lv + h + 1))
            nc.vector.tensor_tensor(w.y[:, h, :, :], w.y_bank[h][:, 0:2 * P].rearrange("p (n c) -> p n c", n=2),
                                    below.unsqueeze(1).to_broadcast([P, 2, P]), ALU.mult).then_inc(s["ly_ready"], 1)
        for h in range(2):
            dve.wait_ge(s["x_ps"], group_at(i, j, "x_ps", 2 * lv + h + 1))
            if lv < LEVELS - 1:
                both = w.xx[:, h].rearrange("p t n c -> p (t n c)")
                nc.vector.tensor_tensor(both, w.x_bank[h][:, :], both, ALU.add).then_inc(s["xx_ready"], 1)
            else:
                out = w.tt[:, GROUP * j + 2 * h:GROUP * j + 2 * h + 2, :]
                nc.vector.tensor_tensor(flat4(out), w.x_bank[h][:, 2 * P:4 * P], flat4(w.xx[:, h, 1, :, :]),
                                        ALU.add).then_inc(s["inv_ready"], 1)


class Work:
    pass



W_W0, W_A0, W_KK, W_KA, W_RK, W_GG, W_GB = 0, 2, 4, 5, 6, 7, 8
W_COLS = 9
W_END = 3 * P + W_COLS


def token_shift(nc, g):
    with phase(nc, "neighbours") as s, nc.Block() as block:

        @block.vector
        def _(dve):
            nc.vector.memset(g.xx[:, :, :], 0.0).then_inc(s["neighbours"], 1)
            for edge in (slice(0, 1), slice(H_LAT.stop, H_CTX.start), slice(H_CTX.stop, HW)):
                nc.vector.memset(g.h[:, :, edge], 0.0).then_inc(s["neighbours"], 1)
            dve.wait_ge(s["neighbours"], 4)
            for b in range(NB):
                nc.vector.tensor_tensor(g.xx[:, b, 1:HW - 1], g.h[:, b, 0:HW - 2], g.h[:, b, 2:HW],
                                        ALU.add).then_inc(s["neighbours"], 1)
            for b in range(NB):
                dve.wait_ge(s["neighbours"], b + 5)
                nc.vector.scalar_tensor_tensor(g.xx[:, b, 1:HW - 1], g.xx[:, b, 1:HW - 1], 0.5, g.h[:, b, 1:HW - 1],
                                               ALU.mult, ALU.subtract)


def low_rank(nc, g, j, low):
    with buffers(nc) as (sb, banks), phase(nc, "loaded", "mixed", "mm_done", "evacuated") as s:
        wt = sb("low_w", 3, NB, P)
        xi = sb("low_x", 2, NB, HW)
        bank = banks(4)
        with nc.Block() as block:

            @block.sync
            def _(sp):
                sp.dma_start(wt[:, :, :, :].rearrange("p a k n -> p a (k n)"),
                             g.d["rw_low"][3 * j:3 * j + 3].rearrange("a p n -> p a n")).then_inc(s["loaded"], 16)

            @block.vector
            def _(dve):
                for n, m in enumerate((1, 4, 5)):
                    if n >= 2:
                        dve.wait_ge(s["mm_done"], n - 1)
                    for b in range(NB):
                        col = V_MU + (j * 6 + m) * NB + b
                        last = nc.vector.scalar_tensor_tensor(xi[:, n % 2, b, :], g.xx[:, b, :], g.vec[:, col:col + 1],
                                                              g.h[:, b, :], ALU.mult, ALU.add)
                    last.then_inc(s["mixed"], 1)

            @block.tensor
            def _(pe):
                pe.wait_ge(s["loaded"], 16)
                for n in range(3):
                    pe.wait_ge(s["mixed"], n + 1)
                    if n >= 2:
                        pe.wait_ge(s["evacuated"], n - 1)
                    for k in range(NB):
                        nc.tensor.matmul(bank[2 * (n % 2)][:, :], wt[:, n, k, :], xi[:, n % 2, k, H_LAT],
                                         start=(k == 0), stop=(k == NB - 1))
                        last = nc.tensor.matmul(bank[2 * (n % 2) + 1][:, 0:CTX], wt[:, n, k, :], xi[:, n % 2, k, H_CTX],
                                                start=(k == 0), stop=(k == NB - 1))
                    last.then_inc(s["mm_done"], 1)

            @block.scalar
            def _(act):
                for n, fn in enumerate((ACT.Tanh, ACT.Copy, ACT.Sigmoid)):
                    act.wait_ge(s["mm_done"], n + 1)
                    nc.scalar.activation(low[:, n, S_LAT], bank[2 * (n % 2)][:, :], fn)
                    nc.scalar.activation(low[:, n, S_CTX], bank[2 * (n % 2) + 1][:, 0:CTX], fn).then_inc(s["evacuated"], 1)


STEPS = NCHUNK
ORDER = (8, 9, 0, 1, 2, 3, 4, 5, 6, 7)


def rwkv_heads(nc, g, j, low):
    names = ["passed", "in_loaded", "s0_loaded", "gains", "y_stored", "state_stored", "link", "squares", "projected", "sums", "sig_w", "sig_a", "gates",
             "roots", "scanned", "g_before", "exps", "reversed_v", "bonus_in", "bonus_sums", "bonus", "operands",
             "products", "masked", "tokens", "tokens_out", "chain_x", "x_out", "chain_sa", "sa_out", "chain_s",
             "s0_ready", "s1_ready", "s_first", "values", "saz_out", "o_done", "s_saved", "y_in", "means", "y_centred", "y_squares", "vars", "y_root", "y_ready",
             ] + INVERSE_SEMS
    with buffers(nc) as (sb, banks), phase(nc, *names) as s:
        w = Work()
        rkv, hw, s0 = sb("rkv", 3, T), sb("head_w", W_END), sb("s0", 2, C)
        t1, rn, bs, os_, sq = (sb(n, T) for n in ("t1", "rn", "bs", "os", "sq"))
        ld, icl, gc, e_in, kk, kd, ve, rt, kt, at_, bt = (
            sb(n, NCHUNK, 2, C) for n in ("ld", "icl", "gc", "e_in", "kk2", "kd", "ve", "rt", "kt", "at", "bt"))
        two = sb("e_ex_inv", 2 * NCHUNK, 2, C)
        e_ex, e_inv, vz = two[:, 0:NCHUNK], two[:, NCHUNK:2 * NCHUNK], two
        w.lt, w.xx, w.y = sb("lt", GROUP, P), sb("xx", 2, 2, 2, P), sb("y", 2, 2, P)
        w.tt, ak, rr = sb("tt", 2 * NCHUNK, P), sb("ak", 2 * NCHUNK, P), sb("rr", 2, 2 * NCHUNK, P)
        spare = g.h[:, :, :].rearrange("p b t -> p (b t)")
        tok = spare[:, 0:3 * TT].rearrange("p (u q c) -> p u q c", q=3, c=C)
        bon, gate = spare[:, 3 * TT:3 * TT + T], spare[:, 3 * TT + T:4 * TT]
        gn = sb("gn", 2)
        xs, sa, saz = sb("xs", 2, C), sb("sa", 2, C), sb("saz", 2, 2, C)
        st = sb("state", 2, 2, C)
        sout = sb("sout", 2, C)
        bank = banks(8)
        w.y_bank, w.x_bank = bank[0:2], bank[2:4]
        lat_banks, ctx_bank = (bank[4], bank[5], bank[6], bank[7]), (bank[2], bank[1])
        GATE_CTX = slice(2 * P, 3 * P)
        ctx_cols_of = lambda m, e: ctx_bank[e][:, (m + e) * P:(m + e + 1) * P]
        r, k, v = rkv[:, 0, :], rkv[:, 1, :], rkv[:, 2, :]
        hcol = lambda n: hw[:, 3 * P + n:3 * P + n + 1]
        flat = lambda buf: buf[:, 0:NCHUNK, :, :].rearrange("p u e c -> p (u e c)")

        with nc.Block() as block:

            @block.sync
            def _(sp):
                def load(n):
                    for m in range(3):
                        sp.dma_start(rkv[:, m, :], slab(g.d["rkv"], n + m * NB)).then_inc(s["in_loaded"], 16)
                    sp.dma_start(hw[:, :], slab(g.d["rw_head"], n + j * NB)).then_inc(s["in_loaded"], 16)

                def load_state(n):
                    sp.dma_start(s0[:, :, :].rearrange("p e v -> p (e v)"),
                                 slab(g.d["rw_state"], n + j * NB)).then_inc(s["s0_loaded"], 16)

                def store_state(i):
                    wait_alone(sp, s["s_saved"], at(i, 2, 2), s["passed"])
                    sp.dma_start(slab(g.d["rw_state_out"], i + j * NB),
                                 sout[:, :, :].rearrange("p e v -> p (e v)")).then_inc(s["state_stored"], 16)

                def store_block(i):
                    wait_alone(sp, s["y_ready"], at(i, 1, 2), s["passed"])
                    sp.dma_start(slab(g.d["mixed"], i), os_[:, :]).then_inc(s["y_stored"], 16)

                sp.sem_inc(s["y_stored"], 16)
                sp.sem_inc(s["state_stored"], 16)
                load(0)
                load_state(0)
                with sp.Fori(0, NB - 1) as i:
                    wait_alone(sp, s["operands"], at(i, 7, 7), s["passed"])
                    wait_alone(sp, s["reversed_v"], at(i, 3, 3), s["passed"])
                    load(i + 1)
                    store_state(i)
                    wait_alone(sp, s["s0_ready"], at(i, STEPS, 2), s["passed"])
                    wait_alone(sp, s["s1_ready"], at(i, STEPS, 2), s["passed"])
                    load_state(i + 1)
                    store_block(i)
                store_state(NB - 1)
                store_block(NB - 1)
                sp.wait_ge(s["state_stored"], 16 * (NB + 1))
                sp.wait_ge(s["y_stored"], 16 * (NB + 1))

            @block.gpsimd
            def _(pool):
                with pool.Fori(0, NB) as i:
                    wait_alone(pool, s["in_loaded"], at(i, 64, 64), s["passed"])
                    for both, plain in by_direction(ve, v):
                        nc.gpsimd.tensor_copy(both, plain).then_inc(s["reversed_v"], 1)
                    for jg in range(NGROUP):
                        wait_alone(pool, s["tokens_out"], at(i, NGROUP, jg + 1), s["passed"])
                        for e in range(2):
                            nc.gpsimd.tensor_tensor(
                                vz[:, GROUP * jg:GROUP * (jg + 1), e, :], tok[:, GROUP * jg:GROUP * (jg + 1), 1, :],
                                g.const[:, K_BO + e * C:K_BO + (e + 1) * C].unsqueeze(1).to_broadcast([P, GROUP, C]),
                                ALU.mult).then_inc(s["values"], 1)

            @block.scalar
            def _(act):
                def rates(i):
                    act.wait_ge(s["projected"], at(i, 1, 1))
                    for m, (buf, col, done) in enumerate(((ld, W_W0, s["sig_w"]), (icl, W_A0, s["sig_a"]))):
                        for e in range(2):
                            lat_bank, ctx_cols = lat_banks[2 * m + e], ctx_cols_of(m, e)
                            turn = slice(None, None, -1 if e else 1)
                            nc.scalar.activation(buf[:, 0:NLAT, e, :], chunked(lat_bank[:, turn]), ACT.Sigmoid,
                                                 bias=hcol(col + e))
                            nc.scalar.activation(buf[:, NLAT:NCHUNK, e, :], chunked(ctx_cols[:, turn]), ACT.Sigmoid,
                                                 bias=hcol(col + e)).then_inc(done, 1)

                rates(0)

                def block_(i, more):
                    act.wait_ge(s["y_ready"], at(i, 1, 1))
                    nc.scalar.copy(gate[:, S_LAT], bank[3][:, :])
                    nc.scalar.copy(gate[:, S_CTX], bank[2][:, GATE_CTX]).then_inc(s["gates"], 1)
                    act.wait_ge(s["sums"], at(i, 1, 1))
                    nc.scalar.activation(rn[:, S_LAT], bank[0][:, :], ACT.Sqrt, bias=g.eps_nrm)
                    nc.scalar.activation(rn[:, S_CTX], bank[1][:, 0:CTX], ACT.Sqrt, bias=g.eps_nrm).then_inc(s["roots"], 1)
                    act.wait_ge(s["scanned"], at(i, 1, 1))
                    nc.scalar.activation(flat(e_in), flat(gc), ACT.Exp).then_inc(s["exps"], 1)
                    nc.scalar.activation(flat(e_inv), flat(gc), ACT.Exp, scale=-1.0).then_inc(s["exps"], 1)
                    act.wait_ge(s["g_before"], at(i, 1, 1))
                    nc.scalar.activation(flat(e_ex), flat(ld), ACT.Exp).then_inc(s["exps"], 1)
                    for jg in range(NGROUP):
                        act.wait_ge(s["tokens"], at(i, 2 * NGROUP, 2 * jg + 2))
                        for hh in range(2):
                            u2 = slice(GROUP * jg + 2 * hh, GROUP * jg + 2 * hh + 2)
                            last = nc.scalar.copy(tok[:, u2, :, :].rearrange("p u q c -> p (u q c)"),
                                                  bank[4 + hh][:, 0:6 * C])
                        last.then_inc(s["tokens_out"], 1)
                    for n in range(STEPS):
                        u = ORDER[n]
                        act.wait_ge(s["chain_s"], at(i, STEPS, n + 1))
                        for e in range(2):
                            last = nc.scalar.activation(st[0:C, e, 0, :], bank[2][0:C, e * C:(e + 1) * C], ACT.Identity,
                                                        scale=e_in[0:C, u, e, C - 1:C])
                        last.then_inc(s["s_first"] if n == 1 else s["s0_ready"], 1)
                    act.wait_ge(s["vars"], at(i, 1, 1))
                    nc.scalar.activation(rn[:, S_LAT], bank[0][:, :], ACT.Sqrt, bias=g.eps_gn)
                    nc.scalar.activation(rn[:, S_CTX], bank[1][:, 0:CTX], ACT.Sqrt, bias=g.eps_gn).then_inc(s["y_root"], 1)
                    if more:
                        rates(i + 1)

                with act.Fori(0, NB - 1) as i:
                    block_(i, True)
                block_(NB - 1, False)

            @block.tensor
            def _(pe):
                def project(dst_l, dst_c, weights, rows, n):
                    nc.tensor.matmul(dst_l, weights, low[rows, n, S_LAT], start=True, stop=True)
                    return nc.tensor.matmul(dst_c, weights, low[rows, n, S_CTX], start=True, stop=True)

                def head_sums(src, lat, ctx):
                    nc.tensor.matmul(lat, g.mask(K_BO), src[:, S_LAT], start=True, stop=True)
                    return nc.tensor.matmul(ctx, g.mask(K_BO), src[:, S_CTX], start=True, stop=True)

                def pair(buf, rows, u):
                    return buf[rows, u, :, :].rearrange("p e c -> p (e c)")

                def project_rate(m, e):
                    rows = slice(C * e, C * (e + 1))
                    return project(lat_banks[2 * m + e][:, :], ctx_cols_of(m, e), hw[rows, m * P:(m + 1) * P], rows, m)

                def project_rest():
                    project_rate(0, 1)
                    project_rate(1, 1)
                    project(bank[3][:, :], bank[2][:, GATE_CTX], hw[:, 2 * P:3 * P], slice(0, P), 2).then_inc(s["projected"], 1)

                pe.wait_ge(s["in_loaded"], 64)
                project_rate(0, 0)
                project_rate(1, 0)
                project_rest()

                def block_(i, more):
                    pe.wait_ge(s["squares"], at(i, 1, 1))
                    pe.wait_ge(s["gates"], at(i, 1, 1))
                    head_sums(sq, bank[0][:, :], bank[1][:, 0:CTX]).then_inc(s["sums"], 1)
                    pe.wait_ge(s["bonus_in"], at(i, 1, 1))
                    pe.wait_ge(s["roots"], at(i, 1, 1))
                    head_sums(bs, bank[0][:, :], bank[1][:, 0:CTX]).then_inc(s["bonus_sums"], 1)
                    pe.wait_ge(s["operands"], at(i, 7, 7))
                    pe.wait_ge(s["reversed_v"], at(i, 3, 3))
                    pe.wait_ge(s["bonus"], at(i, 1, 1))
                    for jg in range(NGROUP):
                        if jg >= 1:
                            pe.wait_ge(s["inv_ready"], group_at(i, jg - 1, "inv_ready", 2))
                            pe.wait_ge(s["tokens_out"], at(i, NGROUP, jg))
                        for hh in range(2):
                            hr = slice(C * hh, C * (hh + 1))
                            for q, (left, right) in enumerate(((bt, at_), (kt, at_), (kt, rt), (bt, rt))):
                                for n in range(2):
                                    c0 = (2 * (q % 2) + n) * P
                                    last = nc.tensor.matmul(bank[2 * hh + q // 2][:, c0:c0 + P], pair(left, hr, 2 * jg + n),
                                                            pair(right, hr, 2 * jg + n), start=True, stop=True)
                            last.then_inc(s["products"], 1)
                        for hh in range(2):
                            hr = slice(C * hh, C * (hh + 1))
                            for n in range(2):
                                for q, src in enumerate((kt, ve, bt)):
                                    c0 = (3 * n + q) * C
                                    last = nc.tensor.transpose(bank[4 + hh][:, c0:c0 + C], pair(src, hr, 2 * jg + n),
                                                               g.const[hr, K_ID + hr.start:K_ID + hr.stop])
                            last.then_inc(s["tokens"], 1)
                        pe.wait_ge(s["masked"], at(i, 6 * NGROUP, 6 * jg + 6))
                        invert_pe(pe, nc, g, s, w, i, jg)
                    pe.wait_ge(s["inv_ready"], group_at(i, NGROUP - 1, "inv_ready", 2))
                    pe.wait_ge(s["tokens_out"], at(i, NGROUP, NGROUP))
                    pe.wait_ge(s["values"], at(i, 2 * NGROUP, 2 * NGROUP))
                    for n in range(STEPS):
                        u = ORDER[n]
                        uks = [unit(u, hh) for hh in range(2)]
                        o_tile = bank[4 + u // 4][:, (u % 4) * P:(u % 4 + 1) * P]
                        if n:
                            pe.wait_ge(s["s0_ready"], at(i, STEPS, n))
                            pe.wait_ge(s["s1_ready"], at(i, STEPS, n))
                        for hh, uk in enumerate(uks):
                            dst = bank[0][:, hh * P:(hh + 1) * P]
                            nc.tensor.matmul(dst, pair(at_, slice(0, P), u), st[:, :, hh, :], start=True, stop=False)
                            last = nc.tensor.matmul(dst, ak[:, uk, :], tok[:, uk, 1, :].unsqueeze(1).to_broadcast([P, 2, C]),
                                                    start=False, stop=True)
                        last.then_inc(s["chain_x"], 1)
                        for hh, uk in enumerate(uks):
                            hr = slice(C * hh, C * (hh + 1))
                            nc.tensor.matmul(o_tile[hr, :], tok[:, uk, 1, :], rr[:, 0, uk, :], start=True, stop=False,
                                             skip_group_check=True)
                        for e in range(2):
                            nc.tensor.matmul(o_tile[:, e * C:(e + 1) * C], st[:, e, :, :].rearrange("p h v -> p (h v)"),
                                             rt[:, u, e, :], start=False, stop=False, skip_group_check=True)
                        pe.wait_ge(s["x_out"], at(i, 2 * STEPS, 2 * n + 2))
                        for hh, uk in enumerate(uks):
                            last = nc.tensor.matmul(bank[1][:, hh * P:(hh + 1) * P], w.tt[:, uk, :],
                                                    xs[:, hh, :].unsqueeze(1).to_broadcast([P, 2, C]), start=True, stop=True)
                        last.then_inc(s["chain_sa"], 1)
                        for hh, uk in enumerate(uks):
                            hr = slice(C * hh, C * (hh + 1))
                            nc.tensor.matmul(bank[2][hr, 0:P], g.ident[:, hr], st[:, :, hh, :], start=True, stop=False)
                            nc.tensor.matmul(bank[2][hr, 0:P], tok[:, uk, 0, :], pair(vz, slice(0, P), uk), start=False, stop=False)
                        pe.wait_ge(s["saz_out"], at(i, STEPS, n + 1))
                        for hh, uk in enumerate(uks):
                            hr = slice(C * hh, C * (hh + 1))
                            last = nc.tensor.matmul(bank[2][hr, 0:P], tok[:, uk, 2, :], pair(saz, slice(0, P), hh),
                                                    start=False, stop=True)
                        last.then_inc(s["chain_s"], 1)
                        pe.wait_ge(s["sa_out"], at(i, STEPS, n + 1))
                        for hh, uk in enumerate(uks):
                            hr = slice(C * hh, C * (hh + 1))
                            last = nc.tensor.matmul(o_tile[hr, :], sa[:, hh, :], rr[:, 1, uk, :], start=False, stop=True,
                                                    skip_group_check=True)
                        last.then_inc(s["o_done"], 1)
                    pe.wait_ge(s["y_in"], at(i, 3, 3))
                    head_sums(os_, bank[0][:, :], bank[1][:, 0:CTX]).then_inc(s["means"], 1)
                    pe.wait_ge(s["s0_ready"], at(i, STEPS, STEPS))
                    pe.wait_ge(s["s1_ready"], at(i, STEPS, STEPS))
                    if more:
                        pe.wait_ge(s["in_loaded"], at(i, 64, 128))
                        project_rate(0, 0)
                        project_rate(1, 0)
                    pe.wait_ge(s["y_squares"], at(i, 1, 1))
                    head_sums(sq, bank[0][:, :], bank[1][:, 0:CTX]).then_inc(s["vars"], 1)
                    if more:
                        pe.wait_ge(s["y_root"], at(i, 1, 1))
                        project_rest()

                with pe.Fori(0, NB - 1) as i:
                    block_(i, True)
                block_(NB - 1, False)

            @block.vector
            def _(dve):
                dve.sem_inc(s["y_ready"], 1)
                with dve.Fori(0, NB) as i:
                    link = Link(dve, s["link"], i, LINKS_RW)
                    dve.wait_ge(s["in_loaded"], at(i, 64, 64))
                    dve.wait_ge(s["y_ready"], at(i, 1, 1))
                    nc.vector.tensor_copy(gn[:, :], hw[:, 3 * P + W_GG:3 * P + W_GB + 1]).then_inc(s["gains"], 1)
                    link(nc.vector.tensor_scalar(t1[:, :], k, hcol(W_KK), None, ALU.mult))
                    nc.vector.tensor_tensor(sq[:, :], t1[:, :], t1[:, :], ALU.mult).then_inc(s["squares"], 1)
                    dve.wait_ge(s["sig_w"], at(i, 2, 2))
                    link(nc.vector.tensor_scalar(flat(ld), flat(ld), -HALF_DECAY, None, ALU.mult))
                    nc.vector.tensor_tensor_scan(flat(gc), g.const[:, K_SCAN:K_SCAN + TT], flat(ld), 0.0,
                                                 ALU.mult, ALU.add).then_inc(s["scanned"], 1)
                    dve.wait_ge(s["scanned"], at(i, 1, 1))
                    nc.vector.tensor_tensor(flat(ld), flat(gc), flat(ld), ALU.subtract).then_inc(s["g_before"], 1)
                    dve.wait_ge(s["sig_a"], at(i, 2, 2))
                    link(nc.vector.tensor_scalar(flat(kd), flat(icl), -1.0, hcol(W_KA), ALU.add, ALU.mult))
                    for both, plain in by_direction(kd, k):
                        last = nc.vector.scalar_tensor_tensor(both, both, 1.0, plain, ALU.add, ALU.mult)
                    link(last)
                    for us in (slice(0, NLAT), slice(NLAT, NCHUNK)):
                        last = nc.vector.tensor_tensor(chunked(bs[:, :])[:, us, :], kd[:, us, 0, :],
                                                       kd[:, us, 1, :][:, ::-1, ::-1], ALU.add)
                    link(last)
                    nc.vector.scalar_tensor_tensor(bs[:, :], r, hcol(W_RK), bs[:, :], ALU.mult, ALU.mult).then_inc(s["bonus_in"], 1)
                    dve.wait_ge(s["roots"], at(i, 1, 1))
                    link(nc.vector.reciprocal(rn[:, :], rn[:, :]))
                    for (both, plain), (_, root) in zip(by_direction(kk, t1[:, :]), by_direction(kk, rn[:, :])):
                        last = nc.vector.tensor_tensor(both, plain, root, ALU.mult)
                    link(last)
                    dve.wait_ge(s["bonus_sums"], at(i, 1, 1))
                    nc.vector.tensor_tensor(bon[:, S_LAT], bank[0][:, :], v[:, S_LAT], ALU.mult)
                    nc.vector.tensor_tensor(bon[:, S_CTX], bank[1][:, 0:CTX], v[:, S_CTX], ALU.mult).then_inc(s["bonus"], 1)
                    link(nc.vector.tensor_tensor(flat(bt), flat(kk), flat(icl), ALU.mult))
                    dve.wait_ge(s["exps"], at(i, 3, 3))
                    nc.vector.scalar_tensor_tensor(flat(bt), flat(bt), -1.0, flat(e_inv), ALU.mult,
                                                   ALU.mult).then_inc(s["operands"], 1)
                    nc.vector.tensor_tensor(flat(at_), flat(kk), flat(e_ex), ALU.mult).then_inc(s["operands"], 1)
                    nc.vector.tensor_tensor(flat(kt), flat(kd), flat(e_inv), ALU.mult).then_inc(s["operands"], 1)
                    for (both, plain), (decay, _) in zip(by_direction(rt, r), by_direction(e_in, r)):
                        nc.vector.tensor_tensor(both, plain, decay, ALU.mult).then_inc(s["operands"], 1)
                    nc.vector.memset(st[:, :, :, :], 0.0).then_inc(s["operands"], 1)
                    for jg in range(NGROUP):
                        for hh in range(2):
                            dve.wait_ge(s["products"], at(i, 2 * NGROUP, 2 * jg + hh + 1))
                            u2 = slice(GROUP * jg + 2 * hh, GROUP * jg + 2 * hh + 2)
                            later = g.mask(K_SP).unsqueeze(1).to_broadcast([P, 2, P])
                            for q, out in enumerate((w.lt[:, 2 * hh:2 * hh + 2, :], ak[:, u2, :])):
                                cols = bank[2 * hh][:, q * 2 * P:(q + 1) * 2 * P].rearrange("p (n c) -> p n c", n=2)
                                nc.vector.tensor_tensor(out, cols, later, ALU.mult).then_inc(s["masked"], 1)
                            nc.vector.tensor_tensor(rr[:, :, u2, :],
                                                    bank[2 * hh + 1][:, :].rearrange("p (q n c) -> p q n c", q=2, n=2),
                                                    g.mask(K_IP).unsqueeze(1).unsqueeze(1).to_broadcast([P, 2, 2, P]),
                                                    ALU.mult).then_inc(s["masked"], 1)
                        dve.wait_ge(s["masked"], at(i, 6 * NGROUP, 6 * jg + 6))
                        invert_dve(dve, nc, g, s, w, i, jg, link)
                    for n in range(STEPS):
                        u = ORDER[n]
                        dve.wait_ge(s["chain_x"], at(i, STEPS, n + 1))
                        for e in range(2):
                            er = slice(C * e, C * (e + 1))
                            nc.vector.tensor_copy(xs[er, :, :], bank[0][er, 0:2 * P].rearrange("p (h n) -> p h n", h=2)[:, :, er]
                                                  ).then_inc(s["x_out"], 1)
                        dve.wait_ge(s["chain_sa"], at(i, STEPS, n + 1))
                        nc.vector.tensor_tensor(saz[:, :, :, :].rearrange("p h e v -> p h (e v)"),
                                                bank[1][:, 0:2 * P].rearrange("p (h n) -> p h n", h=2),
                                                g.mask(K_BO).unsqueeze(1).to_broadcast([P, 2, P]), ALU.mult).then_inc(s["saz_out"], 1)
                        if n >= 1:
                            dve.wait_ge(s["o_done"], at(i, STEPS, n))
                        nc.vector.tensor_copy(sa[:, :, :], bank[1][:, 0:2 * P].rearrange("p (h n) -> p h n", h=2)[:, :, 0:C]
                                              ).then_inc(s["sa_out"], 1)
                        dve.wait_ge(s["chain_s"], at(i, STEPS, n + 1))
                        for e in range(2):
                            last = nc.vector.tensor_scalar(st[C:P, e, 1, :], bank[2][C:P, e * C:(e + 1) * C],
                                                           e_in[C:P, u, e, C - 1:C], None, ALU.mult)
                        if n != 1:
                            last.then_inc(s["s1_ready"], 1)
                            continue
                        link(last)
                        dve.wait_ge(s["s_first"], at(i, 1, 1))
                        dve.wait_ge(s["o_done"], at(i, STEPS, 2))
                        dve.wait_ge(s["state_stored"], at(i, 16, 16))
                        dve.wait_ge(s["s0_loaded"], at(i, 16, 16))
                        for hh in range(2):
                            hr = slice(C * hh, C * (hh + 1))
                            nc.vector.tensor_copy(sout[hr, :, :], st[hr, :, hh, :]).then_inc(s["s_saved"], 1)
                        dve.wait_ge(s["s_saved"], at(i, 2, 2))
                        for hh, done in enumerate((s["s0_ready"], s["s1_ready"])):
                            hr = slice(C * hh, C * (hh + 1))
                            nc.vector.tensor_copy(st[hr, :, hh, :], s0[hr, :, :]).then_inc(done, 1)
                    dve.wait_ge(s["o_done"], at(i, STEPS, STEPS))
                    dve.wait_ge(s["y_stored"], at(i, 16, 16))
                    tiles = lambda b, m: bank[b][:, 0:m * P].rearrange("p (u e c) -> p u e c", u=m, e=2)
                    spans = ((4, 4, 0, 2 * P), (5, 4, 2 * P, 4 * P), (6, 2, LAT, T))
                    turned = ((4, 4, 2 * P, 4 * P), (5, 4, 0, 2 * P), (6, 2, LAT, T))
                    for b, m, t0, t1_ in spans:
                        last = nc.vector.tensor_copy(chunked(os_[:, t0:t1_]), tiles(b, m)[:, :, 0, :])
                    link(last)
                    for b, m, t0, t1_ in turned:
                        out = chunked(os_[:, t0:t1_])
                        nc.vector.tensor_tensor(out, tiles(b, m)[:, ::-1, 1, ::-1], out, ALU.add).then_inc(s["y_in"], 1)
                    dve.wait_ge(s["means"], at(i, 1, 1))
                    nc.vector.scalar_tensor_tensor(os_[:, S_LAT], bank[0][:, :], -1.0 / C, os_[:, S_LAT], ALU.mult, ALU.add)
                    nc.vector.scalar_tensor_tensor(os_[:, S_CTX], bank[1][:, 0:CTX], -1.0 / C, os_[:, S_CTX],
                                                   ALU.mult, ALU.add).then_inc(s["y_centred"], 1)
                    dve.wait_ge(s["y_centred"], at(i, 1, 1))
                    nc.vector.scalar_tensor_tensor(sq[:, :], os_[:, :], 1.0 / C, os_[:, :], ALU.mult,
                                                   ALU.mult).then_inc(s["y_squares"], 1)
                    dve.wait_ge(s["y_root"], at(i, 1, 1))
                    link(nc.vector.reciprocal(rn[:, :], rn[:, :]))
                    link(nc.vector.tensor_tensor(os_[:, :], os_[:, :], rn[:, :], ALU.mult))
                    link(nc.vector.tensor_scalar(os_[:, :], os_[:, :], gn[:, 0:1], gn[:, 1:2], ALU.mult, ALU.add))
                    link(nc.vector.tensor_tensor(os_[:, :], os_[:, :], bon[:, :], ALU.add))
                    nc.vector.tensor_tensor(os_[:, :], os_[:, :], gate[:, :], ALU.mult).then_inc(s["y_ready"], 1)
                    link.end()


LINKS_RW = 13 + 2 * NGROUP + 1



KEYS = P + T
KT_LAT, KT_CTX = slice(0, P + LAT), slice(P + LAT, KEYS)
QTILES = T // P
KTILES = KEYS // P
GROUPS = AT_HEADS // AT_KV
A_GAIN, A_COLS = 0, 2
TILES = GROUPS * QTILES


def normed_rotated(nc, g):
    NQK = 10
    names = ["passed", "const", "loaded:2", "squares", "sums", "root", "normed", "swapped", "link", "link_first", "done", "stored:2", "cache"]
    with buffers(nc) as (sb, banks), phase(nc, *names) as s:
        qb, sq, rn, out = (sb(n, 2, T) for n in ("qk", "sq", "rn", "out"))
        gain = sb("gain", 2, 1)
        tab, perm = sb("rope", 2, T), sb("perm", P)
        bank = banks(8)
        ss = [(bank[2 * b], bank[2 * b + 1]) for b in range(2)]
        sw = [(bank[4 + 2 * b], bank[5 + 2 * b]) for b in range(2)]
        with nc.Block() as block:

            @block.sync
            def _(sp):
                sp.dma_start(tab[:, :, :], g.d["rope_t"]).then_inc(s["const"], 16)
                sp.dma_start(perm[:, :], g.d["rope_perm"]).then_inc(s["const"], 16)
                def load(n, b):
                    sp.dma_start(qb[:, b, :], slab(g.d["qkv"], n)).then_inc(s["loaded"][b], 16)
                    sp.dma_start(gain[:, b, :], slab(g.d["at_gain"], n)).then_inc(s["loaded"][b], 16)

                def store(n, b):
                    sp.dma_start(slab(g.d["qk_rot"], n), out[:, b, :]).then_inc(s["stored"][b], 16)

                for b in range(2):
                    sp.sem_inc(s["stored"][b], 16)
                    load(b, b)
                with sp.Fori(0, NQK // 2 - 1) as i:
                    for b in range(2):
                        wait_alone(sp, s["done"], at(i, 2, b + 1), s["passed"])
                        store(i * 2 + b, b)
                        load(i * 2 + (b + 2), b)
                for b in range(2):
                    sp.wait_ge(s["done"], NQK - 1 + b)
                    store(NQK - 2 + b, b)
                for b in range(2):
                    sp.wait_ge(s["stored"][b], 16 * (NQK // 2 + 1))
                for b in range(2):
                    sp.dma_start(g.d["kv_out"][b], g.d["qk_rot"][8 + b, :, S_CTX]).then_inc(s["cache"], 16)
                    sp.dma_start(g.d["kv_out"][2 + b], g.d["qkv"][10 + b, :, S_CTX]).then_inc(s["cache"], 16)
                sp.wait_ge(s["cache"], 64)

            @block.scalar
            def _(act):
                act.sem_inc(s["swapped"], 1)
                with act.Fori(0, NQK // 2) as i:
                    for b in range(2):
                        act.wait_ge(s["loaded"][b], at(i, 32, 32))
                        act.wait_ge(s["swapped"], at(i, 2, b + 1))
                        nc.scalar.activation(sq[:, b, :], qb[:, b, :], ACT.Square).then_inc(s["squares"], 1)
                        act.wait_ge(s["sums"], at(i, 2, b + 1))
                        lat, ctx = ss[b]
                        nc.scalar.activation(rn[:, b, S_LAT], lat[:, :], ACT.Sqrt, bias=g.eps_nrm, scale=1.0 / HD)
                        nc.scalar.activation(rn[:, b, S_CTX], ctx[:, 0:CTX], ACT.Sqrt, bias=g.eps_nrm,
                                             scale=1.0 / HD).then_inc(s["root"], 1)

            @block.tensor
            def _(pe):
                def sums(i, b, n):
                    pe.wait_ge(s["squares"], at(i, 2, n + 1))
                    lat, ctx = ss[b]
                    nc.tensor.matmul(lat[:, :], g.mask(K_BO), sq[:, b, S_LAT], start=True, stop=True)
                    nc.tensor.matmul(ctx[:, 0:CTX], g.mask(K_BO), sq[:, b, S_CTX], start=True, stop=True).then_inc(s["sums"], 1)

                pe.wait_ge(s["const"], 32)
                with pe.Fori(0, NQK // 2) as i:
                    for b in range(2):
                        sums(i, b, b)
                        pe.wait_ge(s["normed"], at(i, 2, b + 1))
                        lat, ctx = sw[b]
                        nc.tensor.matmul(lat[:, :], perm[:, :], qb[:, b, S_LAT], start=True, stop=True)
                        nc.tensor.matmul(ctx[:, 0:CTX], perm[:, :], qb[:, b, S_CTX], start=True, stop=True).then_inc(s["swapped"], 1)

            @block.vector
            def _(dve):
                dve.wait_ge(s["const"], 32)
                with dve.Fori(0, NQK // 2) as i:
                    link = Link(dve, s["link"], i, 6)
                    for b in range(2):
                        dve.wait_ge(s["root"], at(i, 2, b + 1))
                        link(nc.vector.reciprocal(rn[:, b, :], rn[:, b, :]))
                        nc.vector.scalar_tensor_tensor(qb[:, b, :], qb[:, b, :], gain[:, b, 0:1], rn[:, b, :], ALU.mult,
                                                       ALU.mult).then_inc(s["normed"], 1)
                        dve.wait_ge(s["normed"], at(i, 2, b + 1))
                        dve.wait_ge(s["stored"][b], at(i, 16, 16))
                        link(nc.vector.tensor_tensor(out[:, b, :], qb[:, b, :], tab[:, 0, :], ALU.mult))
                        dve.wait_ge(s["swapped"], at(i, 2, b + 2))
                        nc.vector.tensor_tensor(rn[:, b, S_LAT], sw[b][0][:, :], tab[:, 1, S_LAT], ALU.mult)
                        link(nc.vector.tensor_tensor(rn[:, b, S_CTX], sw[b][1][:, 0:CTX], tab[:, 1, S_CTX], ALU.mult))
                        nc.vector.tensor_tensor(out[:, b, :], out[:, b, :], rn[:, b, :], ALU.add).then_inc(s["done"], 1)
                    link.end()


def attention_heads(nc, g):
    normed_rotated(nc, g)
    SCALE = HD ** -0.5
    names = ["passed", "loaded", "v_ps", "v_out", "scores", "link", "negmax", "exps", "diag", "pt_ps", "pt_out", "o_ps",
             "o_out", "stored"]
    with buffers(nc) as (sb, banks), phase(nc, *names) as s:
        kt, vt, vtok = sb("kt", KEYS), sb("vt", T), sb("vtok", KTILES, HD)
        q4, o4 = sb("q4", GROUPS, T), sb("o4", GROUPS, T)
        pb, pt = sb("probs", 2, P + LAT), sb("probs_t", 2, QTILES, P)
        dg = sb("diag", 2, P)
        mx, rsum = sb("mx", TILES), sb("rsum", TILES)
        with ExitStack() as stack:
            sc = [stack.enter_context(nc.psum_tensor(unique("scores"), [P, 2, 512], F32)) for _ in range(2)]
            tp = stack.enter_context(nc.psum_tensor(unique("probs_t"), [P, 2, 512], F32))
            ob = [stack.enter_context(nc.psum_tensor(unique("ob"), [P, 512], F32)) for _ in range(2)]
            vb = ob[1]
            tiles = [(h, q) for h in range(GROUPS) for q in range(QTILES)]
            flat = lambda t: t[:, :, :].rearrange("p a b -> p (a b)")

            def keys_of(q):
                return (KT_LAT, range(0, KTILES - 1)) if q < QTILES - 1 else (KT_CTX, range(KTILES - 1, KTILES))

            with nc.Block() as block:

                @block.sync
                def _(sp):
                    sp.sem_inc(s["stored"], 16)
                    with sp.Fori(0, AT_KV) as i:
                        wait_alone(sp, s["stored"], at(i, 16, 16), s["passed"])
                        sp.dma_start(kt[0:HD, 0:P], slab(g.d["cache_kt"], i)).then_inc(s["loaded"], 16)
                        sp.dma_start(kt[0:HD, P:KEYS], slab(g.d["qk_rot_heads"], i + AT_HEADS)).then_inc(s["loaded"], 16)
                        sp.dma_start(vt[0:HD, :], slab(g.d["qkv_heads"], i + (AT_HEADS + AT_KV))).then_inc(s["loaded"], 16)
                        sp.dma_start(vtok[:, 0, :], slab(g.d["cache_v_tok"], i)).then_inc(s["loaded"], 16)
                        sp.dma_start(q4[0:HD, :, :], g.d["qk_rot_heads"][bass.ds(i * GROUPS, GROUPS)]
                                     .rearrange("h c t -> c h t")).then_inc(s["loaded"], 16)
                        wait_alone(sp, s["o_out"], at(i, TILES, TILES), s["passed"])
                        sp.dma_start(g.d["mixed_heads"][bass.ds(i * GROUPS, GROUPS)].rearrange("h c t -> c h t"),
                                     o4[0:HD, :, :]).then_inc(s["stored"], 16)
                    sp.wait_ge(s["stored"], 16 * (AT_KV + 1))

                @block.tensor
                def _(pe):
                    def scores(i, n):
                        h, q = tiles[n]
                        cols, _ = keys_of(q)
                        if n >= 2:
                            pe.wait_ge(s["exps"], at(i, TILES, n - 1))
                        qs = q4[0:HD, h, q * P:(q + 1) * P]
                        out = sc[n % 2]
                        if q < QTILES - 1:
                            nc.tensor.matmul(out[:, 0, :], qs, kt[0:HD, 0:512], start=True, stop=True)
                            nc.tensor.matmul(out[:, 1, 0:P], qs, kt[0:HD, 512:P + LAT], start=True,
                                             stop=True).then_inc(s["scores"], 1)
                        else:
                            nc.tensor.matmul(out[:, 0, 0:P], qs, kt[0:HD, cols], start=True, stop=True).then_inc(s["scores"], 1)

                    with pe.Fori(0, AT_KV) as i:
                        wait_alone(pe, s["loaded"], at(i, 80, 80), s["passed"])
                        for n in range(QTILES):
                            last = nc.tensor.transpose(vb[:, n * HD:(n + 1) * HD], vt[0:HD, n * P:(n + 1) * P],
                                                       g.const[0:HD, K_ID:K_ID + HD])
                        last.then_inc(s["v_ps"], 1)
                        def values(n):
                            _, kts = keys_of(tiles[n][1])
                            pe.wait_ge(s["pt_out"], at(i, TILES, n + 1))
                            if n == 0:
                                pe.wait_ge(s["v_out"], at(i, 1, 1))
                            elif n >= 2:
                                pe.wait_ge(s["o_out"], at(i, TILES, n - 1))
                            for m, key in enumerate(kts):
                                last = nc.tensor.matmul(ob[n % 2][0:HD, 0:P], vtok[:, key, :], pt[:, n % 2, m, :],
                                                        start=(m == 0), stop=(m == len(kts) - 1))
                            last.then_inc(s["o_ps"], 1)

                        scores(i, 0)
                        for n, (h, q) in enumerate(tiles):
                            if n + 1 < TILES:
                                scores(i, n + 1)
                            if n >= 1:
                                values(n - 1)
                            pe.wait_ge(s["diag"], at(i, TILES, n + 1))
                            _, kts = keys_of(q)
                            for m in range(len(kts)):
                                last = nc.tensor.matmul(flat(tp)[:, m * P:(m + 1) * P], pb[:, n % 2, m * P:(m + 1) * P],
                                                        dg[:, n % 2, :], start=True, stop=True)
                            last.then_inc(s["pt_ps"], 1)
                        values(TILES - 1)

                @block.scalar
                def _(act):
                    with act.Fori(0, AT_KV) as i:
                        act.wait_ge(s["v_ps"], at(i, 1, 1))
                        nc.scalar.copy(vtok[:, 1:KTILES, :].rearrange("p k c -> p (k c)"),
                                       vb[:, 0:QTILES * HD]).then_inc(s["v_out"], 1)

                        def transposed_out(n):
                            width = P * len(keys_of(tiles[n][1])[1])
                            act.wait_ge(s["pt_ps"], at(i, TILES, n + 1))
                            if n >= 2:
                                act.wait_ge(s["o_ps"], at(i, TILES, n - 1))
                            nc.scalar.copy(pt[:, n % 2, :, :].rearrange("p a b -> p (a b)")[:, 0:width],
                                           flat(tp)[:, 0:width]).then_inc(s["pt_out"], 1)

                        for n, (h, q) in enumerate(tiles):
                            width = P * len(keys_of(q)[1])
                            act.wait_ge(s["negmax"], at(i, TILES, n + 1))
                            if n >= 2:
                                act.wait_ge(s["pt_ps"], at(i, TILES, n - 1))
                            nc.scalar.activation(pb[:, n % 2, 0:width], flat(sc[n % 2])[:, 0:width], ACT.Exp, scale=SCALE,
                                                 bias=mx[:, n:n + 1], accum_out=rsum[:, n:n + 1]).then_inc(s["exps"], 1)
                            if n >= 1:
                                transposed_out(n - 1)
                        transposed_out(TILES - 1)

                @block.vector
                def _(dve):
                    with dve.Fori(0, AT_KV) as i:
                        link = Link(dve, s["link"], i, 2 * TILES)

                        def maximum(n):
                            width = P * len(keys_of(tiles[n][1])[1])
                            dve.wait_ge(s["scores"], at(i, TILES, n + 1))
                            link(nc.vector.reduce_max(mx[:, n:n + 1], flat(sc[n % 2])[:, 0:width], AX.X))
                            nc.vector.tensor_scalar(mx[:, n:n + 1], mx[:, n:n + 1], -SCALE, None, ALU.mult).then_inc(s["negmax"], 1)

                        def output(n):
                            hn, qn = tiles[n]
                            dve.wait_ge(s["o_ps"], at(i, TILES, n + 1))
                            nc.vector.tensor_copy(o4[0:HD, hn, qn * P:(qn + 1) * P], ob[n % 2][0:HD, 0:P]).then_inc(s["o_out"], 1)

                        maximum(0)
                        for n in range(TILES):
                            if n + 1 < TILES:
                                maximum(n + 1)
                            dve.wait_ge(s["exps"], at(i, TILES, n + 1))
                            link(nc.vector.reciprocal(rsum[:, n:n + 1], rsum[:, n:n + 1]))
                            if n >= 2:
                                dve.wait_ge(s["pt_ps"], at(i, TILES, n - 1))
                            nc.vector.tensor_scalar(dg[:, n % 2, :], g.ident, rsum[:, n:n + 1], None, ALU.mult).then_inc(s["diag"], 1)
                            if n >= 2:
                                output(n - 2)
                        output(TILES - 2)
                        output(TILES - 1)
                        link.end()



R_G, R_EG, R_B, R_EL = 0, TT, 2 * TT, 3 * TT
R_END = 3 * TT + 2 * NCHUNK
C_G, C_NBEG, C_B, C_ED = 0, NCHUNK, 2 * NCHUNK, 3 * NCHUNK
C_END = 4 * NCHUNK
N_COLS = 10


def delta_gates(nc, g):
    names = ["passed", "w_loaded", "mm_done", "out", "raw_stored", "raw_loaded", "link", "exps", "rate", "sums", "decays", "scaled",
             "cols_ps", "cols_out", "stored"]
    H8 = slice(0, DN_HEADS)
    with buffers(nc) as (sb, banks), phase(nc, *names) as s:
        wg, raw, small = sb("wg", NB, 4 * DN_HEADS), sb("raw", T), sb("small", 4)
        ab = sb("ab", 2, 2, T)
        tmp = sb("tmp", 2, T)
        rows = sb("rows", R_END)
        nb, ed = sb("neg_beta_decay", TT), sb("to_end", TT)
        cols = sb("cols", DN_HEADS, C_END)
        rate = sb("rate", 2)
        bank = banks(4)
        pairs = lambda r0: rows[H8, r0:r0 + TT].rearrange("p (u e c) -> p u e c", u=NCHUNK, e=2)
        with nc.Block() as block:

            @block.sync
            def _(sp):
                sp.dma_start(wg[:, :, :].rearrange("p k n -> p (k n)"), g.d["dn_wgate"]).then_inc(s["w_loaded"], 16)
                sp.dma_start(small[H8, :], g.d["dn_small"]).then_inc(s["w_loaded"], 16)
                sp.wait_ge(s["out"], 1)
                sp.dma_start(g.d["dn_gates"].rearrange("a e h t -> (a e h) t"), raw[0:4 * DN_HEADS, :]).then_inc(s["raw_stored"], 16)
                sp.wait_ge(s["raw_stored"], 16)
                for a in range(2):
                    sp.dma_start(ab[H8, a, :, :], g.d["dn_gates"][a].rearrange("e h t -> h e t")).then_inc(s["raw_loaded"], 16)
                sp.wait_ge(s["cols_out"], 8)
                for h in range(DN_HEADS):
                    sp.dma_start(g.d["dn_cols"][h], cols[:, h, :]).then_inc(s["stored"], 16)
                sp.dma_start(g.d["dn_rows"], rows[H8, :]).then_inc(s["stored"], 16)
                sp.wait_ge(s["stored"], 16 * (DN_HEADS + 1))

            @block.tensor
            def _(pe):
                pe.wait_ge(s["w_loaded"], 32)
                for k in range(NB):
                    nc.tensor.matmul(bank[0][0:4 * DN_HEADS, :], wg[:, k, :], g.h[:, k, H_LAT], start=(k == 0), stop=(k == NB - 1))
                    last = nc.tensor.matmul(bank[1][0:4 * DN_HEADS, 0:CTX], wg[:, k, :], g.h[:, k, H_CTX],
                                            start=(k == 0), stop=(k == NB - 1))
                last.then_inc(s["mm_done"], 1)
                pe.wait_ge(s["scaled"], 4)
                for n, src in enumerate((rows[H8, R_G:R_G + TT], nb[H8, :], rows[H8, R_B:R_B + TT], ed[H8, :])):
                    if n >= 1:
                        pe.wait_ge(s["cols_out"], 2 * n)
                    for u in range(NCHUNK):
                        last = nc.tensor.transpose(bank[2 + n % 2][:, u * DN_HEADS:(u + 1) * DN_HEADS], src[:, u * P:(u + 1) * P],
                                                   g.ident[H8, H8])
                    last.then_inc(s["cols_ps"], 1)

            @block.scalar
            def _(act):
                act.wait_ge(s["mm_done"], 1)
                nc.scalar.copy(raw[0:4 * DN_HEADS, S_LAT], bank[0][0:4 * DN_HEADS, :])
                nc.scalar.copy(raw[0:4 * DN_HEADS, S_CTX], bank[1][0:4 * DN_HEADS, 0:CTX]).then_inc(s["out"], 1)
                act.wait_ge(s["rate"], 1)
                nc.scalar.activation(tmp[H8, :, :], tmp[H8, :, :], ACT.Exp, scale=-1.0).then_inc(s["exps"], 1)
                nc.scalar.activation(rate[H8, :], small[H8, 0:2], ACT.Exp).then_inc(s["exps"], 1)
                act.wait_ge(s["exps"], 1)
                nc.scalar.activation(tmp[H8, :, :], tmp[H8, :, :], ACT.Ln, bias=g.const[H8, K_ONE:K_ONE + 1]).then_inc(s["exps"], 1)
                nc.scalar.activation(ab[H8, 1, :, :], ab[H8, 1, :, :], ACT.Sigmoid).then_inc(s["exps"], 1)
                act.wait_ge(s["sums"], 1)
                nc.scalar.activation(rows[H8, R_EG:R_EG + TT], rows[H8, R_G:R_G + TT], ACT.Exp).then_inc(s["decays"], 1)
                nc.scalar.activation(rows[H8, R_EL:R_END].rearrange("p (u e) -> p u e", e=2), pairs(R_G)[:, :, :, C - 1],
                                     ACT.Exp).then_inc(s["decays"], 1)
                act.wait_ge(s["sums"], 2)
                nc.scalar.activation(ed[H8, :], ed[H8, :], ACT.Exp).then_inc(s["scaled"], 1)
                for n in range(4):
                    act.wait_ge(s["cols_ps"], n + 1)
                    nc.scalar.copy(cols[:, :, n * NCHUNK:(n + 1) * NCHUNK].rearrange("p h u -> p u h"),
                                   bank[2 + n % 2][:, 0:NCHUNK * DN_HEADS].rearrange("p (u h) -> p u h", h=DN_HEADS)).then_inc(s["cols_out"], 2)

            @block.vector
            def _(dve):
                link = Link(dve, s["link"])
                dve.wait_ge(s["raw_loaded"], 32)
                dve.wait_ge(s["w_loaded"], 32)
                for e in range(2):
                    last = nc.vector.tensor_scalar(ab[H8, 0, e, :], ab[H8, 0, e, :], small[H8, 2 + e:3 + e], None, ALU.add)
                link(last)
                link(nc.vector.tensor_scalar(tmp[H8, :, :], ab[H8, 0, :, :], -1.0, None, ALU.mult))
                nc.vector.tensor_tensor(tmp[H8, :, :], tmp[H8, :, :], ab[H8, 0, :, :], ALU.max).then_inc(s["rate"], 1)
                dve.wait_ge(s["exps"], 4)
                link(nc.vector.scalar_tensor_tensor(ab[H8, 0, :, :], ab[H8, 0, :, :], 0.0, tmp[H8, :, :], ALU.max, ALU.add))
                for e in range(2):
                    last = nc.vector.tensor_scalar(ab[H8, 0, e, :], ab[H8, 0, e, :], rate[H8, e:e + 1], -1.0, ALU.mult, ALU.mult)
                link(last)
                flat_nb = nb[H8, :].rearrange("p (u e c) -> p u e c", u=NCHUNK, e=2)
                for a, out in ((0, flat_nb), (1, pairs(R_B))):
                    for us, ts in ((slice(0, NLAT), S_LAT), (slice(NLAT, NCHUNK), S_CTX)):
                        nc.vector.tensor_copy(out[:, us, 0, :], chunked(ab[H8, a, 0, ts]))
                        last = nc.vector.tensor_copy(out[:, us, 1, :], chunked(ab[H8, a, 1, ts][:, ::-1]))
                link(last)
                nc.vector.tensor_tensor_scan(rows[H8, R_G:R_G + TT], g.const[H8, K_SCAN:K_SCAN + TT], nb[H8, :], 0.0,
                                             ALU.mult, ALU.add).then_inc(s["sums"], 1)
                dve.wait_ge(s["sums"], 1)
                nc.vector.tensor_tensor(ed[H8, :].rearrange("p (n c) -> p n c", c=C),
                                        rows[H8, R_G:R_G + TT].rearrange("p (n c) -> p n c", c=C)[:, :, C - 1:C]
                                        .to_broadcast([DN_HEADS, 2 * NCHUNK, C]),
                                        rows[H8, R_G:R_G + TT].rearrange("p (n c) -> p n c", c=C), ALU.subtract).then_inc(s["sums"], 1)
                dve.wait_ge(s["decays"], 2)
                nc.vector.scalar_tensor_tensor(nb[H8, :], rows[H8, R_EG:R_EG + TT], -1.0, rows[H8, R_B:R_B + TT],
                                               ALU.mult, ALU.mult).then_inc(s["scaled"], 3)


def delta_heads(nc, g):
    D_SCALE = P ** -0.5
    names = ["passed", "taps_loaded", "x_loaded", "r_loaded", "c_loaded", "z_loaded", "taps", "silu", "conv_v", "link_p", "link", "conv", "conv_sig", "link_a", "first", "squares", "sums", "root", "operands", "differ", "decay",
             "prepared", "masks", "products", "masked", "tokens", "tokens_out", "chain_y", "tmp_out", "chain_v", "v_out",
             "chain_s", "s_out", "o_ps", "o_out", "state_stored", "y_squares", "y_sums", "y_root", "z_sig", "y_ready",
             "y_stored"] + INVERSE_SEMS
    with buffers(nc) as (sb, banks), phase(nc, *names) as s:
        w = Work()
        xin, cv, cs, z = sb("xin", 3, HW), sb("cv", 3, HW), sb("cs", 3, T), sb("z", 2, T)
        rows, el, hcols, fcols = sb("rows", 3 * TT), sb("el", 2, 2 * NCHUNK), sb("hcols", 2, C_END), sb("fcols", 2, N_COLS)
        taps = sb("taps", DN_HEADS // 2, 2 * N_COLS)
        k2, q2, qd, ve = (sb(n, 2, NCHUNK, P) for n in ("k2", "q2", "qd", "ve"))
        dm, di = sb("dm", 2, NCHUNK, P), sb("di", 2, NCHUNK, P)
        w.lt, w.xx, w.y = sb("lt", GROUP, P), sb("xx", 2, 2, 2, P), sb("y", 2, 2, P)
        w.tt, qk = sb("tt", 2 * NCHUNK, P), sb("qk", 2 * NCHUNK, P)
        sq, rn = sb("sq", 2, T), sb("rn", 2, T)
        tmp, vn, st = sb("tmp", 2, P), sb("vn", 2, P), sb("state", 2, 2, P)
        spare = g.h[:, :, :].rearrange("p b t -> p (b t)")
        kdec = spare[:, 0:2 * TT].rearrange("p (n c) -> p n c", c=P)
        vtok = spare[:, 2 * TT:4 * TT].rearrange("p (n c) -> p n c", c=P)
        os_ = ve
        bank = banks(8)
        w.y_bank, w.x_bank = bank[2:4], bank[6:8]
        split = lambda buf, hh: buf[:, hh, :, :].rearrange("p u (e c) -> p u e c", e=2)
        row = lambda r0: rows[:, r0:r0 + TT].rearrange("p (u n) -> p u n", n=P)
        NI = DN_HEADS // 2
        with nc.Block() as block:

            @block.sync
            def _(sp):
                def load_x(n, hh):
                    for m in range(3):
                        blk = n * 2 + (m * NB + hh)
                        sp.dma_start(xin[:, m, H_LAT], slab(g.d["dn_lat"], blk)).then_inc(s["x_loaded"], 16)
                        sp.dma_start(xin[:, m, H_CTX], slab(g.d["dn_ctx"], blk)).then_inc(s["x_loaded"], 16)

                def load_rows(n, hh):
                    sp.dma_start(rows[:, :], g.d["dn_rows"][bass.ds(n * 2 + hh, 1), 0:3 * TT].to_broadcast([P, 3 * TT])
                                 ).then_inc(s["r_loaded"], 16)

                def load_columns(n):
                    for hh in range(2):
                        sp.dma_start(el[:, hh, :], g.d["dn_rows"][bass.ds(n * 2 + hh, 1), R_EL:R_END].to_broadcast([P, 2 * NCHUNK])
                                     ).then_inc(s["c_loaded"], 16)
                        sp.dma_start(hcols[:, hh, :], slab(g.d["dn_cols"], n * 2 + hh)).then_inc(s["c_loaded"], 16)

                def heads_pass(i, more):
                    wait_alone(sp, s["silu"], at(i, 2, 1), s["passed"])
                    load_x(i, 1)
                    wait_alone(sp, s["y_ready"], at(i, 2, 1), s["passed"])
                    for hh in range(2):
                        sp.dma_start(z[:, hh, :], slab(g.d["dn_proj"], i * 2 + (3 * NB + hh))).then_inc(s["z_loaded"], 16)
                    wait_alone(sp, s["prepared"], at(i, 2, 1), s["passed"])
                    wait_alone(sp, s["masks"], at(i, 4, 2), s["passed"])
                    load_rows(i, 1)
                    if more:
                        wait_alone(sp, s["silu"], at(i, 2, 2), s["passed"])
                        load_x(i + 1, 0)
                        wait_alone(sp, s["prepared"], at(i, 2, 2), s["passed"])
                        wait_alone(sp, s["masks"], at(i, 4, 4), s["passed"])
                        load_rows(i + 1, 0)
                    wait_alone(sp, s["s_out"], at(i, STEPS + 2, 3), s["passed"])
                    sp.dma_start(slab(g.d["dn_state_out"], i), st[:, :, :, :].rearrange("p h e v -> p (h e v)")
                                 ).then_inc(s["state_stored"], 16)
                    wait_alone(sp, s["state_stored"], at(i, 32, 16), s["passed"])
                    sp.dma_start(st[:, :, :, :].rearrange("p h e v -> p (h e v)"), slab(g.d["dn_state"], i)
                                 ).then_inc(s["state_stored"], 16)
                    if more:
                        wait_alone(sp, s["s_out"], at(i, STEPS + 2, STEPS + 2), s["passed"])
                        load_columns(i + 1)
                    for hh in range(2):
                        wait_alone(sp, s["y_ready"], at(i, 2, hh + 2), s["passed"])
                        sp.dma_start(slab(g.d["mixed"], i * 2 + hh), cs[:, hh, :]).then_inc(s["y_stored"], 16)

                sp.sem_inc(s["y_stored"], 32)
                sp.dma_start(taps[:, :, :], g.d["dn_head"].rearrange("i p n -> p i n")).then_inc(s["taps_loaded"], 16)
                load_x(0, 0)
                load_rows(0, 0)
                load_columns(0)
                with sp.Fori(0, NI - 1) as i:
                    heads_pass(i, True)
                heads_pass(NI - 1, False)
                sp.wait_ge(s["state_stored"], 32 * NI)
                sp.wait_ge(s["y_stored"], 32 * (NI + 1))

            @block.gpsimd
            def _(pool):
                with pool.Fori(0, NI) as i:
                    for hh in range(2):
                        wait_alone(pool, s["x_loaded"], at(i, 192, 96 * (hh + 1)), s["passed"])
                        wait_alone(pool, s["taps"], at(i, 1, 1), s["passed"])
                        if hh == 0:
                            wait_alone(pool, s["y_ready"], at(i, 2, 1), s["passed"])
                        else:
                            wait_alone(pool, s["silu"], at(i, 2, 1), s["passed"])
                        part = flat4(dm[:, hh])[:, 0:HW - 2]
                        out = cv[:, 2, 1:HW - 1]
                        nc.gpsimd.tensor_scalar(out, xin[:, 2, 0:HW - 2], fcols[:, hh, 6:7], None, ALU.mult).then_inc(s["link_p"], 1)
                        for tap in range(1, 3):
                            if tap == 2:
                                wait_alone(pool, s["link_p"], at(i, 8, 4 * hh + 3), s["passed"])
                            nc.gpsimd.tensor_scalar(part, xin[:, 2, tap:tap + HW - 2], fcols[:, hh, 6 + tap:7 + tap], None,
                                                    ALU.mult).then_inc(s["link_p"], 1)
                            wait_alone(pool, s["link_p"], at(i, 8, 4 * hh + 2 * tap), s["passed"])
                            nc.gpsimd.tensor_tensor(out, out, part, ALU.add).then_inc(s["link_p"] if tap == 1 else s["conv_v"], 1)
                        wait_alone(pool, s["decay"], at(i, 2, hh + 1), s["passed"])
                        nc.gpsimd.tensor_tensor(dm[:, hh], dm[:, hh], row(R_B), ALU.mult).then_inc(s["masks"], 1)
                        nc.gpsimd.tensor_tensor(di[:, hh], di[:, hh], g.mask(K_IP).unsqueeze(1).to_broadcast([P, NCHUNK, P]),
                                                ALU.mult).then_inc(s["masks"], 1)

            @block.tensor
            def _(pe):
                with pe.Fori(0, NI) as i:
                    for hh in range(2):
                        for n in range(2):
                            pe.wait_ge(s["squares"], at(i, 4, 2 * hh + n + 1))
                            nc.tensor.matmul(bank[2 * n][:, :], g.mask(K_ONE), sq[:, n, S_LAT], start=True, stop=True)
                            nc.tensor.matmul(bank[2 * n + 1][:, 0:CTX], g.mask(K_ONE), sq[:, n, S_CTX],
                                             start=True, stop=True).then_inc(s["sums"], 1)
                    pe.wait_ge(s["operands"], at(i, 2, 2))
                    for jg in range(NGROUP):
                        if jg >= 1:
                            pe.wait_ge(s["tokens_out"], at(i, NGROUP, jg))
                        units = [(2 * jg + n % 2, n // 2) for n in range(GROUP)]
                        for b, (left, right) in enumerate(((k2, k2), (k2, q2))):
                            for n, (u, hh) in enumerate(units):
                                last = nc.tensor.matmul(bank[b][:, n * P:(n + 1) * P], left[:, hh, u, :], right[:, hh, u, :],
                                                        start=True, stop=True)
                            last.then_inc(s["products"], 1)
                        for b, src in ((4, k2), (5, ve)):
                            for n, (u, hh) in enumerate(units):
                                last = nc.tensor.transpose(bank[b][:, n * P:(n + 1) * P], src[:, hh, u, :], g.ident)
                            last.then_inc(s["tokens"], 1)
                        pe.wait_ge(s["masked"], at(i, 4 * NGROUP, 4 * jg + 4))
                        if jg >= 1:
                            pe.wait_ge(s["inv_ready"], group_at(i, jg - 1, "inv_ready", 2))
                        invert_pe(pe, nc, g, s, w, i, jg)
                    pe.wait_ge(s["inv_ready"], group_at(i, NGROUP - 1, "inv_ready", 2))
                    pe.wait_ge(s["tokens_out"], at(i, NGROUP, NGROUP))
                    for n in range(STEPS):
                        u = ORDER[n]
                        if n == 2:
                            pe.wait_ge(s["state_stored"], at(i, 32, 32))
                        pe.wait_ge(s["s_out"], at(i, STEPS + 2, n + 1))
                        for hh in range(2):
                            last = nc.tensor.matmul(bank[0][:, hh * 2 * P:(hh + 1) * 2 * P], k2[:, hh, u, :],
                                                    st[:, hh, :, :].rearrange("p e v -> p (e v)"), start=True, stop=True)
                        last.then_inc(s["chain_y"], 1)
                        if n >= 2:
                            pe.wait_ge(s["o_out"], at(i, STEPS, n - 1))
                        ob = bank[4 + n % 2]
                        for hh in range(2):
                            for e in range(2):
                                nc.tensor.matmul(ob[:, hh * P + e * C:hh * P + (e + 1) * C], st[:, hh, e, :],
                                                 qd[:, hh, u, e * C:(e + 1) * C], start=(hh == 0 and e == 0), stop=False,
                                                 skip_group_check=True)
                        pe.wait_ge(s["tmp_out"], at(i, STEPS, n + 1))
                        for hh in range(2):
                            last = nc.tensor.matmul(bank[1][:, hh * P:(hh + 1) * P], w.tt[:, unit(u, hh), :], tmp[:, hh, :],
                                                    start=True, stop=True)
                        last.then_inc(s["chain_v"], 1)
                        pe.wait_ge(s["v_out"], at(i, STEPS, n + 1))
                        for e in range(2):
                            er = slice(C * e, C * (e + 1))
                            for hh in range(2):
                                last = nc.tensor.matmul(bank[2 + e][:, hh * P:(hh + 1) * P], kdec[er, unit(u, hh), :], vn[er, hh, :],
                                                        start=True, stop=True)
                            last.then_inc(s["chain_s"], 1)
                        for hh in range(2):
                            last = nc.tensor.matmul(ob[:, hh * P:(hh + 1) * P], vn[:, hh, :], qk[:, unit(u, hh), :], start=False,
                                                    stop=True, skip_group_check=True)
                        last.then_inc(s["o_ps"], 1)
                    for hh in range(2):
                        pe.wait_ge(s["y_squares"], at(i, 2, hh + 1))
                        nc.tensor.matmul(bank[6 - 6 * hh][:, :], g.mask(K_ONE), sq[:, hh, S_LAT], start=True, stop=True)
                        nc.tensor.matmul(bank[7 - 6 * hh][:, 0:CTX], g.mask(K_ONE), sq[:, hh, S_CTX],
                                         start=True, stop=True).then_inc(s["y_sums"], 1)

            @block.scalar
            def _(act):
                def root(n, done, lat, ctx, scale):
                    nc.scalar.activation(rn[:, n, S_LAT], lat[:, :], ACT.Sqrt, bias=g.eps_nrm, scale=scale)
                    nc.scalar.activation(rn[:, n, S_CTX], ctx[:, 0:CTX], ACT.Sqrt, bias=g.eps_nrm, scale=scale).then_inc(done, 1)

                with act.Fori(0, NI) as i:
                    for hh in range(2):
                        act.wait_ge(s["conv"], at(i, 2, hh + 1))
                        act.wait_ge(s["conv_v"], at(i, 2, hh + 1))
                        nc.scalar.activation(xin[:, :, 1:HW - 1], cv[:, :, 1:HW - 1], ACT.Sigmoid).then_inc(s["conv_sig"], 1)
                        for n in range(2):
                            act.wait_ge(s["sums"], at(i, 4, 2 * hh + n + 1))
                            root(n, s["root"], bank[2 * n], bank[2 * n + 1], 1.0)
                        act.wait_ge(s["differ"], at(i, 2, hh + 1))
                        nc.scalar.activation(di[:, hh], di[:, hh], ACT.Exp).then_inc(s["link_a"], 1)
                        act.wait_ge(s["link_a"], at(i, 2, hh + 1))
                        nc.scalar.copy(dm[:, hh], di[:, hh]).then_inc(s["decay"], 1)
                    for jg in range(NGROUP):
                        act.wait_ge(s["tokens"], at(i, 2 * NGROUP, 2 * jg + 2))
                        for n in range(GROUP):
                            u, hh = 2 * jg + n % 2, n // 2
                            nc.scalar.activation(kdec[:, GROUP * jg + n, :], bank[4][:, n * P:(n + 1) * P], ACT.Identity,
                                                 scale=hcols[:, hh, C_ED + u:C_ED + u + 1])
                            last = nc.scalar.activation(vtok[:, GROUP * jg + n, :], bank[5][:, n * P:(n + 1) * P], ACT.Identity,
                                                        scale=hcols[:, hh, C_B + u:C_B + u + 1])
                        last.then_inc(s["tokens_out"], 1)
                    for n in range(STEPS):
                        act.wait_ge(s["o_ps"], at(i, STEPS, n + 1))
                        nc.scalar.copy(os_[:, :, ORDER[n], :], bank[4 + n % 2][:, 0:2 * P].rearrange("p (h n) -> p h n", h=2)
                                       ).then_inc(s["o_out"], 1)
                    act.wait_ge(s["z_loaded"], at(i, 32, 32))
                    nc.scalar.activation(cv[:, 0:2, 0:T], z[:, :, :], ACT.Sigmoid).then_inc(s["z_sig"], 1)
                    for hh in range(2):
                        act.wait_ge(s["y_sums"], at(i, 2, hh + 1))
                        root(hh, s["y_root"], bank[6 - 6 * hh], bank[7 - 6 * hh], 1.0 / P)

            @block.vector
            def _(dve):
                link0 = Link(dve, s["first"])
                for edge in (slice(0, 1), slice(H_LAT.stop, H_CTX.start), slice(H_CTX.stop, HW)):
                    link0(nc.vector.memset(xin[:, :, edge], 0.0))
                dve.wait_ge(s["taps_loaded"], 16)
                dve.sem_inc(s["y_ready"], 1)
                with dve.Fori(0, NI) as i:
                    link = Link(dve, s["link"], i, LINKS_DN)
                    dve.wait_ge(s["y_ready"], at(i, 2, 1))
                    nc.vector.tensor_copy(fcols[:, :, :].rearrange("p h n -> p (h n)"),
                                          taps[:, bass.ds(i, 1), :].rearrange("p a n -> p (a n)")).then_inc(s["taps"], 1)
                    dve.wait_ge(s["taps"], at(i, 1, 1))
                    for hh in range(2):
                        dve.wait_ge(s["x_loaded"], at(i, 192, 96 * (hh + 1)))
                        for tap in range(3):
                            for n in range(2):
                                f = fcols[:, hh, 3 * n + tap:3 * n + tap + 1]
                                src, out = xin[:, n, tap:tap + HW - 2], cv[:, n, 1:HW - 1]
                                last = (nc.vector.tensor_scalar(out, src, f, None, ALU.mult) if tap == 0 else
                                        nc.vector.scalar_tensor_tensor(out, src, f, out, ALU.mult, ALU.add))
                            if tap < 2:
                                link(last)
                        last.then_inc(s["conv"], 1)
                        dve.wait_ge(s["conv_sig"], at(i, 2, hh + 1))
                        if hh == 0:
                            dve.wait_ge(s["y_stored"], at(i, 32, 32))
                        for hs, cols in ((H_LAT, S_LAT), (H_CTX, S_CTX)):
                            last = nc.vector.tensor_tensor(cs[:, :, cols], cv[:, :, hs], xin[:, :, hs], ALU.mult)
                        link(last)
                        for edge in (slice(0, 1), slice(H_LAT.stop, H_CTX.start), slice(H_CTX.stop, HW)):
                            last = nc.vector.memset(xin[:, :, edge], 0.0)
                        last.then_inc(s["silu"], 1)
                        for n in range(2):
                            nc.vector.tensor_tensor(sq[:, n, :], cs[:, n, :], cs[:, n, :], ALU.mult).then_inc(s["squares"], 1)
                        dve.wait_ge(s["c_loaded"], at(i, 64, 64))
                        dve.wait_ge(s["r_loaded"], at(i, 32, 16 * (hh + 1)))
                        link(nc.vector.tensor_tensor(di[:, hh], row(R_G), hcols[:, hh, C_G:C_G + NCHUNK].unsqueeze(2)
                                                     .to_broadcast([P, NCHUNK, P]), ALU.subtract))
                        nc.vector.tensor_scalar(di[:, hh], di[:, hh], 0.0, None, ALU.min).then_inc(s["differ"], 1)
                        for n, scale in ((0, D_SCALE), (1, 1.0)):
                            dve.wait_ge(s["root"], at(i, 4, 2 * hh + n + 1))
                            link(nc.vector.reciprocal(rn[:, n, :], rn[:, n, :]))
                            last = nc.vector.scalar_tensor_tensor(cs[:, n, :], cs[:, n, :], scale, rn[:, n, :], ALU.mult, ALU.mult)
                        link(last)
                        for n, buf in enumerate((q2, k2, ve)):
                            for both, plain in by_direction(split(buf, hh), cs[:, n, :]):
                                last = nc.vector.tensor_copy(both, plain)
                        link(last)
                        nc.vector.tensor_tensor(qd[:, hh], q2[:, hh], row(R_EG), ALU.mult).then_inc(s["prepared"], 1)
                        dve.wait_ge(s["prepared"], at(i, 2, hh + 1))
                        dve.wait_ge(s["masks"], at(i, 4, 2 * hh + 2))
                        nc.vector.scalar_tensor_tensor(dm[:, hh], dm[:, hh], -1.0, g.mask(K_SP).unsqueeze(1).to_broadcast([P, NCHUNK, P]),
                                                       ALU.mult, ALU.mult).then_inc(s["operands"], 1)
                    nc.vector.memset(st[:, :, :, :], 0.0).then_inc(s["s_out"], 1)
                    dve.wait_ge(s["operands"], at(i, 2, 2))
                    for jg in range(NGROUP):
                        for b, (mask, out) in enumerate(((dm, w.lt[:, :, :]), (di, qk[:, GROUP * jg:GROUP * (jg + 1), :]))):
                            dve.wait_ge(s["products"], at(i, 2 * NGROUP, 2 * jg + b + 1))
                            for hh in range(2):
                                nc.vector.tensor_tensor(out[:, 2 * hh:2 * hh + 2, :],
                                                        bank[b][:, 2 * hh * P:2 * (hh + 1) * P].rearrange("p (n c) -> p n c", n=2),
                                                        mask[:, hh, 2 * jg:2 * jg + 2, :], ALU.mult).then_inc(s["masked"], 1)
                        dve.wait_ge(s["masked"], at(i, 4 * NGROUP, 4 * jg + 4))
                        invert_dve(dve, nc, g, s, w, i, jg, link)
                    dve.wait_ge(s["tokens_out"], at(i, NGROUP, NGROUP))
                    for n in range(STEPS):
                        u = ORDER[n]
                        dve.wait_ge(s["chain_y"], at(i, STEPS, n + 1))
                        for hh in range(2):
                            for e in range(2):
                                er = slice(C * e, C * (e + 1))
                                last = nc.vector.scalar_tensor_tensor(
                                    tmp[er, hh, :], bank[0][er, (2 * hh + e) * P:(2 * hh + e + 1) * P],
                                    hcols[er, hh, C_NBEG + u:C_NBEG + u + 1], vtok[er, unit(u, hh), :], ALU.mult, ALU.add)
                        last.then_inc(s["tmp_out"], 1)
                        dve.wait_ge(s["chain_v"], at(i, STEPS, n + 1))
                        if n >= 1:
                            dve.wait_ge(s["o_ps"], at(i, STEPS, n))
                        nc.vector.tensor_copy(vn[:, :, :].rearrange("p h v -> p (h v)"), bank[1][:, 0:2 * P]).then_inc(s["v_out"], 1)
                        if n == 2:
                            dve.wait_ge(s["state_stored"], at(i, 32, 32))
                        for e in range(2):
                            dve.wait_ge(s["chain_s"], at(i, 2 * STEPS, 2 * n + e + 1))
                            for hh in range(2):
                                last = nc.vector.scalar_tensor_tensor(
                                    st[:, hh, e, :], st[:, hh, e, :], el[:, hh, 2 * u + e:2 * u + e + 1],
                                    bank[2 + e][:, hh * P:(hh + 1) * P], ALU.mult, ALU.add)
                        last.then_inc(s["s_out"], 1)
                        dve.wait_ge(s["s_out"], at(i, STEPS + 2, n + 2))
                    dve.sem_inc(s["s_out"], 1)
                    dve.wait_ge(s["o_out"], at(i, STEPS, STEPS))
                    for hh in range(2):
                        o4 = split(os_, hh)
                        out = chunked(cs[:, hh, :])
                        for us in (slice(0, NLAT), slice(NLAT, NCHUNK)):
                            last = nc.vector.tensor_tensor(out[:, us, :], o4[:, us, 0, :], o4[:, us, 1, :][:, ::-1, ::-1], ALU.add)
                    link(last)
                    for hh in range(2):
                        nc.vector.tensor_tensor(sq[:, hh, :], cs[:, hh, :], cs[:, hh, :], ALU.mult).then_inc(s["y_squares"], 1)
                    for hh in range(2):
                        dve.wait_ge(s["y_root"], at(i, 2, hh + 1))
                        link(nc.vector.reciprocal(rn[:, hh, :], rn[:, hh, :]))
                        link(nc.vector.scalar_tensor_tensor(cs[:, hh, :], cs[:, hh, :], fcols[:, hh, 9:10], rn[:, hh, :],
                                                            ALU.mult, ALU.mult))
                        dve.wait_ge(s["z_sig"], at(i, 1, 1))
                        link(nc.vector.tensor_tensor(cs[:, hh, :], cs[:, hh, :], z[:, hh, :], ALU.mult))
                        nc.vector.tensor_tensor(cs[:, hh, :], cs[:, hh, :], cv[:, hh, 0:T], ALU.mult).then_inc(s["y_ready"], 1)
                    link.end()


LINKS_DN = 2 * 6 + 2 * NGROUP + 1 + 2 * 3 + 4




class Global:

    def mask(self, col):
        return self.const[:, col:col + P]


def program(nc, d, layers=DEPTH):
    g = Global()
    g.d = d
    with buffers(nc) as (sb, _):
        g.x, g.const, g.vec = sb("x", NB, T), sb("const", K_END), sb("vec", V_END)
        g.mods = sb("mods", DEPTH * 6 * NB, 2)
        g.ident, g.mean_w = g.mask(K_ID), g.mask(K_MEAN)
        g.eps_ln, g.eps_gn, g.eps_nrm = (g.const[:, K_EPS + n:K_EPS + n + 1] for n in range(3))
        g.h = sb("h", NB, HW)
        with buffers(nc) as (sb2, _):
            g.bmod, g.cond, g.silu = sb2("bmod", DEPTH * 6 * NB), sb2("cond", NB, 2), sb2("silu", NB, 2)
            start(nc, g)
            modulation(nc, g)
        first_modulate(nc, g)
        for layer in range(layers):
            kind, j = layer % 3, layer // 3
            with buffers(nc) as (sb2, _):
                if kind == 0:
                    low = sb2("low", 3, T)
                    with buffers(nc) as (sb3, _):
                        g.xx = sb3("xx", NB, HW)
                        token_shift(nc, g)
                        low_rank(nc, g, j, low)
                        for n, m in enumerate((0, 2, 3)):
                            with buffers(nc) as (sb4, _):
                                xi = sb4("xi", NB, HW)
                                cols = lambda k, xi=xi: (xi[:, k, H_LAT], xi[:, k, H_CTX])
                                projection(nc, g, d["rw_wrkv"][(3 * j + n) * 4:(3 * j + n + 1) * 4], 4, 1, cols,
                                           out=d["rkv"][n * NB:(n + 1) * NB], mix=(xi, V_MU + (j * 6 + m) * NB))
                    rwkv_heads(nc, g, j, low)
                    wo = d["rw_wo"][4 * j:4 * j + 4]
                elif kind == 1:
                    projection(nc, g, d["at_wqkv"], 6, 1, h_cols(g), out=d["qkv"])
                    attention_heads(nc, g)
                    wo = d["at_wo"]
                else:
                    projection(nc, g, d["dn_win"], 16, 1, h_cols(g), out=d["dn_proj"])
                    delta_gates(nc, g)
                    delta_heads(nc, g)
                    wo = d["dn_wo"]
            with buffers(nc) as (sb2, _):
                mixed = sb2("mixed", NB, T)
                projection(nc, g, wo, 4, 1, plain_cols(mixed), out=d["delta"], load=(mixed, d["mixed"]))
            norm(nc, g, d["delta"], layer, 0, mod_at(layer, 2), (mod_at(layer, 4), mod_at(layer, 3)))
            with buffers(nc) as (sb2, _):
                hidden = sb2("hidden", NFB, T)
                projection(nc, g, d["w_fc1"][layer * 16:layer * 16 + 16], 16, 1, h_cols(g), hidden=hidden)
                projection(nc, g, d["w_fc2"][layer * 16:layer * 16 + 16], 4, 4, plain_cols(hidden), out=d["delta"])
            nxt = (mod_at(layer + 1, 1), mod_at(layer + 1, 0)) if layer + 1 < layers else None
            norm(nc, g, d["delta"], layer, 1, mod_at(layer, 5), nxt)




def weight_slabs(w, per=2 * P):
    k, n = w.shape
    w = w.reshape(k // D, NB, P, n // per, per)
    return np.ascontiguousarray(w.transpose(3, 0, 2, 1, 4)).reshape(-1, P, NB * per)


def columns(v):
    v = v.reshape(-1, v.shape[-1] // P, P)
    return v.transpose(2, 0, 1).reshape(P, -1)


def transposed(x):
    return x.T.reshape(-1, P, x.shape[0])


def rwkv_layout(a):
    n_j = a["rw_wrkv"].shape[0]
    slabs = [weight_slabs(a["rw_wrkv"][j, n]) for j in range(n_j) for n in range(3)]
    low, head, state = [], [], []
    for j in range(n_j):
        for w in (a["rw_w1"][j], a["rw_a1"][j]):
            low.append(weight_slabs(w.transpose(1, 0, 2).reshape(D, P), P)[0])
        low.append(weight_slabs(a["rw_g1"][j], P)[0])
        mats = [m.reshape(P, D) for m in (a["rw_w2"][j], a["rw_a2"][j], a["rw_g2"][j])]
        cols = [a["rw_w0"][j, 0], a["rw_w0"][j, 1], a["rw_a0"][j, 0], a["rw_a0"][j, 1], a["rw_kk"][j],
                a["rw_ka"][j], a["rw_rk"][j].reshape(D), a["rw_gn_g"][j], a["rw_gn_b"][j]]
        for b in range(NB):
            f = slice(b * P, (b + 1) * P)
            head.append(np.concatenate([m[:, f] for m in mats] + [c[f][:, None] for c in cols], axis=1))
        st = a["state_rwkv"][0, j].transpose(1, 3, 0, 2).reshape(NB, P, 2 * C)
        state.append(st)
    return (np.concatenate(slabs), np.stack(low), np.stack(head), np.concatenate(state),
            np.concatenate([weight_slabs(a["rw_wo"][j]) for j in range(n_j)]))


def arrays_of(a):
    d = {}
    x = np.concatenate([a["x_sample"][0], a["x_prompt"][0]], axis=0)
    d["x_t"] = transposed(x)
    d["consts"] = constant_table()
    mu = [columns(a["rw_mu"][j]) for j in range(RW_LAYERS)]
    ln = np.stack([a["ln_g"], a["ln_b"]], axis=2)
    d["vectors"] = np.concatenate([columns(ln)] + mu, axis=1)
    d["b_mod_t"] = columns(a["b_mod"])
    cond = np.stack([a["c"][0], a["c_ctx"]], axis=0)
    d["cond_t"] = cond.reshape(2, NB, P).transpose(2, 1, 0)
    d["w_mod"] = np.concatenate([weight_slabs(w, 512) for w in a["w_mod"]])
    d["rw_wrkv"], d["rw_low"], d["rw_head"], d["rw_state"], d["rw_wo"] = rwkv_layout(a)
    d["w_fc1"] = np.concatenate([weight_slabs(w) for w in a["w_fc1"]])
    d["w_fc2"] = np.concatenate([weight_slabs(w) for w in a["w_fc2"]])
    attention_layout(a, d)
    delta_layout(a, d)
    return {n: np.ascontiguousarray(v) for n, v in d.items()}


def attention_layout(a, d):
    d["at_wqkv"] = weight_slabs(a["at_wqkv"][0])
    d["at_wo"] = weight_slabs(a["at_wo"][0])
    d["at_gain"] = np.stack([np.tile(a["at_qn"][0], 2)] * 8 + [np.tile(a["at_kn"][0], 2)] * 2)[:, :, None]
    d["cache_kt"] = a["cache_k"][0, 0].transpose(1, 2, 0)
    d["cache_v_tok"] = a["cache_v"][0, 0].transpose(1, 0, 2)
    d["rope_t"], d["rope_perm"] = rope_tables()


def delta_layout(a, d):
    w = a["dn_win"][0]
    gates = 4 * D
    d["dn_win"] = weight_slabs(w[:, :gates])
    d["dn_wgate"] = weight_slabs(w[:, gates:], 4 * DN_HEADS)[0]
    d["dn_wo"] = weight_slabs(a["dn_wo"][0])
    d["dn_small"] = np.concatenate([a["dn_alog"][0].T, a["dn_dtb"][0].T], axis=1)
    taps = a["dn_conv"][0].reshape(3, 3, DN_HEADS, P).transpose(2, 3, 1, 0).reshape(DN_HEADS, P, 9)
    gain = np.broadcast_to(a["dn_ng"][0][None, :, None], (DN_HEADS, P, 1))
    head = np.concatenate([taps, gain], axis=2).reshape(DN_HEADS // 2, 2, P, 10)
    d["dn_head"] = head.transpose(0, 2, 1, 3).reshape(DN_HEADS // 2, P, 20)
    st = a["state_delta"][0, 0].reshape(2, DN_HEADS // 2, 2, P, P)
    d["dn_state"] = st.transpose(1, 3, 2, 0, 4).reshape(DN_HEADS // 2, P, 4 * P)


def rope_tables():
    n_freq = HD // 4
    tok = np.arange(LAT)
    where = np.stack([tok // GRID_W, tok % GRID_W], axis=-1).astype(np.float32)
    inv = np.float32(10000.0) ** (-np.arange(n_freq, dtype=np.float32) / n_freq)
    ang = where[:, :, None] * inv
    tab = np.zeros((P, 2, T), np.float32)
    tab[:, 0, LAT:] = 1.0
    for p in range(P):
        ax, half, f = (p % HD) // (2 * n_freq), (p // n_freq) % 2, p % n_freq
        tab[p, 0, :LAT] = np.cos(ang[:, ax, f])
        tab[p, 1, :LAT] = np.sin(ang[:, ax, f]) * (1.0 if half else -1.0)
    perm = np.zeros((P, P), np.float32)
    perm[np.arange(P) ^ n_freq, np.arange(P)] = 1.0
    return tab, perm


SCRATCH = {"rkv": (3 * NB, P, T), "mixed": (NB, P, T), "delta": (NB, P, T), "qkv": (12, P, T), "qk_rot": (10, P, T),
           "dn_proj": (32, P, T), "dn_gates": (2, 2, DN_HEADS, T),
           "dn_rows": (DN_HEADS, R_END), "dn_cols": (DN_HEADS, P, C_END)}
OUTPUTS = {"y_out": (NB, P, T), "rw_state_out": (RW_LAYERS * NB, P, 2 * C), "kv_out": (4, P, CTX),
           "dn_state_out": (DN_HEADS // 2, P, 2 * 2 * P)}


def declare(nc, arrays):
    d = {}
    for name, a in arrays.items():
        d[name] = nc.dram_tensor(name, a.shape, F32, kind="ExternalInput").ap()
    for name, shape in OUTPUTS.items():
        d[name] = nc.dram_tensor(name, shape, F32, kind="ExternalOutput").ap()
    for name, shape in SCRATCH.items():
        d[name] = nc.dram_tensor(name, shape, F32).ap()
    for name in ("qk_rot", "qkv", "mixed"):
        d[name + "_heads"] = d[name].rearrange("b (h c) t -> (b h) c t", h=2)
    d["dn_lat"], d["dn_ctx"] = d["dn_proj"][:, :, S_LAT], d["dn_proj"][:, :, S_CTX]
    return d


def kernel(**inputs):
    import concourse.bacc as bacc
    from concourse.bass_utils import run_bass_kernel_spmd

    a = {n: np.asarray(v) for n, v in inputs.items()}
    arrays = arrays_of(a)
    nc = bacc.Bacc("TRN2", target_bir_lowering=False, num_devices=1)
    program(nc, declare(nc, arrays))
    r = run_bass_kernel_spmd(nc, [arrays], core_ids=[0]).results[0]
    y = r["y_out"].reshape(D, T).T
    rw = r["rw_state_out"].reshape(RW_LAYERS, RW_HEADS, C, 2, C).transpose(0, 3, 1, 4, 2)[None]
    kv = r["kv_out"].reshape(2, AT_KV, HD, CTX).transpose(0, 3, 1, 2)[:, None, None]
    dn = r["dn_state_out"].reshape(DN_HEADS // 2, P, 2, 2, P).transpose(3, 0, 2, 1, 4).reshape(2, DN_HEADS, P, P)
    out = (y[None, LAT:], y[None, :LAT], rw, kv[0], kv[1], dn[None, None])
    return tuple(np.ascontiguousarray(o) for o in out)
```

```python
from contextlib import ExitStack, contextmanager

import concourse.bass as bass
import numpy as np
from concourse import mybir

F32 = mybir.dt.float32
F32R = mybir.dt.float32r
ACT = mybir.ActivationFunctionType
ALU = mybir.AluOpType
AX = mybir.AxisListType

P = 128
D = 1024
DEPTH = 4
NB = D // P
LAT, CTX = 512, 128
T = LAT + CTX
FF = 4 * D
NFB = FF // P
GRID_W = 64
C = 64
ALPHA = (2.0 * DEPTH) ** 0.25
LN_EPS = 1e-5
GN_EPS = 64e-5
NRM_EPS = 1e-6
HALF_DECAY = float(np.exp(-0.5))
RW_LAYERS = 2
RW_HEADS, DN_HEADS = 16, 8
AT_HEADS, AT_KV, HD = 16, 4, 64

HW = T + 4
H_LAT = slice(1, 1 + LAT)
H_CTX = slice(2 + LAT, 2 + LAT + CTX)
S_LAT = slice(0, LAT)
S_CTX = slice(LAT, T)

TT = 2 * T
NCHUNK = T // C
NLAT = LAT // C
GROUP = 4
NGROUP = NCHUNK // 2
LEVELS = 5

K_ID, K_BO, K_ONE = 0, 128, 256
K_MEAN, K_SP, K_IP, K_L0 = 384, 512, 640, 768
K_LV = 896
K_SCAN = K_LV + LEVELS * P
K_EPS = K_SCAN + TT
K_END = K_EPS + 4

V_LN = 0
V_MU = V_LN + DEPTH * 2 * 2 * NB
V_END = V_MU + RW_LAYERS * 6 * NB


def constant_table():
    t = np.zeros((P, K_END), np.float32)
    r = np.arange(P)
    same = r[:, None] // C == r[None, :] // C
    row, col = r[:, None], r[None, :]
    t[:, K_ID:K_ID + P] = np.eye(P)
    t[:, K_BO:K_BO + P] = same
    t[:, K_ONE:K_ONE + P] = 1.0
    t[:, K_MEAN:K_MEAN + P] = 1.0 / D
    t[:, K_SP:K_SP + P] = same & (col > row)
    t[:, K_IP:K_IP + P] = same & (col >= row)
    t[:, K_L0:K_L0 + P] = (row // 2 == col // 2) & (col > row)
    for n in range(LEVELS):
        b = 2 << n
        at = K_LV + n * P
        t[:, at:at + P] = (row // (2 * b) == col // (2 * b)) & (row // b > col // b)
    t[:, K_SCAN:K_SCAN + TT] = np.arange(TT) % C != 0
    t[:, K_EPS], t[:, K_EPS + 1], t[:, K_EPS + 2] = LN_EPS, GN_EPS, NRM_EPS
    return t


def at(i, per, k):
    return i * per + k


def wait_alone(eng, sem, value, passed):
    eng.wait_ge(sem, value)
    eng.sem_inc(passed, 1)


class Link:

    def __init__(self, eng, sem, i=0, per=0):
        self.eng, self.sem, self.i, self.per, self.n = eng, sem, i, per, 0

    def __call__(self, ins):
        ins.then_inc(self.sem, 1)
        self.n += 1
        self.eng.wait_ge(self.sem, at(self.i, self.per, self.n))

    def end(self):
        assert self.n == self.per, f"the body has {self.n} links"


_count = [0]


def unique(name):
    _count[0] += 1
    return f"{name}_{_count[0]}"


@contextmanager
def phase(nc, *names):
    made, all_of = {}, []
    assert len(set(names)) == len(names)
    for name in names:
        key, _, n = name.partition(":")
        sems = [nc.alloc_semaphore(unique(f"{key}_{m}")) for m in range(int(n or 1))]
        made[key] = sems if n else sems[0]
        all_of += sems
    yield made
    nc.clear_and_free_semaphores(all_of)
    nc.all_engine_barrier()


@contextmanager
def buffers(nc):
    with ExitStack() as stack:
        count = [0]

        def sb(name, *shape, dt=F32):
            return stack.enter_context(nc.sbuf_tensor(unique(name), [P, *shape], dt))

        def banks(n):
            return [stack.enter_context(nc.psum_tensor(unique(f"bank{b}"), [P, 512], F32)) for b in range(n)]

        yield sb, banks


def slab(dram, n):
    return dram[bass.ds(n, 1)].rearrange("a p n -> p (a n)")


def blocks(dram):
    return dram.rearrange("b p t -> p b t")


def mod_at(layer, piece):
    return (layer * 6 + piece) * NB




def start(nc, g):
    with phase(nc, "loaded", "sig") as s, nc.Block() as block:

        @block.sync
        def _(sp):
            sp.dma_start(g.x[:, :, :], blocks(g.d["x_t"])).then_inc(s["loaded"], 16)
            sp.dma_start(g.const[:, :], g.d["consts"]).then_inc(s["loaded"], 16)
            sp.dma_start(g.vec[:, :], g.d["vectors"]).then_inc(s["loaded"], 16)
            sp.dma_start(g.bmod[:, :], g.d["b_mod_t"]).then_inc(s["loaded"], 16)
            sp.dma_start(g.cond[:, :, :], g.d["cond_t"]).then_inc(s["loaded"], 16)

        @block.scalar
        def _(act):
            act.wait_ge(s["loaded"], 80)
            nc.scalar.activation(g.silu[:, :, :], g.cond[:, :, :], ACT.Sigmoid).then_inc(s["sig"], 1)

        @block.vector
        def _(dve):
            dve.wait_ge(s["sig"], 1)
            nc.vector.tensor_tensor(g.silu[:, :, :], g.silu[:, :, :], g.cond[:, :, :], ALU.mult)


NS = 512
MOD_STEPS = 6 * D // NS
MOD_BLOCKS = NS // P


def scales_plus_one(nc, g, layers):
    for layer in layers:
        for piece in (1, 4):
            part = g.mods[:, mod_at(layer, piece):mod_at(layer, piece) + NB, :]
            nc.vector.tensor_scalar_add(part, part, 1.0)


def modulation(nc, g, layer):
    STEPS, first = MOD_STEPS, layer * MOD_STEPS
    with buffers(nc) as (sb, banks), phase(
            nc, "w_loaded:2", "rows_ready", "rows_copied", "cols_ready", "cols_added", "passed") as s:
        ring = sb("mod_ring", 2, NB, NS)
        rows = sb("mod_rows", 2, NS)
        bank = banks(4)
        with nc.Block() as block:

            @block.sync
            def _(sp):
                with sp.Fori(0, STEPS // 2) as i:
                    for b in range(2):
                        sp.wait_ge(s["rows_ready"], at(i, 2, b + 1))
                        sp.dma_start(ring[:, b].rearrange("p k n -> p (k n)"),
                                     slab(g.d["w_mod"], i * 2 + (first + b))).then_inc(s["w_loaded"][b], 16)

            @block.tensor
            def _(pe):
                pe.sem_inc(s["rows_ready"], 2)
                with pe.Fori(0, STEPS // 2) as i:
                    for b in range(2):
                        pe.wait_ge(s["w_loaded"][b], at(i, 16, 16))
                        pe.wait_ge(s["rows_copied"], at(i, 2, b + 1))
                        for k in range(NB):
                            last = nc.tensor.matmul(bank[b][0:2, 0:NS], g.silu[:, k, :], ring[:, b, k, :],
                                                    start=(k == 0), stop=(k == NB - 1))
                        last.then_inc(s["rows_ready"], 1)
                        pe.wait_ge(s["rows_copied"], at(i, 2, b + 3))
                        wait_alone(pe, s["cols_added"], at(i, 2, b + 1), s["passed"])
                        for n in range(NS // P):
                            last = nc.tensor.transpose(bank[2 + b][:, 2 * n:2 * n + 2], rows[0:2, b, n * P:(n + 1) * P],
                                                       g.ident[0:2, 0:2])
                        last.then_inc(s["cols_ready"], 1)

            @block.scalar
            def _(act):
                act.sem_inc(s["rows_copied"], 2)
                with act.Fori(0, STEPS // 2) as i:
                    for b in range(2):
                        act.wait_ge(s["rows_ready"], at(i, 2, b + 3))
                        nc.scalar.copy(rows[0:2, b, :], bank[b][0:2, 0:NS]).then_inc(s["rows_copied"], 1)

            @block.vector
            def _(dve):
                dve.sem_inc(s["cols_added"], 2)
                with dve.Fori(0, STEPS // 2) as i:
                    for b in range(2):
                        dve.wait_ge(s["cols_ready"], at(i, 2, b + 1))
                        for c in range(2):
                            last = nc.vector.tensor_tensor(
                                g.mods[:, bass.ds(i * 8 + MOD_BLOCKS * (first + b), 4), c:c + 1].rearrange("p n o -> p (n o)"),
                                bank[2 + b][:, c:8:2],
                                g.bmod[:, bass.ds(i * 8 + MOD_BLOCKS * (first + b), 4)], ALU.add)
                        last.then_inc(s["cols_added"], 1)
                dve.wait_ge(s["cols_added"], STEPS + 2)
                scales_plus_one(nc, g, (layer,))


def modulate_blocks(dve, nc, g, ready, scale, shift, done=None):
    for b in range(NB):
        ready(b)
        for c, (hs, xs) in enumerate(((H_LAT, S_LAT), (H_CTX, S_CTX))):
            last = nc.vector.tensor_scalar(g.h[:, b, hs], g.x[:, b, xs], g.mods[:, scale + b, c:c + 1],
                                           g.mods[:, shift + b, c:c + 1], ALU.mult, ALU.add)
        if done is not None:
            last.then_inc(done, 1)


def first_modulate(nc, g):
    with phase(nc, "unused"), nc.Block() as block:

        @block.vector
        def _(dve):
            modulate_blocks(dve, nc, g, lambda b: None, mod_at(0, 1), mod_at(0, 0))




SPLIT_SEMS = ["w_loaded:2", "wh_ready", "wl_ready", "mm_done", "evacuated", "hi_ready", "src_ready"]
HALF = T // 2
UNITS = 4


class Splitter:

    def __init__(self, nc, s, sb, w):
        self.nc, self.s, self.w = nc, s, w
        self.raw = sb("ring", 2, NB, 2 * P)
        self.hi, self.lo = (sb(n, 2, NB, 2 * P, dt=F32R) for n in ("ring_hi", "ring_lo"))

    def load(self, sp, i, per, n):
        sp.wait_ge(self.s["wl_ready"], at(i, per, n + 1))
        sp.dma_start(self.raw[:, n % 2].rearrange("p k n -> p (k n)"),
                     slab(self.w, i * per + n)).then_inc(self.s["w_loaded"][n % 2], 16)

    def upper(self, act, i, per, n):
        act.wait_ge(self.s["w_loaded"][n % 2], at(i, 8 * per, 16 * (n // 2 + 1)))
        act.wait_ge(self.s["mm_done"], at(i, 2 * per, 2 * n + 2))
        self.nc.scalar.copy(self.hi[:, n % 2], self.raw[:, n % 2]).then_inc(self.s["wh_ready"], 1)

    def rest(self, dve, i, per, n):
        dve.wait_ge(self.s["wh_ready"], at(i, per, n + 1))
        self.nc.vector.tensor_tensor(self.lo[:, n % 2], self.raw[:, n % 2], self.hi[:, n % 2].bitcast(F32),
                                     ALU.subtract).then_inc(self.s["wl_ready"], 1)

    def product(self, acc, n, m, k, x_hi, x_lo, first, end):
        parts = ((self.hi, x_hi), (self.hi, x_lo), (self.lo, x_hi))
        for q, (wt, x) in enumerate(parts):
            for h in range(2):
                last = self.nc.tensor.matmul(acc[h][:, 0:HALF], wt[:, n % 2, k, m * P:(m + 1) * P],
                                             x[:, k, h * HALF:(h + 1) * HALF], start=first and q == 0, stop=end and q == 2)
        return last


def token_parts(buf, b):
    return ((buf[:, b, H_LAT], S_LAT), (buf[:, b, H_CTX], S_CTX))


def projection(nc, g, w, n_pairs, out=None, keep=None, mix=None, load=None):
    PER = 2
    n_pass = n_pairs // PER
    names = SPLIT_SEMS + ["stored:4", "mixed", f"src_loaded:{NB}"]
    with buffers(nc) as (sb, banks), phase(nc, *names) as s:
        ring = Splitter(nc, s, sb, w)
        x_hi, x_lo = (sb(n, NB, T, dt=F32R) for n in ("src_hi", "src_lo"))
        stage = sb("stage", UNITS, T) if keep is None else None
        src = sb("src", 2, HW) if mix is not None else sb("src", NB, T) if load is not None else None
        bank = banks(8)
        acc = [(bank[2 * u], bank[2 * u + 1]) for u in range(UNITS)]

        def source(b):
            if mix is not None:
                return token_parts(src, b % 2)
            return ((src[:, b, :], slice(0, T)),) if load is not None else token_parts(g.h, b)

        with nc.Block() as block:

            @block.sync
            def _(sp):
                if load is not None:
                    for b in range(NB):
                        sp.dma_start(src[:, b, :], load[b]).then_inc(s["src_loaded"][b], 16)
                        if b == 1:
                            ring.load(sp, 0, PER, 0)
                else:
                    ring.load(sp, 0, PER, 0)
                ring.load(sp, 0, PER, 1)
                with sp.Fori(1, n_pass) as i:
                    for n in range(PER):
                        ring.load(sp, i, PER, n)

            @block.tensor
            def _(pe):
                pe.sem_inc(s["mm_done"], 4)
                with pe.Fori(0, n_pass) as i:
                    for n in range(PER):
                        pe.wait_ge(s["wl_ready"], at(i, PER, n + 3))
                        for m in range(2):
                            u = 2 * n + m
                            pe.wait_ge(s["evacuated"], at(i, UNITS, u + 1))
                            for k in range(NB):
                                if u == 0:
                                    pe.wait_ge(s["src_ready"], k + 1)
                                last = ring.product(acc[u], n, m, k, x_hi, x_lo, k == 0, k == NB - 1)
                            last.then_inc(s["mm_done"], 1)

            @block.scalar
            def _(act):
                act.sem_inc(s["evacuated"], UNITS)
                for b in range(NB):
                    if mix is not None:
                        act.wait_ge(s["mixed"], b + 1)
                    if load is not None:
                        act.wait_ge(s["src_loaded"][b], 16)
                    for ap, cols in source(b):
                        last = nc.scalar.copy(x_hi[:, b, cols], ap)
                    last.then_inc(s["hi_ready"], 1)
                    if b == 2:
                        ring.upper(act, 0, PER, 0)
                if keep is None:
                    for u in range(UNITS):
                        act.sem_inc(s["stored"][u], 16)

                def block_(i, more):
                    for n in range(PER):
                        if n < PER - 1 or more:
                            ring.upper(act, i, PER, n + 1)
                        for m in range(2):
                            u = 2 * n + m
                            act.wait_ge(s["mm_done"], at(i, UNITS, u + 5))
                            if keep is None:
                                act.wait_ge(s["stored"][u], at(i, 16, 16))
                                row = stage[:, u, :]
                            else:
                                row = keep[:, bass.ds(i * UNITS + u, 1), :].rearrange("p o t -> p (o t)")
                            for h in range(2):
                                last = nc.scalar.copy(row[:, h * HALF:(h + 1) * HALF], acc[u][h][:, 0:HALF])
                            last.then_inc(s["evacuated"], 1)
                            if keep is None:
                                act.wait_ge(s["evacuated"], at(i, UNITS, u + 5))
                                act.dma_start(slab(out, i * UNITS + u), stage[:, u, :]).then_inc(s["stored"][u], 16)

                with act.Fori(0, n_pass - 1) as i:
                    block_(i, True)
                block_(n_pass - 1, False)
                if keep is None:
                    for u in range(UNITS):
                        act.wait_ge(s["stored"][u], 16 * (n_pass + 1))

            @block.vector
            def _(dve):
                def lower(b):
                    dve.wait_ge(s["hi_ready"], b + 1)
                    for ap, cols in source(b):
                        last = nc.vector.tensor_tensor(x_lo[:, b, cols], ap, x_hi[:, b, cols].bitcast(F32), ALU.subtract)
                    last.then_inc(s["src_ready"], 1)

                dve.sem_inc(s["wl_ready"], 2)
                for b in range(NB):
                    if mix is not None:
                        if b >= 2:
                            dve.wait_ge(s["src_ready"], b - 1)
                        nc.vector.scalar_tensor_tensor(src[:, b % 2, :], g.xx[:, b, :], g.vec[:, mix + b:mix + b + 1],
                                                       g.h[:, b, :], ALU.mult, ALU.add).then_inc(s["mixed"], 1)
                        if b >= 1:
                            lower(b - 1)
                    else:
                        lower(b)
                    if b == 3:
                        ring.rest(dve, 0, PER, 0)
                if mix is not None:
                    lower(NB - 1)

                def block_(i, more):
                    for n in range(PER):
                        if n < PER - 1 or more:
                            ring.rest(dve, i, PER, n + 1)

                with dve.Fori(0, n_pass - 1) as i:
                    block_(i, True)
                block_(n_pass - 1, False)


def mlp(nc, g, w, delta):
    QUARTERS, PER = NFB // NB, 8
    names = SPLIT_SEMS + ["cleared", "added", "link", "hidden"]
    PASS_UNITS = 2 * PER
    with buffers(nc) as (sb, banks), phase(nc, *names) as s:
        ring = Splitter(nc, s, sb, w)
        x_hi, x_lo = (sb(n, NB, T, dt=F32R) for n in ("src_hi", "src_lo"))
        y_hi, y_lo = (sb(n, NB, T, dt=F32R) for n in ("hidden_hi", "hidden_lo"))
        stage = sb("stage", 2, T)
        bank = banks(8)
        acc = [(bank[2 * u], bank[2 * u + 1]) for u in range(UNITS)]
        with nc.Block() as block:

            @block.sync
            def _(sp):
                with sp.Fori(0, QUARTERS) as i:
                    for n in range(PER):
                        ring.load(sp, i, PER, n)

            @block.tensor
            def _(pe):
                pe.sem_inc(s["mm_done"], 4)
                with pe.Fori(0, QUARTERS) as i:
                    for n in range(PER):
                        pe.wait_ge(s["wl_ready"], at(i, PER, n + 3))
                        for m in range(2):
                            u = 2 * n + m
                            pe.wait_ge(s["evacuated"], at(i, PASS_UNITS, u + 1))
                            for k in range(NB):
                                if u == 0:
                                    pe.wait_ge(s["src_ready"], k + 1)
                                if u == NB:
                                    pe.wait_ge(s["hidden"], at(i, NB, k + 1))
                                hi, lo = (x_hi, x_lo) if u < NB else (y_hi, y_lo)
                                last = ring.product(acc[u % UNITS], n, m, k, hi, lo, k == 0, k == NB - 1)
                            last.then_inc(s["mm_done"], 1)

            @block.scalar
            def _(act):
                act.sem_inc(s["evacuated"], UNITS)
                for b in range(NB):
                    for ap, cols in token_parts(g.h, b):
                        last = nc.scalar.copy(x_hi[:, b, cols], ap)
                    last.then_inc(s["hi_ready"], 1)
                    if b == 2:
                        ring.upper(act, 0, PER, 0)

                def block_(i, more):
                    for n in range(PER):
                        if n < PER - 1 or more:
                            ring.upper(act, i, PER, n + 1)
                        for m in range(2):
                            u = 2 * n + m
                            act.wait_ge(s["mm_done"], at(i, PASS_UNITS, u + 5))
                            row_used = s["added"] if u < 2 or u >= NB + 2 else s["hidden"]
                            act.wait_ge(row_used, at(i, NB, u + 7 if u < 2 else u - 1))
                            for h in range(2):
                                last = nc.scalar.activation(stage[:, u % 2, h * HALF:(h + 1) * HALF],
                                                            acc[u % UNITS][h][:, 0:HALF], ACT.Relu if u < NB else ACT.Copy)
                            last.then_inc(s["evacuated"], 1)

                with act.Fori(0, QUARTERS - 1) as i:
                    block_(i, True)
                block_(QUARTERS - 1, False)

            @block.vector
            def _(dve):
                dve.sem_inc(s["wl_ready"], 2)
                dve.sem_inc(s["added"], NB)
                for b in range(NB):
                    dve.wait_ge(s["hi_ready"], b + 1)
                    for ap, cols in token_parts(g.h, b):
                        last = nc.vector.tensor_tensor(x_lo[:, b, cols], ap, x_hi[:, b, cols].bitcast(F32), ALU.subtract)
                    last.then_inc(s["src_ready"], 1)
                    if b == 3:
                        ring.rest(dve, 0, PER, 0)
                nc.vector.memset(delta[:, :, :], 0.0).then_inc(s["cleared"], 1)
                dve.wait_ge(s["cleared"], 1)

                def block_(i, more):
                    link = Link(dve, s["link"], i, 2 * NB)
                    for n in range(PER):
                        if n < PER - 1 or more:
                            ring.rest(dve, i, PER, n + 1)
                        for m in range(2):
                            u = 2 * n + m
                            row = stage[:, u % 2, :]
                            dve.wait_ge(s["evacuated"], at(i, PASS_UNITS, u + 5))
                            if u < NB:
                                link(nc.vector.tensor_tensor(row, row, row, ALU.mult))
                                link(nc.vector.tensor_copy(y_hi[:, u, :], row))
                                nc.vector.tensor_tensor(y_lo[:, u, :], row, y_hi[:, u, :].bitcast(F32),
                                                        ALU.subtract).then_inc(s["hidden"], 1)
                            else:
                                nc.vector.tensor_tensor(delta[:, u - NB, :], delta[:, u - NB, :], row,
                                                        ALU.add).then_inc(s["added"], 1)
                    link.end()

                with dve.Fori(0, QUARTERS - 1) as i:
                    block_(i, True)
                block_(QUARTERS - 1, False)




def norm(nc, g, delta, layer, sub, gate, nxt):
    col = V_LN + (layer * 2 + sub) * 2 * NB
    names = ["gated", "added", "sums", "centred", "squares", "variances", "root", "inverse",
             "scaled", "gained", "stored"]
    with buffers(nc) as (sb, banks), phase(nc, *names) as s:
        dl = delta
        rs = sb("rstd", T)
        mean_l, mean_c, var_l, var_c = banks(4)
        parts = ((S_LAT, mean_l, var_l, LAT), (S_CTX, mean_c, var_c, CTX))
        with nc.Block() as block:

            @block.sync
            def _(sp):
                if nxt is None:
                    for b in range(NB):
                        sp.wait_ge(s["gained"], b + 1)
                        sp.dma_start(g.d["y_out"][b], g.x[:, b, :]).then_inc(s["stored"], 16)
                    sp.wait_ge(s["stored"], 16 * NB)

            @block.scalar
            def _(act):
                for b in range(NB):
                    for c, (cols, _, _, _) in enumerate(parts):
                        last = nc.scalar.activation(dl[:, b, cols], dl[:, b, cols], ACT.Identity,
                                                    scale=g.mods[:, gate + b, c:c + 1])
                    last.then_inc(s["gated"], 1)
                for b in range(NB):
                    act.wait_ge(s["centred"], b + 1)
                    nc.scalar.activation(dl[:, b, :], g.x[:, b, :], ACT.Square).then_inc(s["squares"], 1)
                act.wait_ge(s["variances"], 1)
                for cols, _, var, n in parts:
                    nc.scalar.activation(rs[:, cols], var[:, 0:n], ACT.Sqrt, bias=g.eps_ln).then_inc(s["root"], 1)
                for b in range(NB):
                    act.wait_ge(s["scaled"], b + 1)
                    nc.scalar.activation(g.x[:, b, :], g.x[:, b, :], ACT.Identity, scale=g.vec[:, col + b:col + b + 1],
                                         bias=g.vec[:, col + NB + b:col + NB + b + 1]).then_inc(s["gained"], 1)

            @block.tensor
            def _(pe):
                for b in range(NB):
                    pe.wait_ge(s["added"], b + 1)
                    for cols, mean, _, n in parts:
                        last = nc.tensor.matmul(mean[:, 0:n], g.mean_w, g.x[:, b, cols], start=(b == 0), stop=(b == NB - 1))
                last.then_inc(s["sums"], 1)
                for b in range(NB):
                    pe.wait_ge(s["squares"], b + 1)
                    for cols, _, var, n in parts:
                        last = nc.tensor.matmul(var[:, 0:n], g.mean_w, dl[:, b, cols], start=(b == 0), stop=(b == NB - 1))
                last.then_inc(s["variances"], 1)

            @block.vector
            def _(dve):
                for b in range(NB):
                    dve.wait_ge(s["gated"], b + 1)
                    nc.vector.scalar_tensor_tensor(g.x[:, b, :], g.x[:, b, :], ALPHA, dl[:, b, :],
                                                   ALU.mult, ALU.add).then_inc(s["added"], 1)
                dve.wait_ge(s["sums"], 1)
                for b in range(NB):
                    for cols, mean, _, n in parts:
                        last = nc.vector.tensor_tensor(g.x[:, b, cols], g.x[:, b, cols], mean[:, 0:n], ALU.subtract)
                    last.then_inc(s["centred"], 1)
                dve.wait_ge(s["root"], 2)
                nc.vector.reciprocal(rs[:, :], rs[:, :]).then_inc(s["inverse"], 1)
                dve.wait_ge(s["inverse"], 1)
                for b in range(NB):
                    nc.vector.tensor_tensor(g.x[:, b, :], g.x[:, b, :], rs[:, :], ALU.mult).then_inc(s["scaled"], 1)
                if nxt is not None:
                    modulate_blocks(dve, nc, g, lambda b: dve.wait_ge(s["gained"], b + 1), *nxt)




def chunked(ap):
    return ap.rearrange("p (u c) -> p u c", c=C)


def by_direction(buf, plain):
    yield buf[:, :, 0, :], chunked(plain)
    yield buf[:, 0:NLAT, 1, :], chunked(plain[:, S_LAT][:, ::-1])
    yield buf[:, NLAT:NCHUNK, 1, :], chunked(plain[:, S_CTX][:, ::-1])


def unit(u, hh):
    return GROUP * (u // 2) + 2 * hh + u % 2


def flat4(ap):
    return ap.rearrange("p u n -> p (u n)")


INVERSE_SEMS = ["first_t", "first_n_ps", "xx_ready", "y_ps", "ly_ready", "x_ps", "inv_ready"]
PER_GROUP = dict(first_t=2, first_n_ps=2, xx_ready=2 + 2 * (LEVELS - 1), y_ps=2 * LEVELS, ly_ready=2 * LEVELS,
                 x_ps=2 * LEVELS, inv_ready=2)


def group_at(i, j, name, k):
    return at(i, PER_GROUP[name] * NGROUP, PER_GROUP[name] * j + k)


def invert_first_pe(pe, nc, g, s, w, i, j, h):
    pe.wait_ge(s["first_t"], group_at(i, j, "first_t", h + 1))
    for n in range(2):
        last = nc.tensor.transpose(w.y_bank[h][:, (2 + n) * P:(3 + n) * P], w.x0[h][:, 1, n, :], g.ident)
    last.then_inc(s["first_n_ps"], 1)


def invert_pe(pe, nc, g, s, w, i, j, more, between):
    for lv in range(LEVELS):
        xx = [w.xx[:, h] if lv else w.x0[h] for h in range(2)]
        for h in range(2):
            pe.wait_ge(s["xx_ready"], group_at(i, j, "xx_ready", 2 * lv + h + 1))
            if lv == LEVELS - 1 and more:
                invert_first_pe(pe, nc, g, s, w, i, j + 1, h)
            for n in range(2):
                last = nc.tensor.matmul(w.y_bank[h][:, n * P:(n + 1) * P], w.lt[:, j % 2, 2 * h + n, :], xx[h][:, 0, n, :],
                                        start=True, stop=True)
            last.then_inc(s["y_ps"], 1)
        for h in range(2):
            pe.wait_ge(s["ly_ready"], group_at(i, j, "ly_ready", 2 * lv + h + 1))
            if lv == 0 and j:
                pe.wait_ge(s["inv_ready"], group_at(i, j - 1, "inv_ready", h + 1))
            for n in range(2):
                last = nc.tensor.matmul(w.x_bank[h][:, (2 + n) * P:(3 + n) * P], w.y[:, h, n, :], xx[h][:, 1, n, :],
                                        start=True, stop=True)
            if lv < LEVELS - 1:
                for n in range(2):
                    last = nc.tensor.matmul(w.x_bank[h][:, n * P:(n + 1) * P], xx[h][:, 1, n, :], w.y[:, h, n, :],
                                            start=True, stop=True)
            last.then_inc(s["x_ps"], 1)
        if lv in between:
            between[lv]()


def invert_first_t(nc, g, s, w, j, link):
    l0 = g.mask(K_L0)
    for h in range(2):
        link(nc.vector.tensor_tensor(w.x0[h][:, 1, :, :], w.lt[:, j % 2, 2 * h:2 * h + 2, :],
                                     l0.unsqueeze(1).to_broadcast([P, 2, P]), ALU.mult))
        nc.vector.tensor_tensor(w.x0[h][:, 1, :, :], w.x0[h][:, 1, :, :],
                                g.ident.unsqueeze(1).to_broadcast([P, 2, P]), ALU.add).then_inc(s["first_t"], 1)


def invert_first_n(dve, nc, s, w, i, j):
    for h in range(2):
        dve.wait_ge(s["first_n_ps"], group_at(i, j, "first_n_ps", h + 1))
        nc.vector.tensor_copy(flat4(w.x0[h][:, 0, :, :]), w.y_bank[h][:, 2 * P:4 * P]).then_inc(s["xx_ready"], 1)


def invert_dve(dve, nc, g, s, w, i, j, more, between):
    for lv in range(LEVELS):
        below = g.mask(K_LV + lv * P)
        for h in range(2):
            dve.wait_ge(s["y_ps"], group_at(i, j, "y_ps", 2 * lv + h + 1))
            nc.vector.tensor_tensor(w.y[:, h, :, :], w.y_bank[h][:, 0:2 * P].rearrange("p (n c) -> p n c", n=2),
                                    below.unsqueeze(1).to_broadcast([P, 2, P]), ALU.mult).then_inc(s["ly_ready"], 1)
        if lv == LEVELS - 1 and more:
            invert_first_n(dve, nc, s, w, i, j + 1)
        for h in range(2):
            dve.wait_ge(s["x_ps"], group_at(i, j, "x_ps", 2 * lv + h + 1))
            if lv < LEVELS - 1:
                both = w.xx[:, h].rearrange("p t n c -> p (t n c)")
                before = both if lv else w.x0[h].rearrange("p t n c -> p (t n c)")
                if lv == 0 and j:
                    dve.wait_ge(s["inv_ready"], group_at(i, j - 1, "inv_ready", 2))
                nc.vector.tensor_tensor(both, w.x_bank[h][:, :], before, ALU.add).then_inc(s["xx_ready"], 1)
            else:
                out = w.tt[:, GROUP * j + 2 * h:GROUP * j + 2 * h + 2, :]
                nc.vector.tensor_tensor(flat4(out), w.x_bank[h][:, 2 * P:4 * P], flat4(w.xx[:, h, 1, :, :]),
                                        ALU.add).then_inc(s["inv_ready"], 1)
        if lv in between:
            between[lv]()


class Work:
    pass



W_W0, W_A0, W_KK, W_KA, W_RK, W_GG, W_GB = 0, 2, 4, 5, 6, 7, 8
W_COLS = 9
W_END = 3 * P + W_COLS


def token_shift(nc, g):
    with phase(nc, "neighbours") as s, nc.Block() as block:

        @block.vector
        def _(dve):
            nc.vector.memset(g.xx[:, :, :], 0.0).then_inc(s["neighbours"], 1)
            for edge in (slice(0, 1), slice(H_LAT.stop, H_CTX.start), slice(H_CTX.stop, HW)):
                nc.vector.memset(g.h[:, :, edge], 0.0).then_inc(s["neighbours"], 1)
            dve.wait_ge(s["neighbours"], 4)
            for b in range(NB):
                nc.vector.tensor_tensor(g.xx[:, b, 1:HW - 1], g.h[:, b, 0:HW - 2], g.h[:, b, 2:HW],
                                        ALU.add).then_inc(s["neighbours"], 1)
            for b in range(NB):
                dve.wait_ge(s["neighbours"], b + 5)
                nc.vector.scalar_tensor_tensor(g.xx[:, b, 1:HW - 1], g.xx[:, b, 1:HW - 1], 0.5, g.h[:, b, 1:HW - 1],
                                               ALU.mult, ALU.subtract)


def low_rank(nc, g, j, low):
    with buffers(nc) as (sb, banks), phase(nc, "loaded", "mixed", "mm_done", "evacuated") as s:
        wt = sb("low_w", 3, NB, P)
        xi = sb("low_x", 2, NB, HW)
        bank = banks(4)
        with nc.Block() as block:

            @block.sync
            def _(sp):
                sp.dma_start(wt[:, :, :, :].rearrange("p a k n -> p a (k n)"),
                             g.d["rw_low"][3 * j:3 * j + 3].rearrange("a p n -> p a n")).then_inc(s["loaded"], 16)

            @block.vector
            def _(dve):
                for n, m in enumerate((1, 4, 5)):
                    if n >= 2:
                        dve.wait_ge(s["mm_done"], n - 1)
                    for b in range(NB):
                        col = V_MU + (j * 6 + m) * NB + b
                        last = nc.vector.scalar_tensor_tensor(xi[:, n % 2, b, :], g.xx[:, b, :], g.vec[:, col:col + 1],
                                                              g.h[:, b, :], ALU.mult, ALU.add)
                    last.then_inc(s["mixed"], 1)

            @block.tensor
            def _(pe):
                pe.wait_ge(s["loaded"], 16)
                for n in range(3):
                    pe.wait_ge(s["mixed"], n + 1)
                    if n >= 2:
                        pe.wait_ge(s["evacuated"], n - 1)
                    for k in range(NB):
                        nc.tensor.matmul(bank[2 * (n % 2)][:, :], wt[:, n, k, :], xi[:, n % 2, k, H_LAT],
                                         start=(k == 0), stop=(k == NB - 1))
                        last = nc.tensor.matmul(bank[2 * (n % 2) + 1][:, 0:CTX], wt[:, n, k, :], xi[:, n % 2, k, H_CTX],
                                                start=(k == 0), stop=(k == NB - 1))
                    last.then_inc(s["mm_done"], 1)

            @block.scalar
            def _(act):
                for n, fn in enumerate((ACT.Tanh, ACT.Copy, ACT.Sigmoid)):
                    act.wait_ge(s["mm_done"], n + 1)
                    nc.scalar.activation(low[:, n, S_LAT], bank[2 * (n % 2)][:, :], fn)
                    nc.scalar.activation(low[:, n, S_CTX], bank[2 * (n % 2) + 1][:, 0:CTX], fn).then_inc(s["evacuated"], 1)


STEPS = NCHUNK
ORDER = (8, 9, 0, 1, 2, 3, 4, 5, 6, 7)


def rwkv_heads(nc, g, j, low, mod_layers):
    MODS = len(mod_layers) * MOD_STEPS // NB
    assert MODS in (0, 3)
    first_slab = mod_layers[0] * MOD_STEPS if MODS else 0
    names = ["passed", "in_loaded", "s0_loaded", "gains", "keys", "bias_in", "kt_ready", "y_stored", "state_stored", "link", "squares", "projected", "sums", "sig_w", "sig_a", "gates",
             "roots", "scanned", "g_before", "exps", "reversed_v", "bonus_in", "bonus_sums", "bonus", "operands",
             "products", "masked", "tokens", "tokens_out", "chain_x", "x_out", "chain_sa", "sa_out", "chain_s",
             "s0_ready", "s1_ready", "s_first", "values", "saz_out", "o_done", "s_saved", "y_in", "means", "y_centred", "y_squares", "vars", "y_root", "y_ready",
             "mod_loaded", "mod_done", "mod_rows", "mod_cols", "mod_added"] + INVERSE_SEMS
    with buffers(nc) as (sb, banks), phase(nc, *names) as s:
        w = Work()
        rkv, hw, s0 = sb("rkv", 3, T), sb("head_w", W_END), sb("s0", 2, C)
        rn, bs, os_, sq = (sb(n, T) for n in ("rn", "bs", "os", "sq"))
        ld, icl, gc, e_in, kk, kd, ve, rt, at_ = (
            sb(n, NCHUNK, 2, C) for n in ("ld", "icl", "gc", "e_in", "kk2", "kd", "ve", "rt", "at"))
        kt, bt = kd, icl
        t1 = rt[:, 0:NCHUNK // 2].rearrange("p u e c -> p (u e c)")
        two = sb("e_ex_inv", 2 * NCHUNK, 2, C)
        e_ex, e_inv, vz = two[:, 0:NCHUNK], two[:, NCHUNK:2 * NCHUNK], two
        w.lt, w.xx, w.y = sb("lt", 2, GROUP, P), sb("xx", 2, 2, 2, P), sb("y", 2, 2, P)
        w.tt, ak, rr = sb("tt", 2 * NCHUNK, P), sb("ak", 2 * NCHUNK, P), sb("rr", 2, 2 * NCHUNK, P)
        w.x0 = [buf[:, 0:4 * P].rearrange("p (t n c) -> p t n c", t=2, n=2) for buf in (rn, bs)]
        spare = g.h[:, :, :].rearrange("p b t -> p (b t)")
        tok = spare[:, 0:3 * TT].rearrange("p (u q c) -> p u q c", q=3, c=C)
        bon, gate = spare[:, 3 * TT:3 * TT + T], spare[:, 3 * TT + T:4 * TT]
        gn = sb("gn", 2)
        if MODS:
            mod_slab = sb("mod_slab", NB, NS)
            mod_rows = [gc[0:2, 0:4].rearrange("p u e c -> p (u e c)"), gc[0:2, 4:8].rearrange("p u e c -> p (u e c)"),
                        kk[0:2, 0:4].rearrange("p u e c -> p (u e c)")]
        xs, sa, saz = sb("xs", 2, C), sb("sa", 2, C), sb("saz", 2, 2, C)
        st = sb("state", 2, 2, C)
        sout = sb("sout", 2, C)
        bank = banks(8)
        w.y_bank, w.x_bank = bank[0:2], bank[2:4]
        lat_banks, ctx_bank = (bank[4], bank[5], bank[6], bank[7]), (bank[2], bank[1])
        GATE_CTX = slice(2 * P, 3 * P)
        ctx_cols_of = lambda m, e: ctx_bank[e][:, (m + e) * P:(m + e + 1) * P]
        r, k, v = rkv[:, 0, :], rkv[:, 1, :], rkv[:, 2, :]
        hcol = lambda n: hw[:, 3 * P + n:3 * P + n + 1]
        flat = lambda buf: buf[:, 0:NCHUNK, :, :].rearrange("p u e c -> p (u e c)")

        with nc.Block() as block:

            @block.sync
            def _(sp):
                def load(n):
                    for m in range(3):
                        sp.dma_start(rkv[:, m, :], slab(g.d["rkv"], n + m * NB)).then_inc(s["in_loaded"], 16)
                    sp.dma_start(hw[:, :], slab(g.d["rw_head"], n + j * NB)).then_inc(s["in_loaded"], 16)

                def load_state(n):
                    sp.dma_start(s0[:, :, :].rearrange("p e v -> p (e v)"),
                                 slab(g.d["rw_state"], n + j * NB)).then_inc(s["s0_loaded"], 16)

                def store_state(i):
                    wait_alone(sp, s["s_saved"], at(i, 2, 2), s["passed"])
                    sp.dma_start(slab(g.d["rw_state_out"], i + j * NB),
                                 sout[:, :, :].rearrange("p e v -> p (e v)")).then_inc(s["state_stored"], 16)

                def store_block(i):
                    wait_alone(sp, s["y_ready"], at(i, 1, 2), s["passed"])
                    sp.dma_start(slab(g.d["mixed"], i), os_[:, :]).then_inc(s["y_stored"], 16)

                def load_mod(i, m):
                    if MODS:
                        if not (m == 0 and isinstance(i, int)):
                            wait_alone(sp, s["mod_done"], at(i, MODS, m), s["passed"])
                        sp.dma_start(mod_slab[:, :, :].rearrange("p k n -> p (k n)"),
                                     slab(g.d["w_mod"], i * MODS + (first_slab + m))).then_inc(s["mod_loaded"], 16)

                sp.sem_inc(s["y_stored"], 16)
                sp.sem_inc(s["state_stored"], 16)
                load(0)
                load_state(0)
                load_mod(0, 0)
                with sp.Fori(0, NB - 1) as i:
                    load_mod(i, 1)
                    load_mod(i, 2)
                    wait_alone(sp, s["operands"], at(i, 6, 6), s["passed"])
                    wait_alone(sp, s["reversed_v"], at(i, 3, 3), s["passed"])
                    load(i + 1)
                    store_state(i)
                    wait_alone(sp, s["s0_ready"], at(i, STEPS, 2), s["passed"])
                    wait_alone(sp, s["s1_ready"], at(i, STEPS, 2), s["passed"])
                    load_state(i + 1)
                    load_mod(i + 1, 0)
                    store_block(i)
                load_mod(NB - 1, 1)
                load_mod(NB - 1, 2)
                store_state(NB - 1)
                store_block(NB - 1)
                sp.wait_ge(s["state_stored"], 16 * (NB + 1))
                sp.wait_ge(s["y_stored"], 16 * (NB + 1))

            @block.gpsimd
            def _(pool):
                with pool.Fori(0, NB) as i:
                    wait_alone(pool, s["in_loaded"], at(i, 64, 64), s["passed"])
                    for both, plain in by_direction(ve, v):
                        nc.gpsimd.tensor_copy(both, plain).then_inc(s["reversed_v"], 1)
                    wait_alone(pool, s["keys"], at(i, 1, 1), s["passed"])
                    wait_alone(pool, s["exps"], at(i, 3, 3), s["passed"])
                    nc.gpsimd.tensor_tensor(flat(kt), flat(kd), flat(e_inv), ALU.mult).then_inc(s["kt_ready"], 1)
                    wait_alone(pool, s["bonus"], at(i, 1, 1), s["passed"])
                    wait_alone(pool, s["gains"], at(i, 1, 1), s["passed"])
                    nc.gpsimd.tensor_scalar(bon[:, :], bon[:, :], gn[:, 1:2], None, ALU.add).then_inc(s["bias_in"], 1)
                    for jg in range(NGROUP):
                        wait_alone(pool, s["tokens_out"], at(i, NGROUP, jg + 1), s["passed"])
                        for e in range(2):
                            nc.gpsimd.tensor_tensor(
                                vz[:, GROUP * jg:GROUP * (jg + 1), e, :], tok[:, GROUP * jg:GROUP * (jg + 1), 1, :],
                                g.const[:, K_BO + e * C:K_BO + (e + 1) * C].unsqueeze(1).to_broadcast([P, GROUP, C]),
                                ALU.mult).then_inc(s["values"], 1)

            @block.scalar
            def _(act):
                def rates(i):
                    act.wait_ge(s["projected"], at(i, 1, 1))
                    for m, (buf, col, done) in enumerate(((ld, W_W0, s["sig_w"]), (icl, W_A0, s["sig_a"]))):
                        for e in range(2):
                            lat_bank, ctx_cols = lat_banks[2 * m + e], ctx_cols_of(m, e)
                            turn = slice(None, None, -1 if e else 1)
                            nc.scalar.activation(buf[:, 0:NLAT, e, :], chunked(lat_bank[:, turn]), ACT.Sigmoid,
                                                 bias=hcol(col + e))
                            nc.scalar.activation(buf[:, NLAT:NCHUNK, e, :], chunked(ctx_cols[:, turn]), ACT.Sigmoid,
                                                 bias=hcol(col + e)).then_inc(done, 1)

                rates(0)

                def block_(i, more):
                    act.wait_ge(s["y_ready"], at(i, 1, 1))
                    nc.scalar.copy(gate[:, S_LAT], bank[3][:, :])
                    nc.scalar.copy(gate[:, S_CTX], bank[2][:, GATE_CTX]).then_inc(s["gates"], 1)
                    act.wait_ge(s["sums"], at(i, 1, 1))
                    nc.scalar.activation(rn[:, S_LAT], bank[4][:, :], ACT.Sqrt, bias=g.eps_nrm)
                    nc.scalar.activation(rn[:, S_CTX], bank[5][:, 0:CTX], ACT.Sqrt, bias=g.eps_nrm).then_inc(s["roots"], 1)
                    act.wait_ge(s["scanned"], at(i, 1, 1))
                    nc.scalar.activation(flat(e_in), flat(gc), ACT.Exp, scale=-HALF_DECAY).then_inc(s["exps"], 1)
                    nc.scalar.activation(flat(e_inv), flat(gc), ACT.Exp, scale=HALF_DECAY).then_inc(s["exps"], 1)
                    act.wait_ge(s["g_before"], at(i, 1, 1))
                    nc.scalar.activation(flat(e_ex), flat(ld), ACT.Exp, scale=-HALF_DECAY).then_inc(s["exps"], 1)
                    if MODS:
                        act.wait_ge(s["exps"], at(i, 3, 3))
                    for m in range(MODS - 1):
                        act.wait_ge(s["mod_done"], at(i, MODS, m + 1))
                        nc.scalar.copy(mod_rows[m], bank[3 * m][0:2, :]).then_inc(s["mod_rows"], 1)
                    for jg in range(NGROUP):
                        act.wait_ge(s["tokens"], at(i, 2 * NGROUP, 2 * jg + 2))
                        for hh in range(2):
                            u2 = slice(GROUP * jg + 2 * hh, GROUP * jg + 2 * hh + 2)
                            last = nc.scalar.copy(tok[:, u2, :, :].rearrange("p u q c -> p (u q c)"),
                                                  bank[4 + hh][:, 0:6 * C])
                        last.then_inc(s["tokens_out"], 1)
                    for n in range(STEPS):
                        u = ORDER[n]
                        act.wait_ge(s["chain_s"], at(i, STEPS, n + 1))
                        for e in range(2):
                            last = nc.scalar.activation(st[0:C, e, 0, :], bank[2][0:C, e * C:(e + 1) * C], ACT.Identity,
                                                        scale=e_in[0:C, u, e, C - 1:C])
                        last.then_inc(s["s_first"] if n == 1 else s["s0_ready"], 1)
                        if MODS and n == STEPS - 2:
                            act.wait_ge(s["mod_done"], at(i, MODS, MODS))
                            nc.scalar.copy(mod_rows[MODS - 1], bank[7][0:2, :]).then_inc(s["mod_rows"], 1)
                    act.wait_ge(s["vars"], at(i, 1, 1))
                    nc.scalar.activation(rn[:, S_LAT], bank[0][:, :], ACT.Sqrt, bias=g.eps_gn)
                    nc.scalar.activation(rn[:, S_CTX], bank[1][:, 0:CTX], ACT.Sqrt, bias=g.eps_gn).then_inc(s["y_root"], 1)
                    if more:
                        rates(i + 1)

                with act.Fori(0, NB - 1) as i:
                    block_(i, True)
                block_(NB - 1, False)

            @block.tensor
            def _(pe):
                def project(dst_l, dst_c, weights, rows, n):
                    nc.tensor.matmul(dst_l, weights, low[rows, n, S_LAT], start=True, stop=True)
                    return nc.tensor.matmul(dst_c, weights, low[rows, n, S_CTX], start=True, stop=True)

                def head_sums(src, lat, ctx):
                    nc.tensor.matmul(lat, g.mask(K_BO), src[:, S_LAT], start=True, stop=True)
                    return nc.tensor.matmul(ctx, g.mask(K_BO), src[:, S_CTX], start=True, stop=True)

                def pair(buf, rows, u):
                    return buf[rows, u, :, :].rearrange("p e c -> p (e c)")

                def project_rate(m, e):
                    rows = slice(C * e, C * (e + 1))
                    return project(lat_banks[2 * m + e][:, :], ctx_cols_of(m, e), hw[rows, m * P:(m + 1) * P], rows, m)

                def project_rest():
                    project_rate(0, 1)
                    project_rate(1, 1)
                    project(bank[3][:, :], bank[2][:, GATE_CTX], hw[:, 2 * P:3 * P], slice(0, P), 2).then_inc(s["projected"], 1)

                def mod_products(i, m, out, ks):
                    pe.wait_ge(s["mod_loaded"], at(i, 16 * MODS, 16 * (m + 1)))
                    for k in ks:
                        last = nc.tensor.matmul(out[0:2, :], g.silu[:, k, :], mod_slab[:, k, :], start=(k == 0), stop=(k == NB - 1))
                    if k == NB - 1:
                        last.then_inc(s["mod_done"], 1)

                pe.wait_ge(s["in_loaded"], 64)
                project_rate(0, 0)
                project_rate(1, 0)
                project_rest()

                def block_(i, more):
                    if MODS:
                        pe.wait_ge(s["y_ready"], at(i, 1, 1))
                        mod_products(i, 0, bank[0], range(0, 3))
                    pe.wait_ge(s["squares"], at(i, 1, 1))
                    pe.wait_ge(s["gates"], at(i, 1, 1))
                    head_sums(sq, bank[4][:, :], bank[5][:, 0:CTX]).then_inc(s["sums"], 1)
                    if MODS:
                        mod_products(i, 0, bank[0], range(3, NB))
                    pe.wait_ge(s["bonus_in"], at(i, 1, 1))
                    head_sums(bs, bank[6][:, :], bank[7][:, 0:CTX]).then_inc(s["bonus_sums"], 1)
                    if MODS:
                        mod_products(i, 1, bank[3], range(0, 5))
                    pe.wait_ge(s["operands"], at(i, 6, 6))
                    pe.wait_ge(s["kt_ready"], at(i, 1, 1))
                    pe.wait_ge(s["reversed_v"], at(i, 3, 3))
                    pe.wait_ge(s["bonus"], at(i, 1, 1))

                    def products(jg, hh):
                        if jg and hh == 0:
                            pe.wait_ge(s["tokens_out"], at(i, NGROUP, jg))
                        if jg and hh == 1:
                            pe.wait_ge(s["masked"], at(i, 6 * NGROUP, 6 * jg))
                        hr = slice(C * hh, C * (hh + 1))
                        for q, (left, right) in enumerate(((bt, at_), (kt, at_), (kt, rt), (bt, rt))):
                            for n in range(2):
                                c0 = (2 * (q % 2) + n) * P
                                last = nc.tensor.matmul(bank[4 + 2 * hh + q // 2][:, c0:c0 + P], pair(left, hr, 2 * jg + n),
                                                        pair(right, hr, 2 * jg + n), start=True, stop=True)
                        last.then_inc(s["products"], 1)

                    def tokens(jg):
                        wait_alone(pe, s["masked"], at(i, 6 * NGROUP, 6 * jg + 3), s["passed"])
                        for hh in range(2):
                            hr = slice(C * hh, C * (hh + 1))
                            for n in range(2):
                                for q, src in enumerate((kt, ve, bt)):
                                    c0 = (3 * n + q) * C
                                    last = nc.tensor.transpose(bank[4 + hh][:, c0:c0 + C], pair(src, hr, 2 * jg + n),
                                                               g.const[hr, K_ID + hr.start:K_ID + hr.stop])
                            last.then_inc(s["tokens"], 1)

                    products(0, 0)
                    products(0, 1)
                    tokens(0)
                    if MODS:
                        mod_products(i, 1, bank[3], range(5, NB))
                        wait_alone(pe, s["mod_rows"], at(i, MODS, 1), s["passed"])
                    for h in range(2):
                        invert_first_pe(pe, nc, g, s, w, i, 0, h)
                    if MODS:
                        pe.wait_ge(s["mod_rows"], at(i, MODS, 2))
                    for jg in range(NGROUP):
                        ahead = {0: lambda: products(jg + 1, 0), 1: lambda: products(jg + 1, 1), 3: lambda: tokens(jg + 1)}
                        ahead = ahead if jg < NGROUP - 1 else {}
                        invert_pe(pe, nc, g, s, w, i, jg, bool(ahead), ahead)
                    pe.wait_ge(s["inv_ready"], group_at(i, NGROUP - 1, "inv_ready", 2))
                    pe.wait_ge(s["tokens_out"], at(i, NGROUP, NGROUP))
                    pe.wait_ge(s["values"], at(i, 2 * NGROUP, 2 * NGROUP))
                    for n in range(STEPS):
                        u = ORDER[n]
                        uks = [unit(u, hh) for hh in range(2)]
                        o_tile = bank[4 + u // 4][:, (u % 4) * P:(u % 4 + 1) * P]
                        for hh, uk in enumerate(uks):
                            nc.tensor.matmul(bank[0][:, hh * P:(hh + 1) * P], ak[:, uk, :],
                                             tok[:, uk, 1, :].unsqueeze(1).to_broadcast([P, 2, C]), start=(hh == 0),
                                             stop=False, skip_group_check=True)
                        if n:
                            pe.wait_ge(s["s0_ready"], at(i, STEPS, n))
                            pe.wait_ge(s["s1_ready"], at(i, STEPS, n))
                        for hh, uk in enumerate(uks):
                            last = nc.tensor.matmul(bank[0][:, hh * P:(hh + 1) * P], pair(at_, slice(0, P), u), st[:, :, hh, :],
                                                    start=False, stop=True, skip_group_check=True)
                        last.then_inc(s["chain_x"], 1)
                        for hh, uk in enumerate(uks):
                            hr = slice(C * hh, C * (hh + 1))
                            nc.tensor.matmul(o_tile[hr, :], tok[:, uk, 1, :], rr[:, 0, uk, :], start=True, stop=False,
                                             skip_group_check=True)
                        for e in range(2):
                            nc.tensor.matmul(o_tile[:, e * C:(e + 1) * C], st[:, e, :, :].rearrange("p h v -> p (h v)"),
                                             rt[:, u, e, :], start=False, stop=False, skip_group_check=True)
                        if MODS and n == STEPS - 1:
                            wait_alone(pe, s["mod_rows"], at(i, MODS, MODS), s["passed"])
                            for m in range(MODS * MOD_BLOCKS):
                                last = nc.tensor.transpose(bank[3][:, 2 * m:2 * m + 2],
                                                           mod_rows[m // MOD_BLOCKS][:, m % MOD_BLOCKS * P:(m % MOD_BLOCKS + 1) * P],
                                                           g.ident[0:2, 0:2])
                            last.then_inc(s["mod_cols"], 1)
                        pe.wait_ge(s["x_out"], at(i, 2 * STEPS, 2 * n + 2))
                        for hh, uk in enumerate(uks):
                            last = nc.tensor.matmul(bank[1][:, hh * P:(hh + 1) * P], w.tt[:, uk, :],
                                                    xs[:, hh, :].unsqueeze(1).to_broadcast([P, 2, C]), start=True, stop=True)
                        last.then_inc(s["chain_sa"], 1)
                        for hh, uk in enumerate(uks):
                            hr = slice(C * hh, C * (hh + 1))
                            nc.tensor.matmul(bank[2][hr, 0:P], g.ident[:, hr], st[:, :, hh, :], start=True, stop=False)
                            nc.tensor.matmul(bank[2][hr, 0:P], tok[:, uk, 0, :], pair(vz, slice(0, P), uk), start=False, stop=False)
                        pe.wait_ge(s["saz_out"], at(i, STEPS, n + 1))
                        for hh, uk in enumerate(uks):
                            hr = slice(C * hh, C * (hh + 1))
                            last = nc.tensor.matmul(bank[2][hr, 0:P], tok[:, uk, 2, :], pair(saz, slice(0, P), hh),
                                                    start=False, stop=True)
                        last.then_inc(s["chain_s"], 1)
                        pe.wait_ge(s["sa_out"], at(i, STEPS, n + 1))
                        for hh, uk in enumerate(uks):
                            hr = slice(C * hh, C * (hh + 1))
                            last = nc.tensor.matmul(o_tile[hr, :], sa[:, hh, :], rr[:, 1, uk, :], start=False, stop=True,
                                                    skip_group_check=True)
                        last.then_inc(s["o_done"], 1)
                        if MODS and n < NB:
                            if n == 0:
                                pe.wait_ge(s["mod_loaded"], at(i, 16 * MODS, 16 * MODS))
                            last = nc.tensor.matmul(bank[7][0:2, :], g.silu[:, n, :], mod_slab[:, n, :], start=(n == 0),
                                                    stop=(n == NB - 1))
                            if n == NB - 1:
                                last.then_inc(s["mod_done"], 1)
                    pe.wait_ge(s["y_in"], at(i, 3, 3))
                    head_sums(os_, bank[0][:, :], bank[1][:, 0:CTX]).then_inc(s["means"], 1)
                    pe.wait_ge(s["s0_ready"], at(i, STEPS, STEPS))
                    pe.wait_ge(s["s1_ready"], at(i, STEPS, STEPS))
                    if more:
                        pe.wait_ge(s["in_loaded"], at(i, 64, 128))
                        project_rate(0, 0)
                        project_rate(1, 0)
                    pe.wait_ge(s["y_squares"], at(i, 1, 1))
                    head_sums(sq, bank[0][:, :], bank[1][:, 0:CTX]).then_inc(s["vars"], 1)
                    if more:
                        pe.wait_ge(s["y_root"], at(i, 1, 1))
                        if MODS:
                            pe.wait_ge(s["mod_added"], at(i, 1, 1))
                        project_rest()

                with pe.Fori(0, NB - 1) as i:
                    block_(i, True)
                block_(NB - 1, False)

            @block.vector
            def _(dve):
                dve.sem_inc(s["y_ready"], 1)
                with dve.Fori(0, NB) as i:
                    link = Link(dve, s["link"], i, LINKS_RW)
                    dve.wait_ge(s["in_loaded"], at(i, 64, 64))
                    dve.wait_ge(s["y_ready"], at(i, 1, 1))
                    nc.vector.tensor_copy(gn[:, :], hw[:, 3 * P + W_GG:3 * P + W_GB + 1]).then_inc(s["gains"], 1)
                    link(nc.vector.tensor_scalar(t1[:, :], k, hcol(W_KK), None, ALU.mult))
                    nc.vector.tensor_tensor(sq[:, :], t1[:, :], t1[:, :], ALU.mult).then_inc(s["squares"], 1)
                    dve.wait_ge(s["sig_w"], at(i, 2, 2))
                    nc.vector.tensor_tensor_scan(flat(gc), g.const[:, K_SCAN:K_SCAN + TT], flat(ld), 0.0,
                                                 ALU.mult, ALU.add).then_inc(s["scanned"], 1)
                    dve.wait_ge(s["scanned"], at(i, 1, 1))
                    nc.vector.tensor_tensor(flat(ld), flat(gc), flat(ld), ALU.subtract).then_inc(s["g_before"], 1)
                    dve.wait_ge(s["sig_a"], at(i, 2, 2))
                    link(nc.vector.tensor_scalar(flat(kd), flat(icl), -1.0, hcol(W_KA), ALU.add, ALU.mult))
                    for both, plain in by_direction(kd, k):
                        last = nc.vector.scalar_tensor_tensor(both, both, 1.0, plain, ALU.add, ALU.mult)
                    link(last)
                    for us in (slice(0, NLAT), slice(NLAT, NCHUNK)):
                        last = nc.vector.tensor_tensor(chunked(bs[:, :])[:, us, :], kd[:, us, 0, :],
                                                       kd[:, us, 1, :][:, ::-1, ::-1], ALU.add)
                    last.then_inc(s["keys"], 1)
                    dve.wait_ge(s["keys"], at(i, 1, 1))
                    nc.vector.scalar_tensor_tensor(bs[:, :], r, hcol(W_RK), bs[:, :], ALU.mult, ALU.mult).then_inc(s["bonus_in"], 1)
                    dve.wait_ge(s["roots"], at(i, 1, 1))
                    link(nc.vector.reciprocal(rn[:, :], rn[:, :]))
                    for (both, plain), (_, root) in zip(by_direction(kk, t1[:, :]), by_direction(kk, rn[:, :])):
                        last = nc.vector.tensor_tensor(both, plain, root, ALU.mult)
                    link(last)
                    dve.wait_ge(s["bonus_sums"], at(i, 1, 1))
                    nc.vector.tensor_tensor(bon[:, S_LAT], bank[6][:, :], v[:, S_LAT], ALU.mult)
                    nc.vector.tensor_tensor(bon[:, S_CTX], bank[7][:, 0:CTX], v[:, S_CTX], ALU.mult).then_inc(s["bonus"], 1)
                    link(nc.vector.tensor_tensor(flat(bt), flat(kk), flat(icl), ALU.mult))
                    dve.wait_ge(s["exps"], at(i, 3, 3))
                    nc.vector.scalar_tensor_tensor(flat(bt), flat(bt), -1.0, flat(e_inv), ALU.mult,
                                                   ALU.mult).then_inc(s["operands"], 1)
                    nc.vector.tensor_tensor(flat(at_), flat(kk), flat(e_ex), ALU.mult).then_inc(s["operands"], 1)
                    for (both, plain), (decay, _) in zip(by_direction(rt, r), by_direction(e_in, r)):
                        nc.vector.tensor_tensor(both, plain, decay, ALU.mult).then_inc(s["operands"], 1)
                    nc.vector.memset(st[:, :, :, :], 0.0).then_inc(s["operands"], 1)

                    def masks(jg, hh):
                        dve.wait_ge(s["products"], at(i, 2 * NGROUP, 2 * jg + hh + 1))
                        u2 = slice(GROUP * jg + 2 * hh, GROUP * jg + 2 * hh + 2)
                        later = g.mask(K_SP).unsqueeze(1).to_broadcast([P, 2, P])
                        for q, out in enumerate((w.lt[:, jg % 2, 2 * hh:2 * hh + 2, :], ak[:, u2, :])):
                            cols = bank[4 + 2 * hh][:, q * 2 * P:(q + 1) * 2 * P].rearrange("p (n c) -> p n c", n=2)
                            nc.vector.tensor_tensor(out, cols, later, ALU.mult).then_inc(s["masked"], 1)
                        nc.vector.tensor_tensor(rr[:, :, u2, :],
                                                bank[5 + 2 * hh][:, :].rearrange("p (q n c) -> p q n c", q=2, n=2),
                                                g.mask(K_IP).unsqueeze(1).unsqueeze(1).to_broadcast([P, 2, 2, P]),
                                                ALU.mult).then_inc(s["masked"], 1)

                    def first(jg):
                        dve.wait_ge(s["masked"], at(i, 6 * NGROUP, 6 * jg + 6))
                        invert_first_t(nc, g, s, w, jg, link)

                    masks(0, 0)
                    masks(0, 1)
                    first(0)
                    invert_first_n(dve, nc, s, w, i, 0)
                    for jg in range(NGROUP):
                        ahead = {1: lambda: masks(jg + 1, 0), 2: lambda: masks(jg + 1, 1), 3: lambda: first(jg + 1)}
                        ahead = ahead if jg < NGROUP - 1 else {}
                        invert_dve(dve, nc, g, s, w, i, jg, bool(ahead), ahead)
                    for n in range(STEPS):
                        u = ORDER[n]
                        dve.wait_ge(s["chain_x"], at(i, STEPS, n + 1))
                        for e in range(2):
                            er = slice(C * e, C * (e + 1))
                            nc.vector.tensor_copy(xs[er, :, :], bank[0][er, 0:2 * P].rearrange("p (h n) -> p h n", h=2)[:, :, er]
                                                  ).then_inc(s["x_out"], 1)
                        dve.wait_ge(s["chain_sa"], at(i, STEPS, n + 1))
                        nc.vector.tensor_tensor(saz[:, :, :, :].rearrange("p h e v -> p h (e v)"),
                                                bank[1][:, 0:2 * P].rearrange("p (h n) -> p h n", h=2),
                                                g.mask(K_BO).unsqueeze(1).to_broadcast([P, 2, P]), ALU.mult).then_inc(s["saz_out"], 1)
                        if n >= 1:
                            dve.wait_ge(s["o_done"], at(i, STEPS, n))
                        nc.vector.tensor_copy(sa[:, :, :], bank[1][:, 0:2 * P].rearrange("p (h n) -> p h n", h=2)[:, :, 0:C]
                                              ).then_inc(s["sa_out"], 1)
                        dve.wait_ge(s["chain_s"], at(i, STEPS, n + 1))
                        for e in range(2):
                            last = nc.vector.tensor_scalar(st[C:P, e, 1, :], bank[2][C:P, e * C:(e + 1) * C],
                                                           e_in[C:P, u, e, C - 1:C], None, ALU.mult)
                        if n != 1:
                            last.then_inc(s["s1_ready"], 1)
                            continue
                        link(last)
                        dve.wait_ge(s["s_first"], at(i, 1, 1))
                        dve.wait_ge(s["o_done"], at(i, STEPS, 2))
                        dve.wait_ge(s["state_stored"], at(i, 16, 16))
                        dve.wait_ge(s["s0_loaded"], at(i, 16, 16))
                        for hh in range(2):
                            hr = slice(C * hh, C * (hh + 1))
                            nc.vector.tensor_copy(sout[hr, :, :], st[hr, :, hh, :]).then_inc(s["s_saved"], 1)
                        dve.wait_ge(s["s_saved"], at(i, 2, 2))
                        for hh, done in enumerate((s["s0_ready"], s["s1_ready"])):
                            hr = slice(C * hh, C * (hh + 1))
                            nc.vector.tensor_copy(st[hr, :, hh, :], s0[hr, :, :]).then_inc(done, 1)
                    dve.wait_ge(s["o_done"], at(i, STEPS, STEPS))
                    dve.wait_ge(s["y_stored"], at(i, 16, 16))
                    tiles = lambda b, m: bank[b][:, 0:m * P].rearrange("p (u e c) -> p u e c", u=m, e=2)
                    spans = ((4, 4, 0, 2 * P), (5, 4, 2 * P, 4 * P), (6, 2, LAT, T))
                    turned = ((4, 4, 2 * P, 4 * P), (5, 4, 0, 2 * P), (6, 2, LAT, T))
                    for b, m, t0, t1_ in spans:
                        last = nc.vector.tensor_copy(chunked(os_[:, t0:t1_]), tiles(b, m)[:, :, 0, :])
                    link(last)
                    for b, m, t0, t1_ in turned:
                        out = chunked(os_[:, t0:t1_])
                        nc.vector.tensor_tensor(out, tiles(b, m)[:, ::-1, 1, ::-1], out, ALU.add).then_inc(s["y_in"], 1)
                    if MODS:
                        dve.wait_ge(s["mod_cols"], at(i, 1, 1))
                        here = bass.ds(i * (MODS * MOD_BLOCKS) + first_slab * MOD_BLOCKS, MODS * MOD_BLOCKS)
                        for c in range(2):
                            last = nc.vector.tensor_tensor(g.mods[:, here, c:c + 1].rearrange("p n o -> p (n o)"),
                                                           bank[3][:, c:2 * MODS * MOD_BLOCKS:2], g.bmod[:, here], ALU.add)
                        last.then_inc(s["mod_added"], 1)
                    dve.wait_ge(s["means"], at(i, 1, 1))
                    nc.vector.scalar_tensor_tensor(os_[:, S_LAT], bank[0][:, :], -1.0 / C, os_[:, S_LAT], ALU.mult, ALU.add)
                    nc.vector.scalar_tensor_tensor(os_[:, S_CTX], bank[1][:, 0:CTX], -1.0 / C, os_[:, S_CTX],
                                                   ALU.mult, ALU.add).then_inc(s["y_centred"], 1)
                    dve.wait_ge(s["y_centred"], at(i, 1, 1))
                    nc.vector.scalar_tensor_tensor(sq[:, :], os_[:, :], 1.0 / C, os_[:, :], ALU.mult,
                                                   ALU.mult).then_inc(s["y_squares"], 1)
                    dve.wait_ge(s["y_root"], at(i, 1, 1))
                    link(nc.vector.reciprocal(rn[:, :], rn[:, :]))
                    link(nc.vector.scalar_tensor_tensor(os_[:, :], os_[:, :], gn[:, 0:1], rn[:, :], ALU.mult, ALU.mult))
                    dve.wait_ge(s["bias_in"], at(i, 1, 1))
                    link(nc.vector.tensor_tensor(os_[:, :], os_[:, :], bon[:, :], ALU.add))
                    nc.vector.tensor_tensor(os_[:, :], os_[:, :], gate[:, :], ALU.mult).then_inc(s["y_ready"], 1)
                    link.end()
                if MODS:
                    dve.wait_ge(s["mod_added"], NB)
                    scales_plus_one(nc, g, mod_layers)


LINKS_RW = 10 + 2 * NGROUP + 1



KEYS = P + T
KT_LAT, KT_CTX = slice(0, P + LAT), slice(P + LAT, KEYS)
QTILES = T // P
KTILES = KEYS // P
GROUPS = AT_HEADS // AT_KV
A_GAIN, A_COLS = 0, 2
TILES = GROUPS * QTILES


def normed_rotated(nc, g):
    NQK = 10
    names = ["passed", "const", "loaded:2", "squares", "sums", "root", "normed", "swapped", "link", "link_first", "done", "stored:2", "cache"]
    with buffers(nc) as (sb, banks), phase(nc, *names) as s:
        qb, sq, rn, out = (sb(n, 2, T) for n in ("qk", "sq", "rn", "out"))
        gain = sb("gain", 2, 1)
        tab, perm = sb("rope", 2, T), sb("perm", P)
        bank = banks(8)
        ss = [(bank[2 * b], bank[2 * b + 1]) for b in range(2)]
        sw = [(bank[4 + 2 * b], bank[5 + 2 * b]) for b in range(2)]
        with nc.Block() as block:

            @block.sync
            def _(sp):
                sp.dma_start(tab[:, :, :], g.d["rope_t"]).then_inc(s["const"], 16)
                sp.dma_start(perm[:, :], g.d["rope_perm"]).then_inc(s["const"], 16)
                def load(n, b):
                    sp.dma_start(qb[:, b, :], slab(g.d["qkv"], n)).then_inc(s["loaded"][b], 16)
                    sp.dma_start(gain[:, b, :], slab(g.d["at_gain"], n)).then_inc(s["loaded"][b], 16)

                def store(n, b):
                    sp.dma_start(slab(g.d["qk_rot"], n), out[:, b, :]).then_inc(s["stored"][b], 16)

                for b in range(2):
                    sp.sem_inc(s["stored"][b], 16)
                    load(b, b)
                with sp.Fori(0, NQK // 2 - 1) as i:
                    for b in range(2):
                        wait_alone(sp, s["done"], at(i, 2, b + 1), s["passed"])
                        store(i * 2 + b, b)
                        load(i * 2 + (b + 2), b)
                for b in range(2):
                    sp.wait_ge(s["done"], NQK - 1 + b)
                    store(NQK - 2 + b, b)
                for b in range(2):
                    sp.wait_ge(s["stored"][b], 16 * (NQK // 2 + 1))
                for b in range(2):
                    sp.dma_start(g.d["kv_out"][b], g.d["qk_rot"][8 + b, :, S_CTX]).then_inc(s["cache"], 16)
                    sp.dma_start(g.d["kv_out"][2 + b], g.d["qkv"][10 + b, :, S_CTX]).then_inc(s["cache"], 16)
                sp.wait_ge(s["cache"], 64)

            @block.scalar
            def _(act):
                with act.Fori(0, NQK // 2) as i:
                    for b in range(2):
                        act.wait_ge(s["loaded"][b], at(i, 32, 32))
                        nc.scalar.activation(sq[:, b, :], qb[:, b, :], ACT.Square).then_inc(s["squares"], 1)
                        act.wait_ge(s["sums"], at(i, 2, b + 1))
                        lat, ctx = ss[b]
                        nc.scalar.activation(rn[:, b, S_LAT], lat[:, :], ACT.Sqrt, bias=g.eps_nrm, scale=1.0 / HD)
                        nc.scalar.activation(rn[:, b, S_CTX], ctx[:, 0:CTX], ACT.Sqrt, bias=g.eps_nrm,
                                             scale=1.0 / HD).then_inc(s["root"], 1)

            @block.tensor
            def _(pe):
                def sums(i, b):
                    pe.wait_ge(s["squares"], at(i, 2, b + 1))
                    lat, ctx = ss[b % 2]
                    nc.tensor.matmul(lat[:, :], g.mask(K_BO), sq[:, b % 2, S_LAT], start=True, stop=True)
                    nc.tensor.matmul(ctx[:, 0:CTX], g.mask(K_BO), sq[:, b % 2, S_CTX], start=True, stop=True).then_inc(s["sums"], 1)

                def pair(i, more):
                    for b in range(2):
                        if b == 0 or more:
                            sums(i, b + 1)
                        pe.wait_ge(s["normed"], at(i, 2, b + 1))
                        lat, ctx = sw[b]
                        nc.tensor.matmul(lat[:, :], perm[:, :], qb[:, b, S_LAT], start=True, stop=True)
                        nc.tensor.matmul(ctx[:, 0:CTX], perm[:, :], qb[:, b, S_CTX], start=True, stop=True).then_inc(s["swapped"], 1)

                pe.wait_ge(s["const"], 32)
                sums(0, 0)
                with pe.Fori(0, NQK // 2 - 1) as i:
                    pair(i, True)
                pair(NQK // 2 - 1, False)

            @block.vector
            def _(dve):
                dve.wait_ge(s["const"], 32)
                with dve.Fori(0, NQK // 2) as i:
                    link = Link(dve, s["link"], i, 6)
                    for b in range(2):
                        dve.wait_ge(s["root"], at(i, 2, b + 1))
                        link(nc.vector.reciprocal(rn[:, b, :], rn[:, b, :]))
                        nc.vector.scalar_tensor_tensor(qb[:, b, :], qb[:, b, :], gain[:, b, 0:1], rn[:, b, :], ALU.mult,
                                                       ALU.mult).then_inc(s["normed"], 1)
                        dve.wait_ge(s["normed"], at(i, 2, b + 1))
                        dve.wait_ge(s["stored"][b], at(i, 16, 16))
                        link(nc.vector.tensor_tensor(out[:, b, :], qb[:, b, :], tab[:, 0, :], ALU.mult))
                        dve.wait_ge(s["swapped"], at(i, 2, b + 1))
                        nc.vector.tensor_tensor(rn[:, b, S_LAT], sw[b][0][:, :], tab[:, 1, S_LAT], ALU.mult)
                        link(nc.vector.tensor_tensor(rn[:, b, S_CTX], sw[b][1][:, 0:CTX], tab[:, 1, S_CTX], ALU.mult))
                        nc.vector.tensor_tensor(out[:, b, :], out[:, b, :], rn[:, b, :], ALU.add).then_inc(s["done"], 1)
                    link.end()


def attention_heads(nc, g):
    normed_rotated(nc, g)
    SCALE = HD ** -0.5
    names = ["passed", "loaded", "v_ps", "v_out", "scores", "link", "negmax", "exps", "diag", "pt_ps", "pt_out", "o_ps",
             "o_out", "stored"]
    with buffers(nc) as (sb, banks), phase(nc, *names) as s:
        kt, vt, vtok = sb("kt", KEYS), sb("vt", T), sb("vtok", KTILES, HD)
        q4, o4 = sb("q4", GROUPS, T), sb("o4", GROUPS, T)
        pb, pt = sb("probs", 2, P + LAT), sb("probs_t", 2, QTILES, P)
        dg = sb("diag", 2, P)
        mx, rsum = sb("mx", TILES), sb("rsum", TILES)
        with ExitStack() as stack:
            sc = [stack.enter_context(nc.psum_tensor(unique("scores"), [P, 2, 512], F32)) for _ in range(2)]
            tp = stack.enter_context(nc.psum_tensor(unique("probs_t"), [P, 2, 512], F32))
            ob = [stack.enter_context(nc.psum_tensor(unique("ob"), [P, 512], F32)) for _ in range(2)]
            vb = ob[1]
            tiles = [(h, q) for h in range(GROUPS) for q in range(QTILES)]
            flat = lambda t: t[:, :, :].rearrange("p a b -> p (a b)")

            def keys_of(q):
                return (KT_LAT, range(0, KTILES - 1)) if q < QTILES - 1 else (KT_CTX, range(KTILES - 1, KTILES))

            with nc.Block() as block:

                @block.sync
                def _(sp):
                    sp.sem_inc(s["stored"], 16)
                    with sp.Fori(0, AT_KV) as i:
                        wait_alone(sp, s["stored"], at(i, 16, 16), s["passed"])
                        sp.dma_start(kt[0:HD, 0:P], slab(g.d["cache_kt"], i)).then_inc(s["loaded"], 16)
                        sp.dma_start(kt[0:HD, P:KEYS], slab(g.d["qk_rot_heads"], i + AT_HEADS)).then_inc(s["loaded"], 16)
                        sp.dma_start(vt[0:HD, :], slab(g.d["qkv_heads"], i + (AT_HEADS + AT_KV))).then_inc(s["loaded"], 16)
                        sp.dma_start(vtok[:, 0, :], slab(g.d["cache_v_tok"], i)).then_inc(s["loaded"], 16)
                        sp.dma_start(q4[0:HD, :, :], g.d["qk_rot_heads"][bass.ds(i * GROUPS, GROUPS)]
                                     .rearrange("h c t -> c h t")).then_inc(s["loaded"], 16)
                        wait_alone(sp, s["o_out"], at(i, TILES, TILES), s["passed"])
                        sp.dma_start(g.d["mixed_heads"][bass.ds(i * GROUPS, GROUPS)].rearrange("h c t -> c h t"),
                                     o4[0:HD, :, :]).then_inc(s["stored"], 16)
                    sp.wait_ge(s["stored"], 16 * (AT_KV + 1))

                @block.tensor
                def _(pe):
                    def scores(i, n):
                        h, q = tiles[n]
                        cols, _ = keys_of(q)
                        if n >= 2:
                            pe.wait_ge(s["exps"], at(i, TILES, n - 1))
                        qs = q4[0:HD, h, q * P:(q + 1) * P]
                        out = sc[n % 2]
                        if q < QTILES - 1:
                            nc.tensor.matmul(out[:, 0, :], qs, kt[0:HD, 0:512], start=True, stop=True)
                            nc.tensor.matmul(out[:, 1, 0:P], qs, kt[0:HD, 512:P + LAT], start=True,
                                             stop=True).then_inc(s["scores"], 1)
                        else:
                            nc.tensor.matmul(out[:, 0, 0:P], qs, kt[0:HD, cols], start=True, stop=True).then_inc(s["scores"], 1)

                    with pe.Fori(0, AT_KV) as i:
                        wait_alone(pe, s["loaded"], at(i, 80, 80), s["passed"])
                        for n in range(QTILES):
                            last = nc.tensor.transpose(vb[:, n * HD:(n + 1) * HD], vt[0:HD, n * P:(n + 1) * P],
                                                       g.const[0:HD, K_ID:K_ID + HD])
                        last.then_inc(s["v_ps"], 1)
                        def values(n):
                            _, kts = keys_of(tiles[n][1])
                            pe.wait_ge(s["pt_out"], at(i, TILES, n + 1))
                            if n == 0:
                                pe.wait_ge(s["v_out"], at(i, 1, 1))
                            elif n >= 2:
                                pe.wait_ge(s["o_out"], at(i, TILES, n - 1))
                            for m, key in enumerate(kts):
                                last = nc.tensor.matmul(ob[n % 2][0:HD, 0:P], vtok[:, key, :], pt[:, n % 2, m, :],
                                                        start=(m == 0), stop=(m == len(kts) - 1))
                            last.then_inc(s["o_ps"], 1)

                        scores(i, 0)
                        for n, (h, q) in enumerate(tiles):
                            if n + 1 < TILES:
                                scores(i, n + 1)
                            if n >= 1:
                                values(n - 1)
                            pe.wait_ge(s["diag"], at(i, TILES, n + 1))
                            _, kts = keys_of(q)
                            for m in range(len(kts)):
                                last = nc.tensor.matmul(flat(tp)[:, m * P:(m + 1) * P], pb[:, n % 2, m * P:(m + 1) * P],
                                                        dg[:, n % 2, :], start=True, stop=True)
                            last.then_inc(s["pt_ps"], 1)
                        values(TILES - 1)

                @block.scalar
                def _(act):
                    with act.Fori(0, AT_KV) as i:
                        act.wait_ge(s["v_ps"], at(i, 1, 1))
                        nc.scalar.copy(vtok[:, 1:KTILES, :].rearrange("p k c -> p (k c)"),
                                       vb[:, 0:QTILES * HD]).then_inc(s["v_out"], 1)

                        def transposed_out(n):
                            width = P * len(keys_of(tiles[n][1])[1])
                            act.wait_ge(s["pt_ps"], at(i, TILES, n + 1))
                            if n >= 2:
                                act.wait_ge(s["o_ps"], at(i, TILES, n - 1))
                            nc.scalar.copy(pt[:, n % 2, :, :].rearrange("p a b -> p (a b)")[:, 0:width],
                                           flat(tp)[:, 0:width]).then_inc(s["pt_out"], 1)

                        for n, (h, q) in enumerate(tiles):
                            width = P * len(keys_of(q)[1])
                            act.wait_ge(s["negmax"], at(i, TILES, n + 1))
                            if n >= 2:
                                act.wait_ge(s["pt_ps"], at(i, TILES, n - 1))
                            nc.scalar.activation(pb[:, n % 2, 0:width], flat(sc[n % 2])[:, 0:width], ACT.Exp, scale=SCALE,
                                                 bias=mx[:, n:n + 1], accum_out=rsum[:, n:n + 1]).then_inc(s["exps"], 1)
                            if n >= 1:
                                transposed_out(n - 1)
                        transposed_out(TILES - 1)

                @block.vector
                def _(dve):
                    with dve.Fori(0, AT_KV) as i:
                        link = Link(dve, s["link"], i, 2 * TILES)

                        def maximum(n):
                            width = P * len(keys_of(tiles[n][1])[1])
                            dve.wait_ge(s["scores"], at(i, TILES, n + 1))
                            link(nc.vector.reduce_max(mx[:, n:n + 1], flat(sc[n % 2])[:, 0:width], AX.X))
                            nc.vector.tensor_scalar(mx[:, n:n + 1], mx[:, n:n + 1], -SCALE, None, ALU.mult).then_inc(s["negmax"], 1)

                        def output(n):
                            hn, qn = tiles[n]
                            dve.wait_ge(s["o_ps"], at(i, TILES, n + 1))
                            nc.vector.tensor_copy(o4[0:HD, hn, qn * P:(qn + 1) * P], ob[n % 2][0:HD, 0:P]).then_inc(s["o_out"], 1)

                        maximum(0)
                        for n in range(TILES):
                            if n + 1 < TILES:
                                maximum(n + 1)
                            dve.wait_ge(s["exps"], at(i, TILES, n + 1))
                            link(nc.vector.reciprocal(rsum[:, n:n + 1], rsum[:, n:n + 1]))
                            if n >= 2:
                                dve.wait_ge(s["pt_ps"], at(i, TILES, n - 1))
                            nc.vector.tensor_scalar(dg[:, n % 2, :], g.ident, rsum[:, n:n + 1], None, ALU.mult).then_inc(s["diag"], 1)
                            if n >= 2:
                                output(n - 2)
                        output(TILES - 2)
                        output(TILES - 1)
                        link.end()



R_G, R_EG, R_B, R_EL = 0, TT, 2 * TT, 3 * TT
R_END = 3 * TT + 2 * NCHUNK
C_G, C_NBEG, C_B, C_ED = 0, NCHUNK, 2 * NCHUNK, 3 * NCHUNK
C_END = 4 * NCHUNK
N_COLS = 10


def delta_gates(nc, g):
    names = ["passed", "w_loaded", "mm_done", "out", "raw_stored", "raw_loaded", "link", "exps", "rate", "sums", "decays", "scaled",
             "cols_ps", "cols_out", "stored"]
    H8 = slice(0, DN_HEADS)
    with buffers(nc) as (sb, banks), phase(nc, *names) as s:
        wg, raw, small = sb("wg", NB, 4 * DN_HEADS), sb("raw", T), sb("small", 4)
        ab = sb("ab", 2, 2, T)
        tmp = sb("tmp", 2, T)
        rows = sb("rows", R_END)
        nb, ed = sb("neg_beta_decay", TT), sb("to_end", TT)
        cols = sb("cols", DN_HEADS, C_END)
        rate = sb("rate", 2)
        bank = banks(4)
        pairs = lambda r0: rows[H8, r0:r0 + TT].rearrange("p (u e c) -> p u e c", u=NCHUNK, e=2)
        with nc.Block() as block:

            @block.sync
            def _(sp):
                sp.dma_start(wg[:, :, :].rearrange("p k n -> p (k n)"), g.d["dn_wgate"]).then_inc(s["w_loaded"], 16)
                sp.dma_start(small[H8, :], g.d["dn_small"]).then_inc(s["w_loaded"], 16)
                sp.wait_ge(s["out"], 1)
                sp.dma_start(g.d["dn_gates"].rearrange("a e h t -> (a e h) t"), raw[0:4 * DN_HEADS, :]).then_inc(s["raw_stored"], 16)
                sp.wait_ge(s["raw_stored"], 16)
                for a in range(2):
                    sp.dma_start(ab[H8, a, :, :], g.d["dn_gates"][a].rearrange("e h t -> h e t")).then_inc(s["raw_loaded"], 16)
                sp.wait_ge(s["cols_out"], 8)
                for h in range(DN_HEADS):
                    sp.dma_start(g.d["dn_cols"][h], cols[:, h, :]).then_inc(s["stored"], 16)
                sp.dma_start(g.d["dn_rows"], rows[H8, :]).then_inc(s["stored"], 16)
                sp.wait_ge(s["stored"], 16 * (DN_HEADS + 1))

            @block.tensor
            def _(pe):
                pe.wait_ge(s["w_loaded"], 32)
                for k in range(NB):
                    nc.tensor.matmul(bank[0][0:4 * DN_HEADS, :], wg[:, k, :], g.h[:, k, H_LAT], start=(k == 0), stop=(k == NB - 1))
                    last = nc.tensor.matmul(bank[1][0:4 * DN_HEADS, 0:CTX], wg[:, k, :], g.h[:, k, H_CTX],
                                            start=(k == 0), stop=(k == NB - 1))
                last.then_inc(s["mm_done"], 1)
                pe.wait_ge(s["scaled"], 4)
                for n, src in enumerate((rows[H8, R_G:R_G + TT], nb[H8, :], rows[H8, R_B:R_B + TT], ed[H8, :])):
                    if n >= 1:
                        pe.wait_ge(s["cols_out"], 2 * n)
                    for u in range(NCHUNK):
                        last = nc.tensor.transpose(bank[2 + n % 2][:, u * DN_HEADS:(u + 1) * DN_HEADS], src[:, u * P:(u + 1) * P],
                                                   g.ident[H8, H8])
                    last.then_inc(s["cols_ps"], 1)

            @block.scalar
            def _(act):
                act.wait_ge(s["mm_done"], 1)
                nc.scalar.copy(raw[0:4 * DN_HEADS, S_LAT], bank[0][0:4 * DN_HEADS, :])
                nc.scalar.copy(raw[0:4 * DN_HEADS, S_CTX], bank[1][0:4 * DN_HEADS, 0:CTX]).then_inc(s["out"], 1)
                act.wait_ge(s["rate"], 1)
                nc.scalar.activation(tmp[H8, :, :], tmp[H8, :, :], ACT.Exp, scale=-1.0).then_inc(s["exps"], 1)
                nc.scalar.activation(rate[H8, :], small[H8, 0:2], ACT.Exp).then_inc(s["exps"], 1)
                act.wait_ge(s["exps"], 1)
                nc.scalar.activation(tmp[H8, :, :], tmp[H8, :, :], ACT.Ln, bias=g.const[H8, K_ONE:K_ONE + 1]).then_inc(s["exps"], 1)
                nc.scalar.activation(ab[H8, 1, :, :], ab[H8, 1, :, :], ACT.Sigmoid).then_inc(s["exps"], 1)
                act.wait_ge(s["sums"], 1)
                nc.scalar.activation(rows[H8, R_EG:R_EG + TT], rows[H8, R_G:R_G + TT], ACT.Exp).then_inc(s["decays"], 1)
                nc.scalar.activation(rows[H8, R_EL:R_END].rearrange("p (u e) -> p u e", e=2), pairs(R_G)[:, :, :, C - 1],
                                     ACT.Exp).then_inc(s["decays"], 1)
                act.wait_ge(s["sums"], 2)
                nc.scalar.activation(ed[H8, :], ed[H8, :], ACT.Exp).then_inc(s["scaled"], 1)
                for n in range(4):
                    act.wait_ge(s["cols_ps"], n + 1)
                    nc.scalar.copy(cols[:, :, n * NCHUNK:(n + 1) * NCHUNK].rearrange("p h u -> p u h"),
                                   bank[2 + n % 2][:, 0:NCHUNK * DN_HEADS].rearrange("p (u h) -> p u h", h=DN_HEADS)).then_inc(s["cols_out"], 2)

            @block.vector
            def _(dve):
                link = Link(dve, s["link"])
                dve.wait_ge(s["raw_loaded"], 32)
                dve.wait_ge(s["w_loaded"], 32)
                for e in range(2):
                    last = nc.vector.tensor_scalar(ab[H8, 0, e, :], ab[H8, 0, e, :], small[H8, 2 + e:3 + e], None, ALU.add)
                link(last)
                link(nc.vector.tensor_scalar(tmp[H8, :, :], ab[H8, 0, :, :], -1.0, None, ALU.mult))
                nc.vector.tensor_tensor(tmp[H8, :, :], tmp[H8, :, :], ab[H8, 0, :, :], ALU.max).then_inc(s["rate"], 1)
                dve.wait_ge(s["exps"], 4)
                link(nc.vector.scalar_tensor_tensor(ab[H8, 0, :, :], ab[H8, 0, :, :], 0.0, tmp[H8, :, :], ALU.max, ALU.add))
                for e in range(2):
                    last = nc.vector.tensor_scalar(ab[H8, 0, e, :], ab[H8, 0, e, :], rate[H8, e:e + 1], -1.0, ALU.mult, ALU.mult)
                link(last)
                flat_nb = nb[H8, :].rearrange("p (u e c) -> p u e c", u=NCHUNK, e=2)
                for a, out in ((0, flat_nb), (1, pairs(R_B))):
                    for us, ts in ((slice(0, NLAT), S_LAT), (slice(NLAT, NCHUNK), S_CTX)):
                        nc.vector.tensor_copy(out[:, us, 0, :], chunked(ab[H8, a, 0, ts]))
                        last = nc.vector.tensor_copy(out[:, us, 1, :], chunked(ab[H8, a, 1, ts][:, ::-1]))
                link(last)
                nc.vector.tensor_tensor_scan(rows[H8, R_G:R_G + TT], g.const[H8, K_SCAN:K_SCAN + TT], nb[H8, :], 0.0,
                                             ALU.mult, ALU.add).then_inc(s["sums"], 1)
                dve.wait_ge(s["sums"], 1)
                nc.vector.tensor_tensor(ed[H8, :].rearrange("p (n c) -> p n c", c=C),
                                        rows[H8, R_G:R_G + TT].rearrange("p (n c) -> p n c", c=C)[:, :, C - 1:C]
                                        .to_broadcast([DN_HEADS, 2 * NCHUNK, C]),
                                        rows[H8, R_G:R_G + TT].rearrange("p (n c) -> p n c", c=C), ALU.subtract).then_inc(s["sums"], 1)
                dve.wait_ge(s["decays"], 2)
                nc.vector.scalar_tensor_tensor(nb[H8, :], rows[H8, R_EG:R_EG + TT], -1.0, rows[H8, R_B:R_B + TT],
                                               ALU.mult, ALU.mult).then_inc(s["scaled"], 3)


def delta_heads(nc, g):
    D_SCALE = P ** -0.5
    names = ["passed", "taps_loaded", "x_loaded", "r_loaded", "c_loaded", "z_loaded", "taps", "silu", "link", "conv", "conv_sig", "link_a", "first", "squares", "sums", "root", "operands", "differ", "decay",
             "prepared", "masks", "products", "masked", "tokens", "tokens_out", "chain_y", "tmp_out", "chain_v", "v_out",
             "chain_s", "s_out", "o_ps", "o_out", "state_stored", "y_squares", "y_sums", "y_root", "z_sig", "y_ready",
             "y_stored"] + INVERSE_SEMS
    with buffers(nc) as (sb, banks), phase(nc, *names) as s:
        w = Work()
        xin, cv, cs, z = sb("xin", 3, HW), sb("cv", 3, HW), sb("cs", 3, T), sb("z", 2, T)
        rows, el, hcols, fcols = sb("rows", 3 * TT), sb("el", 2, 2 * NCHUNK), sb("hcols", 2, C_END), sb("fcols", 2, N_COLS)
        taps = sb("taps", DN_HEADS // 2, 2 * N_COLS)
        k2, q2, qd, ve = (sb(n, 2, NCHUNK, P) for n in ("k2", "q2", "qd", "ve"))
        dm, di = sb("dm", 2, NCHUNK, P), sb("di", 2, NCHUNK, P)
        w.lt, w.xx, w.y = sb("lt", 2, GROUP, P), sb("xx", 2, 2, 2, P), sb("y", 2, 2, P)
        w.tt, qk = sb("tt", 2 * NCHUNK, P), sb("qk", 2 * NCHUNK, P)
        sq, rn = sb("sq", 2, T), sb("rn", 2, T)
        w.x0 = [sq[:, h, 0:4 * P].rearrange("p (t n c) -> p t n c", t=2, n=2) for h in range(2)]
        tmp, vn, st = sb("tmp", 2, P), sb("vn", 2, P), sb("state", 2, 2, P)
        spare = g.h[:, :, :].rearrange("p b t -> p (b t)")
        kdec = spare[:, 0:2 * TT].rearrange("p (n c) -> p n c", c=P)
        vtok = spare[:, 2 * TT:4 * TT].rearrange("p (n c) -> p n c", c=P)
        os_ = ve
        bank = banks(8)
        w.y_bank, w.x_bank = bank[2:4], bank[6:8]
        split = lambda buf, hh: buf[:, hh, :, :].rearrange("p u (e c) -> p u e c", e=2)
        row = lambda r0: rows[:, r0:r0 + TT].rearrange("p (u n) -> p u n", n=P)
        NI = DN_HEADS // 2
        with nc.Block() as block:

            @block.sync
            def _(sp):
                def load_x(n, hh):
                    for m in range(3):
                        blk = n * 2 + (m * NB + hh)
                        sp.dma_start(xin[:, m, H_LAT], slab(g.d["dn_lat"], blk)).then_inc(s["x_loaded"], 16)
                        sp.dma_start(xin[:, m, H_CTX], slab(g.d["dn_ctx"], blk)).then_inc(s["x_loaded"], 16)

                def load_rows(n, hh):
                    sp.dma_start(rows[:, :], g.d["dn_rows"][bass.ds(n * 2 + hh, 1), 0:3 * TT].to_broadcast([P, 3 * TT])
                                 ).then_inc(s["r_loaded"], 16)

                def load_columns(n):
                    for hh in range(2):
                        sp.dma_start(el[:, hh, :], g.d["dn_rows"][bass.ds(n * 2 + hh, 1), R_EL:R_END].to_broadcast([P, 2 * NCHUNK])
                                     ).then_inc(s["c_loaded"], 16)
                        sp.dma_start(hcols[:, hh, :], slab(g.d["dn_cols"], n * 2 + hh)).then_inc(s["c_loaded"], 16)

                def heads_pass(i, more):
                    wait_alone(sp, s["silu"], at(i, 2, 1), s["passed"])
                    load_x(i, 1)
                    wait_alone(sp, s["y_ready"], at(i, 2, 1), s["passed"])
                    for hh in range(2):
                        sp.dma_start(z[:, hh, :], slab(g.d["dn_proj"], i * 2 + (3 * NB + hh))).then_inc(s["z_loaded"], 16)
                    wait_alone(sp, s["prepared"], at(i, 2, 1), s["passed"])
                    wait_alone(sp, s["masks"], at(i, 4, 2), s["passed"])
                    load_rows(i, 1)
                    if more:
                        wait_alone(sp, s["silu"], at(i, 2, 2), s["passed"])
                        load_x(i + 1, 0)
                        wait_alone(sp, s["prepared"], at(i, 2, 2), s["passed"])
                        wait_alone(sp, s["masks"], at(i, 4, 4), s["passed"])
                        load_rows(i + 1, 0)
                    wait_alone(sp, s["s_out"], at(i, STEPS + 2, 3), s["passed"])
                    sp.dma_start(slab(g.d["dn_state_out"], i), st[:, :, :, :].rearrange("p h e v -> p (h e v)")
                                 ).then_inc(s["state_stored"], 16)
                    wait_alone(sp, s["state_stored"], at(i, 32, 16), s["passed"])
                    sp.dma_start(st[:, :, :, :].rearrange("p h e v -> p (h e v)"), slab(g.d["dn_state"], i)
                                 ).then_inc(s["state_stored"], 16)
                    if more:
                        wait_alone(sp, s["s_out"], at(i, STEPS + 2, STEPS + 2), s["passed"])
                        load_columns(i + 1)
                    for hh in range(2):
                        wait_alone(sp, s["y_ready"], at(i, 2, hh + 2), s["passed"])
                        sp.dma_start(slab(g.d["mixed"], i * 2 + hh), cs[:, hh, :]).then_inc(s["y_stored"], 16)

                sp.sem_inc(s["y_stored"], 32)
                sp.dma_start(taps[:, :, :], g.d["dn_head"].rearrange("i p n -> p i n")).then_inc(s["taps_loaded"], 16)
                load_x(0, 0)
                load_rows(0, 0)
                load_columns(0)
                with sp.Fori(0, NI - 1) as i:
                    heads_pass(i, True)
                heads_pass(NI - 1, False)
                sp.wait_ge(s["state_stored"], 32 * NI)
                sp.wait_ge(s["y_stored"], 32 * (NI + 1))

            @block.gpsimd
            def _(pool):
                with pool.Fori(0, NI) as i:
                    for hh in range(2):
                        wait_alone(pool, s["decay"], at(i, 2, hh + 1), s["passed"])
                        nc.gpsimd.tensor_tensor(dm[:, hh], dm[:, hh], row(R_B), ALU.mult).then_inc(s["masks"], 1)
                        nc.gpsimd.tensor_tensor(di[:, hh], di[:, hh], g.mask(K_IP).unsqueeze(1).to_broadcast([P, NCHUNK, P]),
                                                ALU.mult).then_inc(s["masks"], 1)

            @block.tensor
            def _(pe):
                with pe.Fori(0, NI) as i:
                    for hh in range(2):
                        for n in range(2):
                            pe.wait_ge(s["squares"], at(i, 4, 2 * hh + n + 1))
                            nc.tensor.matmul(bank[2 * n][:, :], g.mask(K_ONE), sq[:, n, S_LAT], start=True, stop=True)
                            nc.tensor.matmul(bank[2 * n + 1][:, 0:CTX], g.mask(K_ONE), sq[:, n, S_CTX],
                                             start=True, stop=True).then_inc(s["sums"], 1)
                    pe.wait_ge(s["operands"], at(i, 2, 2))

                    def products(jg, b):
                        if jg:
                            pe.wait_ge(s["masked"], at(i, 4 * NGROUP, 4 * jg))
                        left, right = ((k2, k2), (k2, q2))[b]
                        for n in range(GROUP):
                            u, hh = 2 * jg + n % 2, n // 2
                            last = nc.tensor.matmul(bank[b][:, n * P:(n + 1) * P], left[:, hh, u, :], right[:, hh, u, :],
                                                    start=True, stop=True)
                        last.then_inc(s["products"], 1)

                    def tokens(jg):
                        if jg:
                            wait_alone(pe, s["tokens_out"], at(i, NGROUP, jg), s["passed"])
                        for b, src in ((4, k2), (5, ve)):
                            for n in range(GROUP):
                                u, hh = 2 * jg + n % 2, n // 2
                                last = nc.tensor.transpose(bank[b][:, n * P:(n + 1) * P], src[:, hh, u, :], g.ident)
                            last.then_inc(s["tokens"], 1)

                    products(0, 0)
                    products(0, 1)
                    tokens(0)
                    for h in range(2):
                        invert_first_pe(pe, nc, g, s, w, i, 0, h)
                    for jg in range(NGROUP):
                        ahead = {0: lambda: products(jg + 1, 0), 1: lambda: products(jg + 1, 1), 2: lambda: tokens(jg + 1)}
                        ahead = ahead if jg < NGROUP - 1 else {}
                        invert_pe(pe, nc, g, s, w, i, jg, bool(ahead), ahead)
                    pe.wait_ge(s["inv_ready"], group_at(i, NGROUP - 1, "inv_ready", 2))
                    pe.wait_ge(s["tokens_out"], at(i, NGROUP, NGROUP))
                    for n in range(STEPS):
                        u = ORDER[n]
                        if n == 2:
                            pe.wait_ge(s["state_stored"], at(i, 32, 32))
                        pe.wait_ge(s["s_out"], at(i, STEPS + 2, n + 1))
                        for hh in range(2):
                            last = nc.tensor.matmul(bank[0][:, hh * 2 * P:(hh + 1) * 2 * P], k2[:, hh, u, :],
                                                    st[:, hh, :, :].rearrange("p e v -> p (e v)"), start=True, stop=True)
                        last.then_inc(s["chain_y"], 1)
                        if n >= 2:
                            pe.wait_ge(s["o_out"], at(i, STEPS, n - 1))
                        ob = bank[4 + n % 2]
                        for hh in range(2):
                            for e in range(2):
                                nc.tensor.matmul(ob[:, hh * P + e * C:hh * P + (e + 1) * C], st[:, hh, e, :],
                                                 qd[:, hh, u, e * C:(e + 1) * C], start=(hh == 0 and e == 0), stop=False,
                                                 skip_group_check=True)
                        pe.wait_ge(s["tmp_out"], at(i, STEPS, n + 1))
                        for hh in range(2):
                            last = nc.tensor.matmul(bank[1][:, hh * P:(hh + 1) * P], w.tt[:, unit(u, hh), :], tmp[:, hh, :],
                                                    start=True, stop=True)
                        last.then_inc(s["chain_v"], 1)
                        pe.wait_ge(s["v_out"], at(i, STEPS, n + 1))
                        for e in range(2):
                            er = slice(C * e, C * (e + 1))
                            for hh in range(2):
                                last = nc.tensor.matmul(bank[2 + e][:, hh * P:(hh + 1) * P], kdec[er, unit(u, hh), :], vn[er, hh, :],
                                                        start=True, stop=True)
                            last.then_inc(s["chain_s"], 1)
                        for hh in range(2):
                            last = nc.tensor.matmul(ob[:, hh * P:(hh + 1) * P], vn[:, hh, :], qk[:, unit(u, hh), :], start=False,
                                                    stop=True, skip_group_check=True)
                        last.then_inc(s["o_ps"], 1)
                    for hh in range(2):
                        pe.wait_ge(s["y_squares"], at(i, 2, hh + 1))
                        nc.tensor.matmul(bank[6 - 6 * hh][:, :], g.mask(K_ONE), sq[:, hh, S_LAT], start=True, stop=True)
                        nc.tensor.matmul(bank[7 - 6 * hh][:, 0:CTX], g.mask(K_ONE), sq[:, hh, S_CTX],
                                         start=True, stop=True).then_inc(s["y_sums"], 1)

            @block.scalar
            def _(act):
                def root(n, done, lat, ctx, scale):
                    nc.scalar.activation(rn[:, n, S_LAT], lat[:, :], ACT.Sqrt, bias=g.eps_nrm, scale=scale)
                    nc.scalar.activation(rn[:, n, S_CTX], ctx[:, 0:CTX], ACT.Sqrt, bias=g.eps_nrm, scale=scale).then_inc(done, 1)

                with act.Fori(0, NI) as i:
                    for hh in range(2):
                        act.wait_ge(s["conv"], at(i, 2, hh + 1))
                        nc.scalar.activation(xin[:, :, 1:HW - 1], cv[:, :, 1:HW - 1], ACT.Sigmoid).then_inc(s["conv_sig"], 1)
                        for n in range(2):
                            act.wait_ge(s["sums"], at(i, 4, 2 * hh + n + 1))
                            root(n, s["root"], bank[2 * n], bank[2 * n + 1], 1.0)
                        act.wait_ge(s["differ"], at(i, 2, hh + 1))
                        nc.scalar.activation(di[:, hh], di[:, hh], ACT.Exp).then_inc(s["link_a"], 1)
                        act.wait_ge(s["link_a"], at(i, 2, hh + 1))
                        nc.scalar.copy(dm[:, hh], di[:, hh]).then_inc(s["decay"], 1)
                    for jg in range(NGROUP):
                        act.wait_ge(s["tokens"], at(i, 2 * NGROUP, 2 * jg + 2))
                        for n in range(GROUP):
                            u, hh = 2 * jg + n % 2, n // 2
                            nc.scalar.activation(kdec[:, GROUP * jg + n, :], bank[4][:, n * P:(n + 1) * P], ACT.Identity,
                                                 scale=hcols[:, hh, C_ED + u:C_ED + u + 1])
                            last = nc.scalar.activation(vtok[:, GROUP * jg + n, :], bank[5][:, n * P:(n + 1) * P], ACT.Identity,
                                                        scale=hcols[:, hh, C_B + u:C_B + u + 1])
                        last.then_inc(s["tokens_out"], 1)
                    for n in range(STEPS):
                        act.wait_ge(s["o_ps"], at(i, STEPS, n + 1))
                        nc.scalar.copy(os_[:, :, ORDER[n], :], bank[4 + n % 2][:, 0:2 * P].rearrange("p (h n) -> p h n", h=2)
                                       ).then_inc(s["o_out"], 1)
                    act.wait_ge(s["z_loaded"], at(i, 32, 32))
                    nc.scalar.activation(cv[:, 0:2, 0:T], z[:, :, :], ACT.Sigmoid).then_inc(s["z_sig"], 1)
                    for hh in range(2):
                        act.wait_ge(s["y_sums"], at(i, 2, hh + 1))
                        root(hh, s["y_root"], bank[6 - 6 * hh], bank[7 - 6 * hh], 1.0 / P)

            @block.vector
            def _(dve):
                link0 = Link(dve, s["first"])
                for edge in (slice(0, 1), slice(H_LAT.stop, H_CTX.start), slice(H_CTX.stop, HW)):
                    link0(nc.vector.memset(xin[:, :, edge], 0.0))
                dve.wait_ge(s["taps_loaded"], 16)
                dve.sem_inc(s["y_ready"], 1)
                with dve.Fori(0, NI) as i:
                    link = Link(dve, s["link"], i, LINKS_DN)
                    dve.wait_ge(s["y_ready"], at(i, 2, 1))
                    nc.vector.tensor_copy(fcols[:, :, :].rearrange("p h n -> p (h n)"),
                                          taps[:, bass.ds(i, 1), :].rearrange("p a n -> p (a n)")).then_inc(s["taps"], 1)
                    dve.wait_ge(s["taps"], at(i, 1, 1))
                    for hh in range(2):
                        dve.wait_ge(s["x_loaded"], at(i, 192, 96 * (hh + 1)))
                        for tap in range(3):
                            for n in range(3):
                                f = fcols[:, hh, 3 * n + tap:3 * n + tap + 1]
                                src, out = xin[:, n, tap:tap + HW - 2], cv[:, n, 1:HW - 1]
                                last = (nc.vector.tensor_scalar(out, src, f, None, ALU.mult) if tap == 0 else
                                        nc.vector.scalar_tensor_tensor(out, src, f, out, ALU.mult, ALU.add))
                            if tap < 2:
                                link(last)
                        last.then_inc(s["conv"], 1)
                        dve.wait_ge(s["conv_sig"], at(i, 2, hh + 1))
                        if hh == 0:
                            dve.wait_ge(s["y_stored"], at(i, 32, 32))
                        for hs, cols in ((H_LAT, S_LAT), (H_CTX, S_CTX)):
                            last = nc.vector.tensor_tensor(cs[:, :, cols], cv[:, :, hs], xin[:, :, hs], ALU.mult)
                        link(last)
                        for edge in (slice(0, 1), slice(H_LAT.stop, H_CTX.start), slice(H_CTX.stop, HW)):
                            last = nc.vector.memset(xin[:, :, edge], 0.0)
                        last.then_inc(s["silu"], 1)
                        for n in range(2):
                            nc.vector.tensor_tensor(sq[:, n, :], cs[:, n, :], cs[:, n, :], ALU.mult).then_inc(s["squares"], 1)
                        dve.wait_ge(s["c_loaded"], at(i, 64, 64))
                        dve.wait_ge(s["r_loaded"], at(i, 32, 16 * (hh + 1)))
                        link(nc.vector.tensor_tensor(di[:, hh], row(R_G), hcols[:, hh, C_G:C_G + NCHUNK].unsqueeze(2)
                                                     .to_broadcast([P, NCHUNK, P]), ALU.subtract))
                        nc.vector.tensor_scalar(di[:, hh], di[:, hh], 0.0, None, ALU.min).then_inc(s["differ"], 1)
                        for n, scale in ((0, D_SCALE), (1, 1.0)):
                            dve.wait_ge(s["root"], at(i, 4, 2 * hh + n + 1))
                            link(nc.vector.reciprocal(rn[:, n, :], rn[:, n, :]))
                            last = nc.vector.scalar_tensor_tensor(cs[:, n, :], cs[:, n, :], scale, rn[:, n, :], ALU.mult, ALU.mult)
                        link(last)
                        for n, buf in enumerate((q2, k2, ve)):
                            for both, plain in by_direction(split(buf, hh), cs[:, n, :]):
                                last = nc.vector.tensor_copy(both, plain)
                        link(last)
                        nc.vector.tensor_tensor(qd[:, hh], q2[:, hh], row(R_EG), ALU.mult).then_inc(s["prepared"], 1)
                        dve.wait_ge(s["prepared"], at(i, 2, hh + 1))
                        dve.wait_ge(s["masks"], at(i, 4, 2 * hh + 2))
                        nc.vector.scalar_tensor_tensor(dm[:, hh], dm[:, hh], -1.0, g.mask(K_SP).unsqueeze(1).to_broadcast([P, NCHUNK, P]),
                                                       ALU.mult, ALU.mult).then_inc(s["operands"], 1)
                    nc.vector.memset(st[:, :, :, :], 0.0).then_inc(s["s_out"], 1)
                    dve.wait_ge(s["operands"], at(i, 2, 2))

                    def masks(jg, b):
                        mask, out = ((dm, w.lt[:, jg % 2, :, :]), (di, qk[:, GROUP * jg:GROUP * (jg + 1), :]))[b]
                        dve.wait_ge(s["products"], at(i, 2 * NGROUP, 2 * jg + b + 1))
                        for hh in range(2):
                            nc.vector.tensor_tensor(out[:, 2 * hh:2 * hh + 2, :],
                                                    bank[b][:, 2 * hh * P:2 * (hh + 1) * P].rearrange("p (n c) -> p n c", n=2),
                                                    mask[:, hh, 2 * jg:2 * jg + 2, :], ALU.mult).then_inc(s["masked"], 1)

                    def first(jg):
                        dve.wait_ge(s["masked"], at(i, 4 * NGROUP, 4 * jg + 4))
                        invert_first_t(nc, g, s, w, jg, link)

                    masks(0, 0)
                    masks(0, 1)
                    first(0)
                    invert_first_n(dve, nc, s, w, i, 0)
                    for jg in range(NGROUP):
                        ahead = {1: lambda: masks(jg + 1, 0), 2: lambda: masks(jg + 1, 1), 3: lambda: first(jg + 1)}
                        ahead = ahead if jg < NGROUP - 1 else {}
                        invert_dve(dve, nc, g, s, w, i, jg, bool(ahead), ahead)
                    dve.wait_ge(s["tokens_out"], at(i, NGROUP, NGROUP))
                    for n in range(STEPS):
                        u = ORDER[n]
                        dve.wait_ge(s["chain_y"], at(i, STEPS, n + 1))
                        for hh in range(2):
                            for e in range(2):
                                er = slice(C * e, C * (e + 1))
                                last = nc.vector.scalar_tensor_tensor(
                                    tmp[er, hh, :], bank[0][er, (2 * hh + e) * P:(2 * hh + e + 1) * P],
                                    hcols[er, hh, C_NBEG + u:C_NBEG + u + 1], vtok[er, unit(u, hh), :], ALU.mult, ALU.add)
                        last.then_inc(s["tmp_out"], 1)
                        dve.wait_ge(s["chain_v"], at(i, STEPS, n + 1))
                        if n >= 1:
                            dve.wait_ge(s["o_ps"], at(i, STEPS, n))
                        nc.vector.tensor_copy(vn[:, :, :].rearrange("p h v -> p (h v)"), bank[1][:, 0:2 * P]).then_inc(s["v_out"], 1)
                        if n == 2:
                            dve.wait_ge(s["state_stored"], at(i, 32, 32))
                        for e in range(2):
                            dve.wait_ge(s["chain_s"], at(i, 2 * STEPS, 2 * n + e + 1))
                            for hh in range(2):
                                last = nc.vector.scalar_tensor_tensor(
                                    st[:, hh, e, :], st[:, hh, e, :], el[:, hh, 2 * u + e:2 * u + e + 1],
                                    bank[2 + e][:, hh * P:(hh + 1) * P], ALU.mult, ALU.add)
                        last.then_inc(s["s_out"], 1)
                        dve.wait_ge(s["s_out"], at(i, STEPS + 2, n + 2))
                    dve.sem_inc(s["s_out"], 1)
                    dve.wait_ge(s["o_out"], at(i, STEPS, STEPS))
                    for hh in range(2):
                        o4 = split(os_, hh)
                        out = chunked(cs[:, hh, :])
                        for us in (slice(0, NLAT), slice(NLAT, NCHUNK)):
                            last = nc.vector.tensor_tensor(out[:, us, :], o4[:, us, 0, :], o4[:, us, 1, :][:, ::-1, ::-1], ALU.add)
                    link(last)
                    for hh in range(2):
                        nc.vector.tensor_tensor(sq[:, hh, :], cs[:, hh, :], cs[:, hh, :], ALU.mult).then_inc(s["y_squares"], 1)
                    for hh in range(2):
                        dve.wait_ge(s["y_root"], at(i, 2, hh + 1))
                        link(nc.vector.reciprocal(rn[:, hh, :], rn[:, hh, :]))
                        link(nc.vector.scalar_tensor_tensor(cs[:, hh, :], cs[:, hh, :], fcols[:, hh, 9:10], rn[:, hh, :],
                                                            ALU.mult, ALU.mult))
                        dve.wait_ge(s["z_sig"], at(i, 1, 1))
                        link(nc.vector.tensor_tensor(cs[:, hh, :], cs[:, hh, :], z[:, hh, :], ALU.mult))
                        nc.vector.tensor_tensor(cs[:, hh, :], cs[:, hh, :], cv[:, hh, 0:T], ALU.mult).then_inc(s["y_ready"], 1)
                    link.end()


LINKS_DN = 2 * 6 + 2 * NGROUP + 1 + 2 * 3 + 4




class Global:

    def mask(self, col):
        return self.const[:, col:col + P]


def program(nc, d, layers=DEPTH):
    g = Global()
    g.d = d
    with buffers(nc) as (sb, _):
        g.x, g.const, g.vec = sb("x", NB, T), sb("const", K_END), sb("vec", V_END)
        g.mods = sb("mods", DEPTH * 6 * NB, 2)
        g.ident, g.mean_w = g.mask(K_ID), g.mask(K_MEAN)
        g.eps_ln, g.eps_gn, g.eps_nrm = (g.const[:, K_EPS + n:K_EPS + n + 1] for n in range(3))
        g.h = sb("h", NB, HW)
        g.bmod, g.cond, g.silu = sb("bmod", DEPTH * 6 * NB), sb("cond", NB, 2), sb("silu", NB, 2)
        start(nc, g)
        for layer in (0, DEPTH - 1):
            modulation(nc, g, layer)
        first_modulate(nc, g)
        for layer in range(layers):
            kind, j = layer % 3, layer // 3
            with buffers(nc) as (sb2, _):
                if kind == 0:
                    low = sb2("low", 3, T)
                    with buffers(nc) as (sb3, _):
                        g.xx = sb3("xx", NB, HW)
                        token_shift(nc, g)
                        low_rank(nc, g, j, low)
                        for n, m in enumerate((0, 2, 3)):
                            projection(nc, g, d["rw_wrkv"][(3 * j + n) * 4:(3 * j + n + 1) * 4], 4,
                                       out=d["rkv"][n * NB:(n + 1) * NB], mix=V_MU + (j * 6 + m) * NB)
                    rwkv_heads(nc, g, j, low, (1, 2) if layer == 0 else ())
                    wo = d["rw_wo"][4 * j:4 * j + 4]
                elif kind == 1:
                    projection(nc, g, d["at_wqkv"], 6, out=d["qkv"])
                    attention_heads(nc, g)
                    wo = d["at_wo"]
                else:
                    projection(nc, g, d["dn_win"], 16, out=d["dn_proj"])
                    delta_gates(nc, g)
                    delta_heads(nc, g)
                    wo = d["dn_wo"]
            with buffers(nc) as (sb2, _):
                delta = sb2("delta", NB, T)
                projection(nc, g, wo, 4, keep=delta, load=d["mixed"])
                norm(nc, g, delta, layer, 0, mod_at(layer, 2), (mod_at(layer, 4), mod_at(layer, 3)))
                mlp(nc, g, d["w_mlp"][layer * 32:layer * 32 + 32], delta)
                nxt = (mod_at(layer + 1, 1), mod_at(layer + 1, 0)) if layer + 1 < layers else None
                norm(nc, g, delta, layer, 1, mod_at(layer, 5), nxt)




def weight_slabs(w, per=2 * P):
    k, n = w.shape
    w = w.reshape(k // D, NB, P, n // per, per)
    return np.ascontiguousarray(w.transpose(3, 0, 2, 1, 4)).reshape(-1, P, NB * per)


def columns(v):
    v = v.reshape(-1, v.shape[-1] // P, P)
    return v.transpose(2, 0, 1).reshape(P, -1)


def transposed(x):
    return x.T.reshape(-1, P, x.shape[0])


def rwkv_layout(a):
    n_j = a["rw_wrkv"].shape[0]
    slabs = [weight_slabs(a["rw_wrkv"][j, n]) for j in range(n_j) for n in range(3)]
    low, head, state = [], [], []
    for j in range(n_j):
        for w in (a["rw_w1"][j], a["rw_a1"][j]):
            low.append(weight_slabs(w.transpose(1, 0, 2).reshape(D, P), P)[0])
        low.append(weight_slabs(a["rw_g1"][j], P)[0])
        mats = [m.reshape(P, D) for m in (a["rw_w2"][j], a["rw_a2"][j], a["rw_g2"][j])]
        cols = [a["rw_w0"][j, 0], a["rw_w0"][j, 1], a["rw_a0"][j, 0], a["rw_a0"][j, 1], a["rw_kk"][j],
                a["rw_ka"][j], a["rw_rk"][j].reshape(D), a["rw_gn_g"][j], a["rw_gn_b"][j]]
        for b in range(NB):
            f = slice(b * P, (b + 1) * P)
            head.append(np.concatenate([m[:, f] for m in mats] + [c[f][:, None] for c in cols], axis=1))
        st = a["state_rwkv"][0, j].transpose(1, 3, 0, 2).reshape(NB, P, 2 * C)
        state.append(st)
    return (np.concatenate(slabs), np.stack(low), np.stack(head), np.concatenate(state),
            np.concatenate([weight_slabs(a["rw_wo"][j]) for j in range(n_j)]))


def arrays_of(a):
    d = {}
    x = np.concatenate([a["x_sample"][0], a["x_prompt"][0]], axis=0)
    d["x_t"] = transposed(x)
    d["consts"] = constant_table()
    mu = [columns(a["rw_mu"][j]) for j in range(RW_LAYERS)]
    ln = np.stack([a["ln_g"], a["ln_b"]], axis=2)
    d["vectors"] = np.concatenate([columns(ln)] + mu, axis=1)
    d["b_mod_t"] = columns(a["b_mod"])
    cond = np.stack([a["c"][0], a["c_ctx"]], axis=0)
    d["cond_t"] = cond.reshape(2, NB, P).transpose(2, 1, 0)
    d["w_mod"] = np.concatenate([weight_slabs(w, 512) for w in a["w_mod"]])
    d["rw_wrkv"], d["rw_low"], d["rw_head"], d["rw_state"], d["rw_wo"] = rwkv_layout(a)
    fc1 = np.stack([weight_slabs(w) for w in a["w_fc1"]]).reshape(DEPTH, 4, 4, P, -1)
    fc2 = np.stack([weight_slabs(w) for w in a["w_fc2"]]).reshape(DEPTH, 4, 4, P, -1).transpose(0, 2, 1, 3, 4)
    d["w_mlp"] = np.concatenate([fc1, fc2], axis=2).reshape(DEPTH * 32, P, -1)
    attention_layout(a, d)
    delta_layout(a, d)
    return {n: np.ascontiguousarray(v) for n, v in d.items()}


def attention_layout(a, d):
    d["at_wqkv"] = weight_slabs(a["at_wqkv"][0])
    d["at_wo"] = weight_slabs(a["at_wo"][0])
    d["at_gain"] = np.stack([np.tile(a["at_qn"][0], 2)] * 8 + [np.tile(a["at_kn"][0], 2)] * 2)[:, :, None]
    d["cache_kt"] = a["cache_k"][0, 0].transpose(1, 2, 0)
    d["cache_v_tok"] = a["cache_v"][0, 0].transpose(1, 0, 2)
    d["rope_t"], d["rope_perm"] = rope_tables()


def delta_layout(a, d):
    w = a["dn_win"][0]
    gates = 4 * D
    d["dn_win"] = weight_slabs(w[:, :gates])
    d["dn_wgate"] = weight_slabs(w[:, gates:], 4 * DN_HEADS)[0]
    d["dn_wo"] = weight_slabs(a["dn_wo"][0])
    d["dn_small"] = np.concatenate([a["dn_alog"][0].T, a["dn_dtb"][0].T], axis=1)
    taps = a["dn_conv"][0].reshape(3, 3, DN_HEADS, P).transpose(2, 3, 1, 0).reshape(DN_HEADS, P, 9)
    gain = np.broadcast_to(a["dn_ng"][0][None, :, None], (DN_HEADS, P, 1))
    head = np.concatenate([taps, gain], axis=2).reshape(DN_HEADS // 2, 2, P, 10)
    d["dn_head"] = head.transpose(0, 2, 1, 3).reshape(DN_HEADS // 2, P, 20)
    st = a["state_delta"][0, 0].reshape(2, DN_HEADS // 2, 2, P, P)
    d["dn_state"] = st.transpose(1, 3, 2, 0, 4).reshape(DN_HEADS // 2, P, 4 * P)


def rope_tables():
    n_freq = HD // 4
    tok = np.arange(LAT)
    where = np.stack([tok // GRID_W, tok % GRID_W], axis=-1).astype(np.float32)
    inv = np.float32(10000.0) ** (-np.arange(n_freq, dtype=np.float32) / n_freq)
    ang = where[:, :, None] * inv
    tab = np.zeros((P, 2, T), np.float32)
    tab[:, 0, LAT:] = 1.0
    for p in range(P):
        ax, half, f = (p % HD) // (2 * n_freq), (p // n_freq) % 2, p % n_freq
        tab[p, 0, :LAT] = np.cos(ang[:, ax, f])
        tab[p, 1, :LAT] = np.sin(ang[:, ax, f]) * (1.0 if half else -1.0)
    perm = np.zeros((P, P), np.float32)
    perm[np.arange(P) ^ n_freq, np.arange(P)] = 1.0
    return tab, perm


SCRATCH = {"rkv": (3 * NB, P, T), "mixed": (NB, P, T), "qkv": (12, P, T), "qk_rot": (10, P, T),
           "dn_proj": (32, P, T), "dn_gates": (2, 2, DN_HEADS, T),
           "dn_rows": (DN_HEADS, R_END), "dn_cols": (DN_HEADS, P, C_END)}
OUTPUTS = {"y_out": (NB, P, T), "rw_state_out": (RW_LAYERS * NB, P, 2 * C), "kv_out": (4, P, CTX),
           "dn_state_out": (DN_HEADS // 2, P, 2 * 2 * P)}


def declare(nc, arrays):
    d = {}
    for name, a in arrays.items():
        d[name] = nc.dram_tensor(name, a.shape, F32, kind="ExternalInput").ap()
    for name, shape in OUTPUTS.items():
        d[name] = nc.dram_tensor(name, shape, F32, kind="ExternalOutput").ap()
    for name, shape in SCRATCH.items():
        d[name] = nc.dram_tensor(name, shape, F32).ap()
    for name in ("qk_rot", "qkv", "mixed"):
        d[name + "_heads"] = d[name].rearrange("b (h c) t -> (b h) c t", h=2)
    d["dn_lat"], d["dn_ctx"] = d["dn_proj"][:, :, S_LAT], d["dn_proj"][:, :, S_CTX]
    return d


def kernel(**inputs):
    import concourse.bacc as bacc
    from concourse.bass_utils import run_bass_kernel_spmd

    a = {n: np.asarray(v) for n, v in inputs.items()}
    arrays = arrays_of(a)
    nc = bacc.Bacc("TRN2", target_bir_lowering=False, num_devices=1)
    program(nc, declare(nc, arrays))
    r = run_bass_kernel_spmd(nc, [arrays], core_ids=[0]).results[0]
    y = r["y_out"].reshape(D, T).T
    rw = r["rw_state_out"].reshape(RW_LAYERS, RW_HEADS, C, 2, C).transpose(0, 3, 1, 4, 2)[None]
    kv = r["kv_out"].reshape(2, AT_KV, HD, CTX).transpose(0, 3, 1, 2)[:, None, None]
    dn = r["dn_state_out"].reshape(DN_HEADS // 2, P, 2, 2, P).transpose(3, 0, 2, 1, 4).reshape(2, DN_HEADS, P, P)
    out = (y[None, LAT:], y[None, :LAT], rw, kv[0], kv[1], dn[None, None])
    return tuple(np.ascontiguousarray(o) for o in out)
```
